# Optimizing a Trainium2 kernel written in Bass

```python
import math
import jax, jax.numpy as jnp
from jax import lax
import numpy as np

D_MODEL = 1024
BATCH = 1
SEQ = 1024
DEPTH = 1

HEAD_DIM = 64
BLOCK = 128
A_Q_HEADS = 6
A_KV_HEADS = 2
WINDOW = 128
A_WIDTH = A_Q_HEADS * HEAD_DIM
A_KV_WIDTH = A_KV_HEADS * HEAD_DIM
B_HEADS = 4
B_WIDTH = B_HEADS * HEAD_DIM
DECAY_RANK = 64
ICLR_RANK = 64
GATE_RANK = 128
GN_EPS = 64e-5
C_HEADS = 6
C_WIDTH = C_HEADS * HEAD_DIM
MIX_WIDTH = A_WIDTH + B_WIDTH + C_WIDTH
A_COLS = A_WIDTH + 2 * A_KV_WIDTH
B_COLS = 3 * B_WIDTH + DECAY_RANK + ICLR_RANK + GATE_RANK
C_COLS = 3 * C_WIDTH
IN_COLS = A_COLS + B_COLS + C_COLS
NUM_BUCKETS = 32
MAX_EXACT = NUM_BUCKETS // 2
MAX_DISTANCE = 128
N_EXPERTS = 16
N_GROUPS = 4
EXPERTS_PER_GROUP = N_EXPERTS // N_GROUPS
TOP_K = 2
D_FF_EXPERT = 256
LN_EPS = 1e-5
ALPHA = (2 * DEPTH) ** 0.25
BETA_INIT = (8 * DEPTH) ** -0.25

kernel_name = "hybrid_swa_rwkv7_stickbreak_grouped_moe"

def layer_norm(x, g, b):
    xf = x.astype(jnp.float32)
    mu = xf.mean(-1, keepdims=True)
    var = jnp.square(xf - mu).mean(-1, keepdims=True)
    return ((xf - mu) * lax.rsqrt(var + LN_EPS) * g + b).astype(x.dtype)

def t5_causal_bucket(dist):
    dist = jnp.maximum(dist, 0)
    d = jnp.maximum(dist, 1).astype(jnp.float32)
    large = MAX_EXACT + (jnp.log(d / MAX_EXACT) / math.log(MAX_DISTANCE / MAX_EXACT)
                         * (NUM_BUCKETS - MAX_EXACT)).astype(jnp.int32)
    large = jnp.minimum(large, NUM_BUCKETS - 1)
    return jnp.where(dist < MAX_EXACT, dist, large)

def swa_sink_attention(q, k, v, sinks, rel_bias):
    B_, S, Hq, Dh = q.shape
    nb = S // BLOCK
    grp = Hq // A_KV_HEADS
    f32 = jnp.float32
    qb = q.astype(f32).reshape(B_, nb, BLOCK, A_KV_HEADS, grp, Dh)
    pad = ((0, 0), (BLOCK, 0), (0, 0), (0, 0))
    kb = jnp.pad(k.astype(f32), pad).reshape(B_, nb + 1, BLOCK, A_KV_HEADS, Dh)
    vb = jnp.pad(v.astype(f32), pad).reshape(B_, nb + 1, BLOCK, A_KV_HEADS, Dh)
    kband = jnp.concatenate([kb[:, :-1], kb[:, 1:]], axis=2)
    vband = jnp.concatenate([vb[:, :-1], vb[:, 1:]], axis=2)
    logits = jnp.einsum('bnqhgd,bnkhd->bnhgqk', qb, kband) * (Dh ** -0.5)
    qi = jnp.arange(BLOCK)[:, None]
    ki = jnp.arange(2 * BLOCK)[None, :]
    dist = qi + BLOCK - ki
    in_window = (dist >= 0) & (dist < WINDOW)
    key_pos = jnp.arange(nb)[:, None, None] * BLOCK - BLOCK + ki[None]
    valid = in_window[None] & (key_pos >= 0)
    bias = rel_bias.astype(f32)[t5_causal_bucket(dist)]
    bias = bias.transpose(2, 0, 1).reshape(A_KV_HEADS, grp, BLOCK, 2 * BLOCK)
    logits = jnp.where(valid[None, :, None, None], logits + bias[None, None], -jnp.inf)
    sink = sinks.astype(f32).reshape(1, 1, A_KV_HEADS, grp, 1, 1)
    m = jnp.maximum(logits.max(-1, keepdims=True), sink)
    p = jnp.exp(logits - m)
    probs = p / (p.sum(-1, keepdims=True) + jnp.exp(sink - m))
    out = jnp.einsum('bnhgqk,bnkhd->bnqhgd', probs, vband)
    return out.reshape(B_, S, Hq * Dh)

def stick_breaking_attention(q, k, v):
    B_, S, H, Dh = q.shape
    nb = S // BLOCK
    f32 = jnp.float32
    qb = q.astype(f32).reshape(B_, nb, BLOCK, H, Dh).transpose(1, 0, 3, 2, 4)
    kt = k.astype(f32).transpose(0, 2, 1, 3)
    vt = v.astype(f32).transpose(0, 2, 1, 3)
    key_pos = jnp.arange(S)
    scale = Dh ** -0.5

    def one_block(args):
        qblk, start = args
        z = jnp.einsum('bhqd,bhkd->bhqk', qblk, kt) * scale
        q_pos = start + jnp.arange(BLOCK)
        before = key_pos[None, :] < q_pos[:, None]
        log_beta = jnp.where(before, jax.nn.log_sigmoid(z), -jnp.inf)
        log_keep = jnp.where(before, jax.nn.log_sigmoid(-z), 0.0)
        suffix = lax.cumsum(log_keep, axis=3, reverse=True) - log_keep
        w = jnp.exp(log_beta + suffix)
        return jnp.einsum('bhqk,bhkd->bhqd', w, vt)

    out = lax.map(one_block, (qb, jnp.arange(nb) * BLOCK))
    return out.transpose(1, 0, 3, 2, 4).reshape(B_, S, H * Dh)

def token_shift_mix(p, mu):
    prev = jnp.pad(p, ((0, 0), (1, 0), (0, 0)))[:, :-1]
    return p + (prev - p) * mu

def rwkv7_scan(r, w, k, v, a, b):
    B_, S, H, N = r.shape

    def step(state, inp):
        r_t, w_t, k_t, v_t, a_t, b_t = inp
        sa = jnp.einsum('bhvk,bhk->bhv', state, a_t)
        state = (state * w_t[:, :, None, :] + sa[..., None] * b_t[:, :, None, :]
                 + v_t[..., None] * k_t[:, :, None, :])
        return state, jnp.einsum('bhvk,bhk->bhv', state, r_t)

    xs = tuple(t.transpose(1, 0, 2, 3) for t in (r, w, k, v, a, b))
    _, ys = lax.scan(step, jnp.zeros((B_, H, N, N), jnp.float32), xs)
    return ys.transpose(1, 0, 2, 3)

def rwkv7_time_mix(p, shift_mu, decay_w0, decay_up, iclr_a0, iclr_up, gate_up,
                   k_k, k_a, r_k, lnx_g, lnx_b):
    f32 = jnp.float32
    B_, S, _ = p.shape
    p = token_shift_mix(p, shift_mu)
    cuts = [B_WIDTH, 2 * B_WIDTH, 3 * B_WIDTH, 3 * B_WIDTH + DECAY_RANK,
            3 * B_WIDTH + DECAY_RANK + ICLR_RANK]
    r, k, v, xw, xa, xg = jnp.split(p, cuts, axis=-1)
    log_decay = -jax.nn.softplus(-(decay_w0 + jnp.tanh(xw) @ decay_up).astype(f32)) - 0.5
    decay = jnp.exp(-jnp.exp(log_decay))
    a = jax.nn.sigmoid((iclr_a0 + xa @ iclr_up).astype(f32))
    g = (jax.nn.sigmoid(xg) @ gate_up).astype(f32)
    heads = lambda t: t.astype(f32).reshape(B_, S, B_HEADS, HEAD_DIM)
    r, k, v, a_h, decay_h = heads(r), heads(k), heads(v), heads(a), heads(decay)
    kk = k * k_k.astype(f32).reshape(B_HEADS, HEAD_DIM)
    kk = kk * lax.rsqrt(jnp.maximum(jnp.sum(kk * kk, -1, keepdims=True), 1e-24))
    k = k * (1.0 + (a_h - 1.0) * k_a.astype(f32).reshape(B_HEADS, HEAD_DIM))
    y = rwkv7_scan(r, decay_h, k, v, -kk, kk * a_h)
    mu = y.mean(-1, keepdims=True)
    var = jnp.square(y - mu).mean(-1, keepdims=True)
    y = ((y - mu) * lax.rsqrt(var + GN_EPS)).reshape(B_, S, B_WIDTH) * lnx_g + lnx_b
    bonus = (jnp.sum(r * k * r_k.astype(f32), -1, keepdims=True) * v).reshape(B_, S, B_WIDTH)
    return (y + bonus) * g

def hybrid_mixer(h, w_in, w_out, sinks, rel_bias, shift_mu, decay_w0, decay_up,
                 iclr_a0, iclr_up, gate_up, k_k, k_a, r_k, lnx_g, lnx_b):
    B_, S, _ = h.shape
    proj = h @ w_in
    pa = proj[..., :A_COLS]
    pb = proj[..., A_COLS:A_COLS + B_COLS]
    pc = proj[..., A_COLS + B_COLS:]
    qa = pa[..., :A_WIDTH].reshape(B_, S, A_Q_HEADS, HEAD_DIM)
    ka = pa[..., A_WIDTH:A_WIDTH + A_KV_WIDTH].reshape(B_, S, A_KV_HEADS, HEAD_DIM)
    va = pa[..., A_WIDTH + A_KV_WIDTH:].reshape(B_, S, A_KV_HEADS, HEAD_DIM)
    out_a = swa_sink_attention(qa, ka, va, sinks, rel_bias).astype(h.dtype)
    out_b = rwkv7_time_mix(pb, shift_mu, decay_w0, decay_up, iclr_a0, iclr_up, gate_up,
                           k_k, k_a, r_k, lnx_g, lnx_b).astype(h.dtype)
    qc, kc, vc = [t.reshape(B_, S, C_HEADS, HEAD_DIM) for t in jnp.split(pc, 3, axis=-1)]
    out_c = stick_breaking_attention(qc, kc, vc).astype(h.dtype)
    return jnp.concatenate([out_a, out_b, out_c], axis=-1) @ w_out

def grouped_moe(h, router_w, router_bias, w_gate, w_up, w_down):
    B_, S, D = h.shape
    xt = h.reshape(-1, D)
    scores = jax.nn.sigmoid((xt @ router_w).astype(jnp.float32))
    sel = scores + router_bias.astype(jnp.float32)
    group_score = lax.top_k(sel.reshape(-1, N_GROUPS, EXPERTS_PER_GROUP), TOP_K)[0].sum(-1)
    best_group = jnp.argmax(group_score, axis=-1)
    in_group = jnp.repeat(jax.nn.one_hot(best_group, N_GROUPS, dtype=jnp.bool_),
                          EXPERTS_PER_GROUP, axis=1)
    _, top_idx = lax.top_k(jnp.where(in_group, sel, -jnp.inf), TOP_K)
    top_w = jnp.take_along_axis(scores, top_idx, axis=-1)
    top_w = top_w / top_w.sum(-1, keepdims=True)
    gates = (jax.nn.one_hot(top_idx, N_EXPERTS, dtype=jnp.float32) * top_w[..., None]).sum(1)
    hg = jnp.einsum('nd,edf->enf', xt, w_gate)
    hu = jnp.einsum('nd,edf->enf', xt, w_up)
    act = jax.nn.silu(hg) * hu * gates.T[:, :, None].astype(hg.dtype)
    y = jnp.einsum('enf,efd->nd', act, w_down)
    return y.reshape(B_, S, D).astype(h.dtype)

def setup_inputs(seed: int = 0) -> dict:
    key = jax.random.key(seed)
    ks = iter(jax.random.split(key, 40))
    f32 = jnp.float32
    L = DEPTH
    nrm = lambda shape, s: jax.random.normal(next(ks), shape, f32) * s
    uni = lambda shape, lo, hi: jax.random.uniform(next(ks), shape, f32, lo, hi)
    return {
        "x": nrm((BATCH, SEQ, D_MODEL), 1.0),
        "ln0_g": 1.0 + nrm((D_MODEL,), 0.02),
        "ln0_b": nrm((D_MODEL,), 0.02),
        "w_in": nrm((L, D_MODEL, IN_COLS), D_MODEL ** -0.5),
        "w_out": nrm((L, MIX_WIDTH, D_MODEL), MIX_WIDTH ** -0.5 * BETA_INIT),
        "sinks": nrm((L, A_Q_HEADS), 0.5),
        "rel_bias": nrm((NUM_BUCKETS, A_Q_HEADS), 0.5),
        "shift_mu": uni((L, B_COLS), 0.0, 1.0),
        "decay_w0": uni((L, B_WIDTH), -6.0, -1.0),
        "decay_up": nrm((L, DECAY_RANK, B_WIDTH), 0.5 * DECAY_RANK ** -0.5),
        "iclr_a0": nrm((L, B_WIDTH), 0.1),
        "iclr_up": nrm((L, ICLR_RANK, B_WIDTH), ICLR_RANK ** -0.5),
        "gate_up": nrm((L, GATE_RANK, B_WIDTH), GATE_RANK ** -0.5),
        "k_k": 0.85 + nrm((L, B_WIDTH), 0.05),
        "k_a": 1.0 + nrm((L, B_WIDTH), 0.05),
        "r_k": nrm((L, B_HEADS, HEAD_DIM), 0.1),
        "lnx_g": 1.0 + nrm((L, B_WIDTH), 0.02),
        "lnx_b": nrm((L, B_WIDTH), 0.02),
        "ln1_g": 1.0 + nrm((L, D_MODEL), 0.02),
        "ln1_b": nrm((L, D_MODEL), 0.02),
        "router_w": nrm((D_MODEL, N_EXPERTS), D_MODEL ** -0.5),
        "router_bias": nrm((N_EXPERTS,), 0.01),
        "w_gate": nrm((L, N_EXPERTS, D_MODEL, D_FF_EXPERT), D_MODEL ** -0.5),
        "w_up": nrm((L, N_EXPERTS, D_MODEL, D_FF_EXPERT), D_MODEL ** -0.5),
        "w_down": nrm((L, N_EXPERTS, D_FF_EXPERT, D_MODEL), D_FF_EXPERT ** -0.5 * BETA_INIT),
        "ln2_g": 1.0 + nrm((L, D_MODEL), 0.02),
        "ln2_b": nrm((L, D_MODEL), 0.02),
    }

def reference(x, ln0_g, ln0_b, w_in, w_out, sinks, rel_bias, shift_mu, decay_w0, decay_up,
              iclr_a0, iclr_up, gate_up, k_k, k_a, r_k, lnx_g, lnx_b, ln1_g, ln1_b,
              router_w, router_bias, w_gate, w_up, w_down, ln2_g, ln2_b):
    h = layer_norm(x, ln0_g, ln0_b)
    for l in range(DEPTH):
        m = hybrid_mixer(h, w_in[l], w_out[l], sinks[l], rel_bias, shift_mu[l], decay_w0[l],
                         decay_up[l], iclr_a0[l], iclr_up[l], gate_up[l], k_k[l], k_a[l],
                         r_k[l], lnx_g[l], lnx_b[l])
        h = layer_norm(ALPHA * h + m, ln1_g[l], ln1_b[l])
        f = grouped_moe(h, router_w, router_bias, w_gate[l], w_up[l], w_down[l])
        h = layer_norm(ALPHA * h + f, ln2_g[l], ln2_b[l])
    return h


_drawn_inputs = setup_inputs


def setup_inputs(seed=0):
    import zlib

    import numpy as np

    out = dict(_drawn_inputs(seed))
    spreads = {}
    factors = {'sinks': 8.0,
     'decay_up': 3.05,
     'iclr_a0': 2.899,
     'lnx_g': 4.725,
     'lnx_b': 4.782,
     'ln2_g': 2.802,
     'ln2_b': 2.803}
    for name, (base, spread) in spreads.items():
        noise = np.random.default_rng([zlib.crc32(name.encode()), seed]).standard_normal(out[name].shape)
        drawn = base * np.exp(spread * noise) if base else spread * noise
        out[name] = __import__('jax').numpy.asarray(drawn.astype(out[name].dtype))
    for name, factor in factors.items():
        out[name] = (out[name] * factor).astype(out[name].dtype)
    return out
```

```python
from contextlib import ExitStack

import numpy as np

import concourse.bass as bass
from concourse import mybir

F32 = mybir.dt.float32
I32 = mybir.dt.int32
U32 = mybir.dt.uint32
ALU = mybir.AluOpType
ACT = mybir.ActivationFunctionType
AX = mybir.AxisListType.X

P = 128
T = 1024
D = 1024
NT, ND = T // P, D // P
HALF = 512
HD = 64
CH = 64
NCH = T // CH
A_COLS, B_COLS, C_COLS = 640, 1024, 1152
LN_EPS, GN_EPS = 1e-5, 64e-5
DECAY_SCALE = float(np.exp(-0.5))
ALPHA = 2 ** 0.25

XWXA, XG, R0, K0, V0, R1, K1, V1 = range(8)
N_B = 8
N_CM = 18
K_TILES = (3, 4, 5, 9)
N_BUCKETS, MAX_EXACT, MAX_DISTANCE, WINDOW = 32, 16, 128, 128
N_TOEPLITZ = 384
NEG = -1e30
CLAMP = 30.0

PC = {}
for _name, _n in (("ln0_g", 8), ("ln0_b", 8), ("mu", 8), ("w0", 2), ("a0", 2), ("k_k", 2), ("k_a", 2),
                  ("r_k", 2), ("lnx_g", 2), ("lnx_b", 2), ("ln1_g", 8), ("ln1_b", 8)):
    PC[_name] = sum(n for _, n in PC.values()), _n
N_PC = 56


def constants():
    i, j = np.arange(P)[:, None], np.arange(P)[None, :]
    same = (i // CH) == (j // CH)
    c = {
        "ident": i == j,
        "head_ones": same,
        "head_mean": same / HD,
        "level0": (i // 2 == j // 2) & (i % 2 == 0) & (j % 2 == 1),
        "suffix": -1.0 * (i >= j),
        "all_later": -np.ones((P, P)),
        "key_before": i < j,
        "ones": np.ones((P, P)),
    }
    s = np.arange(P)[:, None]
    cols = np.arange(512)
    chunk, kind, t = (cols // 64) % 2, (cols // 128) % 2, cols % 64
    c["chunk_mask"] = (s // CH == chunk) & ((s % CH < t) | ((kind == 1) & (s % CH == t)))
    return c


def bias_constants():
    dist = 255 - np.arange(N_TOEPLITZ)
    inside = (dist >= 0) & (dist < WINDOW)
    d = np.maximum(dist, 1).astype(np.float32)
    large = MAX_EXACT + (np.log(d / MAX_EXACT) / np.float32(np.log(MAX_DISTANCE / MAX_EXACT))
                         * (N_BUCKETS - MAX_EXACT)).astype(np.int32)
    bucket = np.where(dist < MAX_EXACT, dist, np.minimum(large, N_BUCKETS - 1))
    hot = (np.arange(N_BUCKETS)[:, None] == bucket[None, :]) & inside[None, :]
    outside = np.broadcast_to(np.where(inside, 0.0, NEG), (N_BUCKETS, N_TOEPLITZ))
    return np.concatenate([hot, outside], axis=1)


CONST = {}
_at = 0
for _name, _m in constants().items():
    CONST[_name] = (_at, _m.shape[1])
    _at += _m.shape[1]
N_CONST = _at


def level_masks():
    i, j = np.arange(P)[:, None], np.arange(P)[None, :]
    out = []
    for m in (2, 4, 8, 16, 32):
        out.append((i // (2 * m) == j // (2 * m)) & ((i // m) % 2 == 0) & ((j // m) % 2 == 1))
    out.append(i >= j)
    return np.concatenate(out, axis=1).astype(np.int32)


N_LEVELS = 5


class Memory:

    def __init__(self, nc, start, end=229344):
        self.nc, self.at, self.end = nc, start, end

    def put(self, name, shape, dtype=F32):
        t = self.nc.alloc_sbuf_tensor_at(name, shape, dtype, offset=self.at)
        size = 4 * int(np.prod(shape[1:]))
        self.at += -(-size // 32) * 32
        assert self.at <= self.end, (name, self.at)
        return t


def bcast(ap, *dims):
    return bass.AP(ap.tensor, ap.offset, [list(ap.ap[0])] + [list(d) for d in dims])


def normalise_input(nc, ctx, x, h_dram, ln_rows, C, params, x_sb, hT, mem):
    sem = lambda n: ctx.enter_context(nc.semaphore(n))
    hb = mem.put("h_rows", [P, 2, D])
    gb = mem.put("ln0_rows", [P, 2, D])
    stats = mem.put("ln0_stats", [P, NT, 12])
    mv = mem.put("ln0_mv", [P, NT, 2])
    std = mem.put("ln0_std", [P, NT])
    rstd = mem.put("ln0_rstd", [P, NT])
    x_in = [sem(f"x_in{i}") for i in range(NT)]
    rows_in, const_in = sem("ln_rows_in"), sem("const_in")
    h_out = [sem("h_out0"), sem("h_out1")]
    stat, aggr, std_done, rstd_done = sem("ln0_stat"), sem("ln0_aggr"), sem("ln0_std"), sem("ln0_rstd")
    xn_done, xT_done, hT_done = sem("xn_done"), sem("xT_done"), sem("hT_done")
    h_mul, h_done = sem("h_mul"), sem("h_done")
    const_sb, const_d, par_sb, par_d, mask_sb, mask_d = params
    with ExitStack() as inner:
        bank = [inner.enter_context(nc.psum_tensor(f"xT{d}", [P, HALF], F32)) for d in range(ND)]
        with nc.Block() as block:
            @block.sync
            def _(sp):
                for i in range(NT):
                    sp.dma_start(x_sb[:, i, :], x[i * P:(i + 1) * P, :]).then_inc(x_in[i], 16)
                for i in range(NT):
                    sp.wait_ge(h_done, i + 1)
                    sp.dma_start(h_dram[i * P:(i + 1) * P, :], hb[:, i % 2, :]).then_inc(h_out[i % 2], 16)
                for s in h_out:
                    sp.wait_ge(s, 16 * NT // 2)

            @block.scalar
            def _(act):
                act.dma_start(const_sb[:], const_d).then_inc(const_in, 16)
                act.dma_start(par_sb[:], par_d).then_inc(const_in, 16)
                act.dma_start(mask_sb[:], mask_d).then_inc(const_in, 16)
                for k in range(2):
                    act.dma_start(gb[:, k, :], ln_rows[k:k + 1, :].to_broadcast([P, D])).then_inc(rows_in, 16)
                act.wait_ge(const_in, 48)
                for half in range(2):
                    i0 = 4 * half
                    act.wait_ge(aggr, i0 + 4)
                    act.activation(std[:, i0:i0 + 4], mv[:, i0:i0 + 4, 1], ACT.Sqrt, bias=LN_EPS).then_inc(std_done, 1)
                    for d in range(ND):
                        act.wait_ge(xT_done, half * ND + d + 1)
                        act.activation(hT[:, d, half * HALF:(half + 1) * HALF], bank[d][:], ACT.Identity,
                                       bias=C("ln0_b", d), scale=C("ln0_g", d)).then_inc(hT_done, 1)

            @block.vector
            def _(dve):
                for half in range(2):
                    for i in range(4 * half, 4 * half + 4):
                        dve.wait_ge(x_in[i], 16)
                        for k in range(2):
                            dve.bn_stats(stats[:, i, 6 * k:6 * k + 6],
                                         x_sb[:, i, k * HALF:(k + 1) * HALF]).then_inc(stat, 1)
                        dve.wait_ge(stat, 2 * i + 2)
                        dve.bn_aggr(mv[:, i, :], stats[:, i, :]).then_inc(aggr, 1)
                    dve.wait_ge(std_done, half + 1)
                    dve.reciprocal(rstd[:, 4 * half:4 * half + 4], std[:, 4 * half:4 * half + 4]).then_inc(rstd_done, 1)
                    dve.wait_ge(rstd_done, half + 1)
                    for i in range(4 * half, 4 * half + 4):
                        dve.tensor_scalar(x_sb[:, i, :], x_sb[:, i, :], mv[:, i, 0:1], rstd[:, i:i + 1],
                                          ALU.subtract, ALU.mult).then_inc(xn_done, 1)

            @block.tensor
            def _(pe):
                pe.wait_ge(const_in, 48)
                for half in range(2):
                    pe.wait_ge(xn_done, 4 * half + 4)
                    for d in range(ND):
                        if half:
                            pe.wait_ge(hT_done, d + 1)
                        for j in range(4):
                            mm = pe.transpose(bank[d][:, j * P:(j + 1) * P],
                                              x_sb[:, 4 * half + j, d * P:(d + 1) * P], C("ident"))
                        mm.then_inc(xT_done, 1)

            @block.gpsimd
            def _(pool):
                pool.wait_ge(rows_in, 32)
                for i in range(NT):
                    pool.wait_ge(xn_done, i + 1)
                    if i >= 2:
                        pool.wait_ge(h_out[i % 2], 16 * (i // 2))
                    pool.tensor_tensor(hb[:, i % 2, :], x_sb[:, i, :], gb[:, 0, :], ALU.mult).then_inc(h_mul, 1)
                    pool.wait_ge(h_mul, i + 1)
                    pool.tensor_tensor(hb[:, i % 2, :], hb[:, i % 2, :], gb[:, 1, :], ALU.add).then_inc(h_done, 1)


PREP = ["scan", "kk", "kk2", "norm0", "norm1", "kfac", "knew", "rk", "recip", "kkn", "bonus0", "bonus1",
        "at", "rt", "ba", "bt", "kt", "pt", "bh", "kh"]


def prep_at(g, name):
    return 1 + g * len(PREP) + PREP.index(name) + 1


def project(nc, ctx, w_cm, w_v, up_d, gate_d, qk_dram, C, hT, pm, v_tok, R, mem):
    sem = lambda n: ctx.enter_context(nc.semaphore(n))
    AR, bt, bh, kh, gT, PT, bonus = (R[n] for n in ("AR", "bt", "bh", "kh", "g", "PT", "bonus"))
    wv_sb = R["wv"]
    w_ring = mem.put("w_ring", [P, 2, ND * P])
    praw = mem.put("praw", [P, T + 8])
    diff = mem.put("diff", [P, T])
    stage = mem.put("qk_stage", [P, 2, T])
    up_sb = mem.put("up_sb", [P, 256])
    gate_sb = mem.put("gate_sb", [P, 256])
    aT = mem.put("iclr", [P, 2, T])
    lw = mem.put("log_decay", [P, 2, T])
    Pe = mem.put("decay", [P, NCH, CH + 1])
    kk = mem.put("kk", [P, T])
    tmp = mem.put("prep_tmp", [P, T])
    scan_mask = mem.put("scan_mask", [P, NCH, CH])
    one_minus_ka = mem.put("one_minus_ka", [P, 8])
    Pinv, rn = praw, diff
    w_in = [sem("w_in0"), sem("w_in1")]
    wv_in, up_in = sem("wv_in"), sem("up_in")
    proj_done, proj_out = sem("proj_done"), sem("proj_out")
    v_done, v_out = sem("v_done"), sem("v_out")
    prepared, mix_diff, mixed = sem("prep_consts"), sem("mix_diff"), sem("mixed")
    stored = [sem("qk_stored0"), sem("qk_stored1")]
    squashed = sem("squashed")
    lora_done, lora_out = sem("lora_done"), sem("lora_out")
    prep, exp_done, sqrt_done = sem("prep"), sem("exp_done"), sem("sqrt_done")
    head_sum = sem("head_sum")
    per_chunk = lambda ap: ap.rearrange("p (c t) -> p c t", c=NCH)
    per_tile = lambda ap: ap.rearrange("p (i c t) -> p i c t", i=NT, c=2)
    by_tile = lambda ap: ap.rearrange("p i (c t) -> p i c t", c=2)
    split = lambda ap: ap.rearrange("p (i c) t -> p i c t", c=2)

    with ExitStack() as inner:
        pb = [inner.enter_context(nc.psum_tensor(f"proj{b}", [P, HALF], F32)) for b in range(6)]
        sb = [inner.enter_context(nc.psum_tensor(f"small{b}", [P, HALF], F32)) for b in range(2)]
        with nc.Block() as block:
            @block.sync
            def _(sp):
                sp.dma_start(up_sb[:], up_d).then_inc(up_in, 16)
                sp.dma_start(gate_sb[:], gate_d).then_inc(up_in, 16)

                def store(u):
                    sp.wait_ge(proj_out, 2 * (N_B + u + 1))
                    sp.dma_start(qk_dram[u], stage[:, u % 2, :]).then_inc(stored[u % 2], 16)

                for t in range(N_CM):
                    if t >= 2:
                        sp.wait_ge(proj_done, 2 * (t - 1))
                    sp.dma_start(w_ring[:, t % 2, :], w_cm[t]).then_inc(w_in[t % 2], 16)
                    if t == 3:
                        sp.dma_start(wv_sb[:], w_v).then_inc(wv_in, 16)
                    if t >= N_B + 2:
                        store(t - N_B - 2)
                store(N_CM - N_B - 2)
                store(N_CM - N_B - 1)
                for s in stored:
                    sp.wait_ge(s, 16 * (N_CM - N_B) // 2)

            @block.tensor
            def _(pe):
                def tile(t):
                    pe.wait_ge(w_in[t % 2], 16 * (t // 2 + 1))
                    for half in range(2):
                        n = 2 * t + half
                        if n >= 6:
                            pe.wait_ge(proj_out, n - 5)
                        for d in range(ND):
                            mm = pe.matmul(pb[n % 6][:], w_ring[:, t % 2, d * P:(d + 1) * P],
                                           hT[:, d, half * HALF:(half + 1) * HALF], start=d == 0, stop=d == ND - 1)
                        mm.then_inc(proj_done, 1)

                def head_sums(g, what, first):
                    pe.wait_ge(prep, prep_at(g, what))
                    for half in range(2):
                        if what == "rk":
                            pe.wait_ge(prep, prep_at(g, f"norm{half}"))
                        elif g:
                            pe.wait_ge(prep, prep_at(g - 1, f"bonus{half}"))
                        else:
                            pe.wait_ge(lora_out, 12)
                        pe.matmul(sb[half][:], C("head_ones"), tmp[:, half * HALF:(half + 1) * HALF],
                                  start=True, stop=True).then_inc(head_sum, 1)

                for t in range(N_B):
                    tile(t)
                pe.wait_ge(up_in, 32)
                pe.wait_ge(squashed, 2)
                n = 0
                for g in range(2):
                    cols = slice(g * P, (g + 1) * P)
                    for half in range(2):
                        hs = slice(half * HALF, (half + 1) * HALF)
                        for lhsT, rhs in ((up_sb[0:64, cols], pm[0:64, XWXA, hs]),
                                          (up_sb[64:128, cols], pm[64:128, XWXA, hs]),
                                          (gate_sb[:, cols], pm[:, XG, hs])):
                            if n >= 2:
                                pe.wait_ge(lora_out, n - 1)
                            pe.matmul(sb[n % 2][:], lhsT, rhs, start=True, stop=True).then_inc(lora_done, 1)
                            n += 1
                pe.wait_ge(wv_in, 16)
                for i in range(NT):
                    if i < 2:
                        pe.wait_ge(proj_out, 2 * N_B)
                    else:
                        pe.wait_ge(v_out, i - 1)
                    for d in range(ND):
                        mm = pe.matmul(pb[4 + i % 2][:], hT[:, d, i * P:(i + 1) * P], wv_sb[:, d, :],
                                       start=d == 0, stop=d == ND - 1)
                    mm.then_inc(v_done, 1)
                pe.wait_ge(v_out, NT)
                for t in range(N_B, N_CM):
                    tile(t)
                    if t in (8, 12):
                        head_sums((t - 8) // 4, "kk2", 0)
                    if t in (10, 14):
                        head_sums((t - 10) // 4, "rk", 0)

            @block.scalar
            def _(act):
                def copy_out(t):
                    for half in range(2):
                        n = 2 * t + half
                        act.wait_ge(proj_done, n + 1)
                        if t < N_B:
                            dst = praw[:, 1 + half * HALF:1 + (half + 1) * HALF]
                            if t and half == 0:
                                act.wait_ge(mixed, t)
                        else:
                            u = t - N_B
                            dst = stage[:, u % 2, half * HALF:(half + 1) * HALF]
                            if u >= 2 and half == 0:
                                act.wait_ge(stored[u % 2], 16 * (u // 2))
                        if t < N_B or t - N_B in K_TILES:
                            act.copy(dst, pb[n % 6][:]).then_inc(proj_out, 1)
                        else:
                            act.mul(dst, pb[n % 6][:], HD ** -0.5).then_inc(proj_out, 1)

                def decay_factors(g):
                    act.wait_ge(prep, prep_at(g, "scan"))
                    if g:
                        act.wait_ge(prep, prep_at(g - 1, "kh"))
                    else:
                        act.wait_ge(mixed, N_B)
                    act.activation(Pe[:, :, 1:], per_chunk(lw[:, g, :]), ACT.Exp, scale=-DECAY_SCALE).then_inc(exp_done, 1)
                    act.activation(Pinv[:, 0:T], lw[:, g, :], ACT.Exp, scale=DECAY_SCALE).then_inc(exp_done, 1)

                def norm(g):
                    act.wait_ge(prep, prep_at(g, "norm1"))
                    act.activation(rn[:], rn[:], ACT.Sqrt).then_inc(sqrt_done, 1)

                for t in range(N_B):
                    copy_out(t)
                    if t == 2:
                        act.wait_ge(mixed, 2)
                        act.activation(pm[0:64, XWXA, :], pm[0:64, XWXA, :], ACT.Tanh).then_inc(squashed, 1)
                        act.activation(pm[:, XG, :], pm[:, XG, :], ACT.Sigmoid).then_inc(squashed, 1)
                n = 0
                for g in range(2):
                    for half in range(2):
                        hs = slice(half * HALF, (half + 1) * HALF)
                        for k in range(3):
                            act.wait_ge(lora_done, n + 1)
                            if k == 0:
                                act.activation(lw[:, g, hs], sb[n % 2][:], ACT.Sigmoid, bias=C("w0", g)).then_inc(lora_out, 1)
                            elif k == 1:
                                act.activation(aT[:, g, hs], sb[n % 2][:], ACT.Sigmoid, bias=C("a0", g)).then_inc(lora_out, 1)
                            else:
                                act.copy(gT[:, g, hs], sb[n % 2][:]).then_inc(lora_out, 1)
                            n += 1
                for i in range(NT):
                    act.wait_ge(v_done, i + 1)
                    act.copy(v_tok[:, i, :], pb[4 + i % 2][:]).then_inc(v_out, 1)
                decay_factors(0)
                for t in range(N_B, N_CM):
                    copy_out(t)
                    if t in (8, 12):
                        norm((t - 8) // 4)
                    if t == 11:
                        decay_factors(1)

            @block.vector
            def _(dve):
                dve.memset(praw[:, 0:1], 0.0).then_inc(prepared, 1)
                dve.memset(scan_mask[:], 1.0).then_inc(prepared, 1)
                dve.memset(Pe[:, :, 0:1], 1.0).then_inc(prepared, 1)
                dve.wait_ge(prepared, 2)
                dve.memset(scan_mask[:, :, 0:1], 0.0).then_inc(prepared, 1)
                dve.tensor_scalar(one_minus_ka[:, 0:2], C("k_a", 0, 2), -1.0, 1.0, ALU.mult, ALU.add).then_inc(prepared, 1)
                dve.wait_ge(prepared, 5)
                for t in range(N_B):
                    dve.wait_ge(proj_out, 2 * t + 2)
                    dve.tensor_tensor(diff[:], praw[:, 0:T], praw[:, 1:T + 1], ALU.subtract).then_inc(mix_diff, 1)
                    dve.wait_ge(mix_diff, t + 1)
                    dve.scalar_tensor_tensor(pm[:, t, :], diff[:], C("mu", t), praw[:, 1:T + 1],
                                             ALU.mult, ALU.add).then_inc(mixed, 1)
                dve.wait_ge(mixed, N_B)
                dve.nop().then_inc(prep, 1)
                for g in range(2):
                    r, k, v = (pm[:, (R0, K0, V0)[j] if g == 0 else (R1, K1, V1)[j], :] for j in range(3))
                    after = lambda name: dve.wait_ge(prep, prep_at(g, name))
                    at_PT = bass.AP(PT, 0, [list(PT[:].ap[0]), [1, NCH], [0, CH]]) if g == 0 else \
                        bass.AP(PT, NCH, [list(PT[:].ap[0]), [1, NCH], [0, CH]])
                    dve.wait_ge(lora_out, 6 * (g + 1))
                    dve.tensor_tensor_scan(lw[:, g, :], scan_mask[:].rearrange("p c t -> p (c t)"), lw[:, g, :],
                                           0.0, ALU.mult, ALU.add).then_inc(prep, 1)
                    dve.tensor_scalar(kk[:], k, C("k_k", g), None, ALU.mult).then_inc(prep, 1)
                    after("kk")
                    dve.tensor_tensor(tmp[:], kk[:], kk[:], ALU.mult).then_inc(prep, 1)
                    for half in range(2):
                        dve.wait_ge(head_sum, 4 * g + half + 1)
                        dve.tensor_scalar(rn[:, half * HALF:(half + 1) * HALF], sb[half][:], 1e-24, None,
                                          ALU.max).then_inc(prep, 1)
                    dve.tensor_scalar(tmp[:], aT[:, g, :], C("k_a", g), one_minus_ka[:, g:g + 1],
                                      ALU.mult, ALU.add).then_inc(prep, 1)
                    after("kfac")
                    dve.tensor_tensor(k, k, tmp[:], ALU.mult).then_inc(prep, 1)
                    after("knew")
                    dve.scalar_tensor_tensor(tmp[:], r, C("r_k", g), k, ALU.mult, ALU.mult).then_inc(prep, 1)
                    dve.wait_ge(sqrt_done, g + 1)
                    dve.reciprocal(rn[:], rn[:]).then_inc(prep, 1)
                    after("recip")
                    dve.scalar_tensor_tensor(kk[:], kk[:], -1.0, rn[:], ALU.mult, ALU.mult).then_inc(prep, 1)
                    for half in range(2):
                        hs = slice(half * HALF, (half + 1) * HALF)
                        dve.wait_ge(head_sum, 4 * g + 2 + half + 1)
                        dve.tensor_tensor(bonus[:, g, hs], sb[half][:], v[:, hs], ALU.mult).then_inc(prep, 1)
                    dve.wait_ge(exp_done, 2 * g + 2)
                    after("kkn")
                    dve.tensor_tensor(by_tile(AR[:, g, :, 0, :]), per_tile(kk[:]), split(Pe[:, :, 0:CH]), ALU.mult).then_inc(prep, 1)
                    dve.tensor_tensor(by_tile(AR[:, g, :, 1, :]), per_tile(r), split(Pe[:, :, 1:]), ALU.mult).then_inc(prep, 1)
                    dve.scalar_tensor_tensor(tmp[:], kk[:], -1.0, aT[:, g, :], ALU.mult, ALU.mult).then_inc(prep, 1)
                    after("ba")
                    dve.tensor_tensor(bt[:, g, :], tmp[:], Pinv[:, 0:T], ALU.mult).then_inc(prep, 1)
                    dve.tensor_tensor(k, k, Pinv[:, 0:T], ALU.mult).then_inc(prep, 1)
                    dve.tensor_copy(PT[:, g, :], Pe[:, :, CH]).then_inc(prep, 1)
                    dve.wait_ge(v_done, NT)
                    after("pt")
                    dve.tensor_tensor(per_chunk(bh[:, g, :]), per_chunk(bt[:, g, :]), at_PT, ALU.mult).then_inc(prep, 1)
                    dve.tensor_tensor(per_chunk(kh[:, g, :]), per_chunk(k), at_PT, ALU.mult).then_inc(prep, 1)


TURNS = [x for level in range(1, N_LEVELS + 1) for x in (f"T{level}", f"Y{level}", f"X{level}")][:-1]
MADE = ["turn", "A0", "A1", "A2", "A3", "AV", "X0", *TURNS, "GU", "RT", "MT"]
KEPT_ACT = ["a_tok", "bh_tok", "X0", *[x for x in TURNS if x[0] != "Y"], "GU"]
KEPT_DVE = ["kh_tok", "v_tok", "A0", "A1", "A2", "A3", "level0", "XT0", "AV",
            *[x for x in TURNS if x[0] == "Y"], "RT", "MT0", "MT1", "MT2", "MT3"]


def upto(steps, n, name):
    return n * len(steps) + steps.index(name) + 1


def rwkv(nc, ctx, C, masks, pm, R, mixT, mem):
    sem = lambda n: ctx.enter_context(nc.semaphore(n))
    AR, bt, bh, kh, gT, PT, bonus = (R[n] for n in ("AR", "bt", "bh", "kh", "g", "PT", "bonus"))
    XR = mem.put("x_rhs", [P, NT, 4, 2, HD])
    bh_tok = R["bh_tok"]
    kh_tok = R["kh_tok"]
    v_tok = mem.put("vb_tok", [P, NT, 256])
    Am = mem.put("chunk_products", [P, 2, 4, 512])
    XT = mem.put("inverse_T", [P, 2, 4, P])
    X = mem.put("inverse", [P, 2, 4, P])
    Tm = mem.put("inverse_step", [P, 2, 4, P])
    GU = mem.put("gu", [P, 2, 2, 4, HD])
    RT, S = R["RT"], R["S"]
    MT = mem.put("state_map", [P, 2, 4, P])
    yc, y2 = R["yc"], R["y2"]
    made = [sem("made0"), sem("made1")]
    kept_act = [sem("kept_act0"), sem("kept_act1")]
    kept_dve = [sem("kept_dve0"), sem("kept_dve1")]
    z_done, s_done, y_done, y_out = sem("z_done"), sem("s_done"), sem("y_done"), sem("y_out")
    mean_done, centred, squared, var_done = sem("mean_done"), sem("centred"), sem("squared"), sem("var_done")
    gn_std, gn_chain = sem("gn_std"), sem("gn_chain")

    def cols4(ap):
        return ap.rearrange("p (h t) -> p h t", h=4)

    def part(st, hh, kind, ar):
        at = kind * 256 + ar * P
        return Am[:, st, hh, at:at + P]

    with ExitStack() as inner:
        bank = [inner.enter_context(nc.psum_tensor(f"rw{b}", [P, HALF], F32)) for b in range(8)]
        ybank, zbank = bank[6], bank[7]
        with nc.Block() as block:
            @block.tensor
            def _(pe):
                def step(name, st, i):
                    n = i // 2
                    B = bank[3 * st:3 * st + 3]
                    act_has = lambda x: pe.wait_ge(kept_act[st], upto(KEPT_ACT, n, x))
                    dve_has = lambda x: pe.wait_ge(kept_dve[st], upto(KEPT_DVE, n, x))
                    ts = slice(i * P, (i + 1) * P)
                    if name == "turn":
                        if n:
                            pe.wait_ge(kept_dve[st], n * len(KEPT_DVE))
                        for g in range(2):
                            pe.transpose(B[0][:, g * P:(g + 1) * P], AR[:, g, i, 0, :], C("ident"))
                            pe.transpose(B[0][:, (2 + g) * P:(3 + g) * P], bh[:, g, ts], C("ident"))
                            pe.transpose(B[1][:, g * P:(g + 1) * P], kh[:, g, ts], C("ident"))
                            mm = pe.transpose(B[1][:, (2 + g) * P:(3 + g) * P], pm[:, (V0, V1)[g], ts], C("ident"))
                    elif name[0] == "A" and name != "AV":
                        hh = int(name[1])
                        g, e = hh // 2, hh % 2
                        if hh == 0:
                            act_has("bh_tok")
                        elif hh == 1:
                            dve_has("v_tok")
                        elif hh == 3:
                            dve_has("A0")
                        ar = AR[e * HD:(e + 1) * HD, g, i, :, :].rearrange("p a t -> p (a t)")
                        dst = B[hh % 3]
                        pe.matmul(dst[:, 0:256], pm[e * HD:(e + 1) * HD, (K0, K1)[g], ts], ar, start=True, stop=True)
                        mm = pe.matmul(dst[:, 256:512], bt[e * HD:(e + 1) * HD, g, ts], ar, start=True, stop=True)
                    elif name == "AV":
                        dve_has("A3")
                        for hh in range(4):
                            mm = pe.matmul(B[1][:, hh * HD:(hh + 1) * HD], part(st, hh, 0, 0),
                                           v_tok[:, i, hh * HD:(hh + 1) * HD], start=True, stop=True)
                    elif name[0] == "X":
                        dve_has("XT0" if name == "X0" else f"Y{name[1]}")
                        for hh in range(4):
                            mm = pe.transpose(B[0][:, hh * P:(hh + 1) * P], XT[:, st, hh, :], C("ident"))
                    elif name[0] == "T":
                        act_has(f"X{int(name[1]) - 1}")
                        if name == "T1":
                            dve_has("AV")
                        for hh in range(4):
                            mm = pe.matmul(B[1][:, hh * P:(hh + 1) * P], part(st, hh, 1, 0), X[:, st, hh, :],
                                           start=True, stop=True)
                    elif name[0] == "Y":
                        act_has(f"T{name[1]}")
                        for hh in range(4):
                            mm = pe.matmul(B[2][:, hh * P:(hh + 1) * P], Tm[:, st, hh, :], XT[:, st, hh, :],
                                           start=True, stop=True)
                    elif name == "GU":
                        dve_has("Y5")
                        for hh in range(4):
                            mm = pe.matmul(B[1][:, hh * P:(hh + 1) * P], XT[:, st, hh, :], XR[:, i, hh, :, :],
                                           start=True, stop=True)
                    elif name == "RT":
                        act_has("GU")
                        for hh in range(4):
                            g, e = hh // 2, hh % 2
                            mm = pe.matmul(B[2][e * HD:(e + 1) * HD, g * P:(g + 1) * P], GU[:, st, 0, hh, :],
                                           part(st, hh, 1, 1), start=True, stop=True)
                    elif name == "MT":
                        for cc in range(2):
                            rows = slice(cc * CH, (cc + 1) * CH)
                            for g in range(2):
                                mm = pe.matmul(B[cc][:, g * P:(g + 1) * P], GU[rows, st, 0, 2 * g:2 * g + 2, :].rearrange("p h d -> p (h d)"),
                                               bh_tok[rows, i, g * P:(g + 1) * P], start=True, stop=True)
                    mm.then_inc(made[st], 1)

                def outputs_and_state(st, i):
                    n = i // 2
                    if i:
                        pe.wait_ge(y_out, i)
                    pe.wait_ge(kept_dve[st], upto(KEPT_DVE, n, "RT"))
                    for g in range(2):
                        for e in range(2):
                            hh = 2 * g + e
                            dst = ybank[e * HD:(e + 1) * HD, g * P:(g + 1) * P]
                            pe.matmul(dst, GU[:, st, 1, hh, :], part(st, hh, 1, 1), start=g == 0, stop=False,
                                      skip_group_check=True)
                            mm = pe.matmul(dst, v_tok[:, i, hh * HD:(hh + 1) * HD], part(st, hh, 0, 1),
                                           start=False, stop=i == 0, skip_group_check=True)
                    pe.wait_ge(kept_dve[st], upto(KEPT_DVE, n, "MT3"))
                    for cc in range(2):
                        c = 2 * i + cc
                        rows = slice(cc * CH, (cc + 1) * CH)
                        if c:
                            pe.wait_ge(s_done, c)
                            for g in range(2):
                                mm = pe.matmul(ybank[:, g * P + cc * CH:g * P + (cc + 1) * CH], S[:, c % 2, g, :],
                                               RT[:, st, g, cc * CH:(cc + 1) * CH], start=False, stop=True,
                                               skip_group_check=True)
                        if cc == 1:
                            mm.then_inc(y_done, 1)
                        if c == NCH - 1:
                            break
                        for g in range(2):
                            dst = zbank[:, g * P:(g + 1) * P]
                            pe.matmul(dst, bh_tok[rows, i, g * P:(g + 1) * P], GU[rows, st, 1, 2 * g:2 * g + 2, :].rearrange("p h d -> p (h d)"),
                                      start=g == 0, stop=False, skip_group_check=True)
                            mm = pe.matmul(dst, kh_tok[rows, i, g * P:(g + 1) * P], v_tok[rows, i, g * P:(g + 1) * P],
                                           start=False, stop=c == 0, skip_group_check=True)
                            if c:
                                mm = pe.matmul(dst, MT[:, st, 2 * cc + g, :], S[:, c % 2, g, :],
                                               start=False, stop=True, skip_group_check=True)
                        mm.then_inc(z_done, 1)

                for i in range(0, NT, 2):
                    for name in MADE:
                        for st in range(2):
                            step(name, st, i + st)
                    for st in range(2):
                        outputs_and_state(st, i + st)
                pe.wait_ge(y_out, NT)
                for u in range(4):
                    g, half = u // 2, u % 2
                    pe.matmul(bank[u][:], C("head_mean"), pm[:, (R0, R1)[g], half * HALF:(half + 1) * HALF],
                              start=True, stop=True).then_inc(mean_done, 1)
                for u in range(4):
                    pe.wait_ge(squared, u + 1)
                    pe.matmul(bank[4 + u][:], C("head_mean"), y2[:, u, :], start=True, stop=True).then_inc(var_done, 1)

            @block.scalar
            def _(act):
                def step(name, st, i):
                    n = i // 2
                    B = bank[3 * st:3 * st + 3]
                    done = kept_act[st]
                    act.wait_ge(made[st], upto(MADE, n, "turn" if name in ("a_tok", "bh_tok") else name))
                    if name == "a_tok":
                        act.copy(XR[:, i, :, 0, :], B[0][:, 0:256].rearrange("p (h d) -> p h d", h=4)).then_inc(done, 1)
                    elif name == "bh_tok":
                        act.copy(bh_tok[:, i, :], B[0][:, 256:512]).then_inc(done, 1)
                    elif name[0] == "X":
                        act.copy(X[:, st, :, :], cols4(B[0][:])).then_inc(done, 1)
                    elif name[0] == "T":
                        act.copy(Tm[:, st, :, :], cols4(B[1][:])).then_inc(done, 1)
                    else:
                        act.copy(GU[:, st, :, :, :].rearrange("p a h d -> p h a d"),
                                 B[1][:].rearrange("p (h a d) -> p h a d", h=4, a=2)).then_inc(done, 1)

                for i in range(0, NT, 2):
                    for name in KEPT_ACT:
                        for st in range(2):
                            step(name, st, i + st)
                    for st in range(2):
                        act.wait_ge(y_done, i + st + 1)
                        cols = slice((i + st) * P, (i + st + 1) * P)
                        for g in range(2):
                            ins = act.copy(pm[:, (R0, R1)[g], cols], ybank[:, g * P:(g + 1) * P])
                        ins.then_inc(y_out, 1)
                for u in range(4):
                    act.wait_ge(centred, u + 1)
                    act.activation(y2[:, u, :], yc[:, u, :], ACT.Square).then_inc(squared, 1)
                for u in range(4):
                    act.wait_ge(var_done, u + 1)
                    act.activation(y2[:, u, :], bank[4 + u][:], ACT.Sqrt, bias=GN_EPS).then_inc(gn_std, 1)

            @block.vector
            def _(dve):
                def step(name, st, i):
                    n = i // 2
                    B = bank[3 * st:3 * st + 3]
                    done = kept_dve[st]
                    was_made = lambda x: dve.wait_ge(made[st], upto(MADE, n, x))
                    own = lambda x: dve.wait_ge(done, upto(KEPT_DVE, n, x))
                    if name == "kh_tok":
                        was_made("turn")
                        dve.tensor_copy(kh_tok[:, i, :], B[1][:, 0:256]).then_inc(done, 1)
                    elif name == "v_tok":
                        dve.tensor_copy(v_tok[:, i, :], B[1][:, 256:512]).then_inc(done, 1)
                    elif name == "AV":
                        was_made("AV")
                        dve.tensor_copy(XR[:, i, :, 1, :],
                                        B[1][:, 0:256].rearrange("p (h d) -> p h d", h=4)).then_inc(done, 1)
                    elif name[0] == "A":
                        was_made(name)
                        if name == "A0" and i >= 2:
                            dve.wait_ge(y_done, i - 1)
                        dve.tensor_tensor(Am[:, st, int(name[1]), :], B[int(name[1]) % 3][:], C("chunk_mask"),
                                          ALU.mult).then_inc(done, 1)
                    elif name == "level0":
                        own("A3")
                        dve.tensor_tensor(XT[:, st, :, :], Am[:, st, :, 256:256 + P],
                                          bcast(C("level0"), [0, 4], [1, P]), ALU.mult).then_inc(done, 1)
                    elif name == "XT0":
                        own("level0")
                        dve.tensor_tensor(XT[:, st, :, :], XT[:, st, :, :], bcast(C("ident"), [0, 4], [1, P]),
                                          ALU.add).then_inc(done, 1)
                    elif name[0] == "Y":
                        was_made(name)
                        level = int(name[1]) - 1
                        dve.copy_predicated(XT[:, st, :, :], bcast(masks[:, level * P:(level + 1) * P], [0, 4], [1, P]),
                                            cols4(B[2][:])).then_inc(done, 1)
                    elif name == "RT":
                        was_made("RT")
                        dve.tensor_tensor(RT[:, st, :, :], B[2][:, 0:256].rearrange("p (g t) -> p g t", g=2),
                                          AR[:, :, i, 1, :], ALU.add).then_inc(done, 1)
                    else:
                        was_made("MT")
                        q = int(name[2])
                        cc, g = q // 2, q % 2
                        dve.scalar_tensor_tensor(MT[:, st, q, :], C("ident"), PT[:, g, 2 * i + cc:2 * i + cc + 1],
                                                 B[cc][:, g * P:(g + 1) * P], ALU.mult, ALU.add).then_inc(done, 1)

                for i in range(0, NT, 2):
                    for name in KEPT_DVE:
                        for st in range(2):
                            step(name, st, i + st)
                    for c in range(2 * i, min(2 * i + 4, NCH - 1)):
                        dve.wait_ge(z_done, c + 1)
                        dve.tensor_tensor(S[:, (c + 1) % 2, :, :], zbank[:, 0:256].rearrange("p (g v) -> p g v", g=2),
                                          bcast(C("head_ones"), [0, 2], [1, P]), ALU.mult).then_inc(s_done, 1)
                for u in range(4):
                    g, half = u // 2, u % 2
                    dve.wait_ge(mean_done, u + 1)
                    dve.tensor_tensor(yc[:, u, :], pm[:, (R0, R1)[g], half * HALF:(half + 1) * HALF], bank[u][:],
                                      ALU.subtract).then_inc(centred, 1)
                n = 0
                for u in range(4):
                    g, half = u // 2, u % 2
                    hs = slice(half * HALF, (half + 1) * HALF)
                    dve.wait_ge(gn_std, u + 1)
                    for k in range(5):
                        if k == 0:
                            ins = dve.reciprocal(y2[:, u, :], y2[:, u, :])
                        elif k == 1:
                            ins = dve.tensor_tensor(yc[:, u, :], yc[:, u, :], y2[:, u, :], ALU.mult)
                        elif k == 2:
                            ins = dve.tensor_scalar(yc[:, u, :], yc[:, u, :], C("lnx_g", g), C("lnx_b", g), ALU.mult, ALU.add)
                        elif k == 3:
                            ins = dve.tensor_tensor(yc[:, u, :], yc[:, u, :], bonus[:, g, hs], ALU.add)
                        else:
                            ins = dve.tensor_tensor(mixT[:, 3 + g, hs], yc[:, u, :], gT[:, g, hs], ALU.mult)
                        ins.then_inc(gn_chain, 1)
                        n += 1
                        dve.wait_ge(gn_chain, n)


UNITS = [(h, qg, kb) for h in range(6) for qg in range(2) for kb in range(4 * qg + 3, -1, -1)]


def attend(nc, ctx, w_out_d, w_out, w_out_in, qk_dram, toep_dram, rel_d, hot_d, sinks_d, C, masks, v_tok, mixT, mem):
    sem = lambda n: ctx.enter_context(nc.semaphore(n))
    qk = mem.put("qk", [P, 2, 2, T])
    ring = 3
    ex = mem.put("exp_z", [P, ring, HALF])
    sp = mem.put("softplus", [P, ring, HALF])
    w = mem.put("weights", [P, ring, HALF])
    acc = mem.put("later_softplus", [P, 2, HALF])
    zeros = mem.put("zeros", [P, P])
    qa = mem.put("window_qk", [P, 4, T])
    rel = mem.put("rel_bias", [32, 8])
    hot = mem.put("bucket_one_hot", [32, 2, N_TOEPLITZ])
    toep = mem.put("toeplitz_rows", [8, N_TOEPLITZ])
    bias = mem.put("bias", [P, 6, 256])
    sink = mem.put("sink", [P, 8])
    L = mem.put("logits", [P, 6, 256])
    Pr = mem.put("probs", [P, 6, 256])
    PrT = mem.put("probs_T", [P, 12, P])
    st = mem.put("softmax_stats", [P, 6, 8])
    qk_in = [sem("qk_in0"), sem("qk_in1")]
    qa_in, rel_in, acc_zero = sem("qa_in"), sem("rel_in"), sem("acc_zero")
    z_done, e_done, l_done, sp_raw, sp_done = (sem(f"sb_{n}") for n in ("z", "exp", "log", "sp_raw", "sp"))
    acc_done, s_done, w_raw, w_done, av_done, o_out = (sem(f"sb_{n}") for n in ("acc", "s", "w_raw", "w", "av", "o"))
    zero_done, toep_made, toep_kept, toep_out, bias_in = (sem(n) for n in ("zero_done", "toep_made", "toep_kept", "toep_out", "bias_in"))
    l_made, l_kept, stat, p_done, p_norm, pT_made, pT_kept, o_made, o_kept = (
        sem(f"win_{n}") for n in ("l_made", "l_kept", "stat", "p", "p_norm", "pT_made", "pT_kept", "o_made", "o_kept"))

    groups = [(h, qg) for h in range(6) for qg in range(2)]
    diag = [kb >= 4 * qg for _, qg, kb in UNITS]
    first = [kb == 4 * qg + 3 for _, qg, kb in UNITS]
    last = [kb == 0 for _, _, kb in UNITS]
    place = [4 * qg + 3 - kb for _, qg, kb in UNITS]
    c0 = [max(0, (kb - 4 * qg) * P) for _, qg, kb in UNITS]
    N = len(UNITS)
    diags = [sum(diag[:u + 1]) for u in range(N)]
    adds = [sum(not x for x in last[:u + 1]) for u in range(N)]
    group_of = [groups.index((h, qg)) for h, qg, _ in UNITS]

    with ExitStack() as inner:
        zb = [inner.enter_context(nc.psum_tensor(f"z{b}", [P, HALF], F32)) for b in range(4)]
        ob = [inner.enter_context(nc.psum_tensor(f"o{b}", [P, HALF], F32)) for b in range(2)]
        tb = inner.enter_context(nc.psum_tensor("toep_bank", [P, HALF], F32))
        with nc.Block() as block:
            @block.sync
            def _(sp_):
                sp_.dma_start(w_out[:].rearrange("p k d -> p (k d)"), w_out_d).then_inc(w_out_in, 16)
                sp_.dma_start(rel[:, 0:6], rel_d).then_inc(rel_in, 16)
                sp_.dma_start(hot[:].rearrange("p a m -> p (a m)"), hot_d).then_inc(rel_in, 16)
                sp_.dma_start(sink[:, 0:6], sinks_d.to_broadcast([P, 6])).then_inc(rel_in, 16)
                for t in range(3):
                    if t == 2:
                        sp_.wait_ge(av_done, 24)
                    sp_.dma_start(qk[:, t % 2, 0, :], qk_dram[t]).then_inc(qk_in[t % 2], 16)
                    sp_.dma_start(qk[:, t % 2, 1, :], qk_dram[3 + t]).then_inc(qk_in[t % 2], 16)
                    if t == 1:
                        for k in range(4):
                            sp_.dma_start(qa[:, k, :], qk_dram[6 + k]).then_inc(qa_in, 16)
                        sp_.wait_ge(toep_kept, 1)
                        sp_.dma_start(toep_dram, toep[0:6, :].unsqueeze(1).to_broadcast([6, P, N_TOEPLITZ])).then_inc(toep_out, 16)
                        sp_.wait_ge(toep_out, 16)
                        sp_.dma_start(bias[:], bass.AP(toep_dram.tensor, 127, [[N_TOEPLITZ - 1, P], [P * N_TOEPLITZ, 6], [1, 256]])
                                      ).then_inc(bias_in, 16)

            @block.tensor
            def _(pe):
                pe.wait_ge(rel_in, 48)
                pe.matmul(tb[0:6, 0:N_TOEPLITZ], rel[:, 0:6], hot[:, 0, :], start=True, stop=True).then_inc(toep_made, 1)

                def scores(u):
                    h, qg, kb = UNITS[u]
                    rows, t = slice((h % 2) * HD, (h % 2 + 1) * HD), h // 2
                    pe.wait_ge(qk_in[t % 2], 32 * (t // 2 + 1))
                    if u >= 4:
                        pe.wait_ge(w_raw, u - 3)
                    pe.matmul(zb[u % 4][:, c0[u]:], qk[rows, t % 2, 1, kb * P:(kb + 1) * P],
                              qk[rows, t % 2, 0, qg * HALF + c0[u]:(qg + 1) * HALF],
                              start=True, stop=True).then_inc(z_done, 1)

                def suffix(u):
                    pe.wait_ge(sp_done, u + 1)
                    mm = pe.matmul(zb[u % 4][:, c0[u]:], C("suffix"), sp[:, u % ring, c0[u]:], start=False, stop=True,
                                   skip_group_check=True)
                    if not first[u]:
                        pe.wait_ge(acc_done, adds[u - 1])
                        from_ = c0[u] + P if diag[u] else 0
                        mm = pe.matmul(zb[u % 4][:, from_:], C("all_later"), acc[:, place[u] % 2, from_:],
                                       start=False, stop=True, skip_group_check=True)
                    mm.then_inc(s_done, 1)

                def values(u):
                    h, qg, kb = UNITS[u]
                    g = group_of[u]
                    pe.wait_ge(w_done, u + 1)
                    if first[u] and g >= 2:
                        pe.wait_ge(o_out, g - 1)
                    rows = slice((h % 2) * HD, (h % 2 + 1) * HD)
                    pe.matmul(ob[g % 2][rows, c0[u]:], v_tok[:, kb, h * HD:(h + 1) * HD], w[:, u % ring, c0[u]:],
                              start=first[u], stop=last[u], skip_group_check=True).then_inc(av_done, 1)

                scores(0)
                for u in range(N + 1):
                    if u + 1 < N:
                        scores(u + 1)
                    if u < N:
                        suffix(u)
                    if u:
                        values(u - 1)

            @block.scalar
            def _(act):
                def weights(u):
                    act.wait_ge(s_done, u + 1)
                    if u >= ring:
                        act.wait_ge(av_done, u - ring + 1)
                    act.activation(w[:, u % ring, c0[u]:], zb[u % 4][:, c0[u]:], ACT.Exp).then_inc(w_raw, 1)

                act.preload_act_table_set("natural_log_exp_and_others")
                for u in range(N + 1):
                    if u < N:
                        act.wait_ge(z_done, u + 1)
                        if u >= ring:
                            act.wait_ge(sp_raw, u - ring + 1)
                        b = ex[:, u % ring, c0[u]:]
                        act.activation(b, zb[u % 4][:, c0[u]:], ACT.Exp).then_inc(e_done, 1)
                        act.wait_ge(e_done, u + 1)
                        act.activation(b, b, ACT.Ln, bias=1.0).then_inc(l_done, 1)
                    if u:
                        weights(u - 1)

            @block.vector
            def _(dve):
                dve.memset(zeros[:], 0.0).then_inc(zero_done, 1)
                dve.wait_ge(toep_made, 1)
                dve.tensor_tensor(toep[0:6, :], tb[0:6, 0:N_TOEPLITZ], hot[0:6, 1, :], ALU.add).then_inc(toep_kept, 1)
                dve.wait_ge(zero_done, 1)
                for u in range(N + 1):
                    if u < N:
                        dve.wait_ge(l_done, u + 1)
                        if u >= ring:
                            dve.wait_ge(s_done, u - ring + 1)
                            dve.wait_ge(acc_done, adds[u - ring])
                        d = slice(c0[u], c0[u] + P)
                        dve.scalar_tensor_tensor(sp[:, u % ring, c0[u]:], ex[:, u % ring, c0[u]:], CLAMP,
                                                 zb[u % 4][:, c0[u]:], ALU.min, ALU.max).then_inc(sp_raw, 1)
                        dve.wait_ge(sp_raw, u + 1)
                        if diag[u]:
                            dve.tensor_tensor(sp[:, u % ring, d], sp[:, u % ring, d], C("key_before"),
                                              ALU.mult).then_inc(sp_done, 1)
                        else:
                            dve.nop().then_inc(sp_done, 1)
                    if u:
                        v = u - 1
                        dve.wait_ge(w_raw, v + 1)
                        if diag[v]:
                            dve.copy_predicated(w[:, v % ring, c0[v]:c0[v] + P], masks[:, N_LEVELS * P:(N_LEVELS + 1) * P],
                                                zeros[:]).then_inc(w_done, 1)
                        else:
                            dve.nop().then_inc(w_done, 1)
                        if last[v]:
                            h, qg, _ = UNITS[v]
                            g = group_of[v]
                            rows = slice((h % 2) * HD, (h % 2 + 1) * HD)
                            dve.wait_ge(av_done, v + 1)
                            dve.tensor_copy(mixT[rows, 5 + h // 2, qg * HALF:(qg + 1) * HALF], ob[g % 2][rows, :]
                                            ).then_inc(o_out, 1)

            @block.gpsimd
            def _(pool):
                n = 0
                for u in range(N):
                    if first[u]:
                        if u:
                            pool.wait_ge(s_done, u)
                        for b in range(2):
                            pool.memset(acc[:, b, :], 0.0).then_inc(acc_zero, 1)
                        n += 2
                        pool.wait_ge(acc_zero, n)
                    if last[u]:
                        continue
                    pool.wait_ge(sp_done, u + 1)
                    k = place[u]
                    if k >= 1:
                        pool.wait_ge(s_done, u)
                        pool.wait_ge(acc_done, adds[u - 1])
                    pool.tensor_tensor(acc[:, (k + 1) % 2, c0[u]:], acc[:, k % 2, c0[u]:], sp[:, u % ring, c0[u]:],
                                       ALU.add).then_inc(acc_done, 1)

    with ExitStack() as inner:
        lb = inner.enter_context(nc.psum_tensor("logit_banks", [P, 4 * HALF], F32))
        pTb = inner.enter_context(nc.psum_tensor("prob_banks", [P, 3 * HALF], F32))
        ob = inner.enter_context(nc.psum_tensor("out_bank", [P, HALF], F32))
        keys = [slice(P, 256) if n == 0 else slice(0, 256) for n in range(NT)]
        with nc.Block() as block:
            @block.tensor
            def _(pe):
                pe.wait_ge(qa_in, 64)

                def logits(n):
                    if n:
                        pe.wait_ge(l_kept, n)
                    lo = keys[n].start
                    for e in range(2):
                        rows = slice(e * HD, (e + 1) * HD)
                        for j in range(3):
                            at = e * 2 * HALF + j * 256
                            mm = pe.matmul(lb[:, at + lo:at + 256], qa[rows, j, n * P:(n + 1) * P],
                                           qa[rows, 3, (n - 1) * P + lo:(n + 1) * P], start=True, stop=True)
                    mm.then_inc(l_made, 1)

                def outputs(n):
                    pe.wait_ge(p_norm, n + 1)
                    blocks = (1,) if n == 0 else (0, 1)
                    if n:
                        pe.wait_ge(pT_kept, n)
                    for h in range(6):
                        for kb in blocks:
                            mm = pe.transpose(pTb[:, (2 * h + kb) * P:(2 * h + kb + 1) * P],
                                              Pr[:, h, kb * P:(kb + 1) * P], C("ident"))
                    mm.then_inc(pT_made, 1)
                    pe.wait_ge(pT_kept, n + 1)
                    if n:
                        pe.wait_ge(o_kept, n)
                    for h in range(6):
                        e, j = h // 3, h % 3
                        for kb in blocks:
                            mm = pe.matmul(ob[e * HD:(e + 1) * HD, j * P:(j + 1) * P],
                                           v_tok[:, n - 1 + kb, 384 + e * HD:384 + (e + 1) * HD], PrT[:, 2 * h + kb, :],
                                           start=kb == blocks[0], stop=kb == 1)
                    mm.then_inc(o_made, 1)

                logits(0)
                for n in range(NT):
                    if n + 1 < NT:
                        logits(n + 1)
                    outputs(n)

            @block.scalar
            def _(act):
                for n in range(NT):
                    act.wait_ge(stat, 6 * n + 4)
                    if n:
                        act.wait_ge(pT_made, n)
                    for h in range(6):
                        act.activation(Pr[:, h, keys[n]], L[:, h, keys[n]], ACT.Exp, bias=st[:, 1, h:h + 1],
                                       accum_out=st[:, 2, h:h + 1])
                    act.activation(st[:, 3, 0:6], st[:, 3, 0:6], ACT.Exp).then_inc(p_done, 1)
                    act.wait_ge(pT_made, n + 1)
                    if n:
                        act.wait_ge(o_made, n)
                    if n == 0:
                        act.copy(PrT[:].rearrange("p (h k) q -> p h k q", k=2)[:, :, 1, :],
                                 pTb[:].rearrange("p (h k q) -> p h k q", h=6, k=2)[:, :, 1, :]).then_inc(pT_kept, 1)
                    else:
                        act.copy(PrT[:].rearrange("p a q -> p (a q)"), pTb[:]).then_inc(pT_kept, 1)

            @block.vector
            def _(dve):
                dve.wait_ge(bias_in, 16)
                dve.wait_ge(rel_in, 48)
                for n in range(NT):
                    dve.wait_ge(l_made, n + 1)
                    if n:
                        dve.wait_ge(p_done, n)
                    k = keys[n]
                    logit = lb[:].rearrange("p (e x) -> p e x", e=2)[:, :, 0:768].rearrange("p e (j k) -> p e j k", j=3)
                    dve.tensor_tensor(L[:].rearrange("p (e j) k -> p e j k", e=2)[:, :, :, k], logit[:, :, :, k],
                                      bias[:].rearrange("p (e j) k -> p e j k", e=2)[:, :, :, k], ALU.add).then_inc(l_kept, 1)
                    dve.wait_ge(l_kept, n + 1)
                    m, neg, total, at_sink, both, inv = (st[:, j, 0:6] for j in range(6))
                    for j in range(6):
                        if j == 0:
                            ins = dve.tensor_reduce(m, L[:, :, k], AX, ALU.max)
                        elif j == 1:
                            ins = dve.tensor_tensor(m, m, sink[:, 0:6], ALU.max)
                        elif j == 2:
                            ins = dve.tensor_scalar(neg, m, -1.0, None, ALU.mult)
                        elif j == 3:
                            ins = dve.tensor_tensor(at_sink, sink[:, 0:6], neg, ALU.add)
                        elif j == 4:
                            dve.wait_ge(p_done, n + 1)
                            ins = dve.tensor_tensor(both, total, at_sink, ALU.add)
                        else:
                            ins = dve.reciprocal(inv, both)
                        ins.then_inc(stat, 1)
                        if j != 3:
                            dve.wait_ge(stat, 6 * n + j + 1)
                    width = k.stop - k.start
                    dve.tensor_tensor(Pr[:, :, k], Pr[:, :, k], bcast(inv, [1, 6], [0, width]), ALU.mult).then_inc(p_norm, 1)
                    dve.wait_ge(o_made, n + 1)
                    dve.tensor_copy(mixT[:, 0:3, n * P:(n + 1) * P],
                                    ob[:, 0:3 * P].rearrange("p (j q) -> p j q", j=3)).then_inc(o_kept, 1)


N_EXPERTS, N_GROUPS, PER_GROUP, TOP_K, FF = 16, 4, 4, 2, 256
MAX_BLOCKS = TOP_K * T // P + N_EXPERTS - 1 + 1
MIN_BLOCKS = TOP_K * T // P
PLAN_ENDS = MAX_BLOCKS + 1
PLAN = PLAN_ENDS + N_EXPERTS
N_WBUF = 3
SLOT_BLOCKS = MAX_BLOCKS + 1
BIG = 1e30

ROUTE = {"iota16": (0, 16), "group16": (16, 16), "iota4": (32, 4), "edges": (36, 8), "blocks": (48, 32)}


def routing_constants():
    c = np.zeros((1, 80), np.float32)
    c[0, 0:16] = np.arange(16)
    c[0, 16:32] = np.arange(16) // PER_GROUP
    c[0, 32:36] = np.arange(4)
    c[0, 36:44] = np.arange(8) * P
    c[0, 48:80] = np.arange(32)
    return c


def mix_and_route(nc, ctx, h_dram, h1_dram, slot_dram, rows4, rw_d, rb_d, route_d, C, mixT, w_out, w_out_in, K, mem):
    sem = lambda n: ctx.enter_context(nc.semaphore(n))
    h1, rows, gates, slots, plan = K["h1"], K["rows"], K["gates"], K["slots"], K["plan"]
    hb = mem.put("h_in", [P, 2, D])
    r = mem.put("residual", [P, 2, D])
    xT = mem.put("h1_T", [P, ND, P])
    rw = mem.put("router_w", [P, ND, 16])
    rb = mem.put("router_bias", [P, 16])
    rc = mem.put("route_consts", [P, 80])
    stats = mem.put("ln1_stats", [P, 12])
    mv = mem.put("ln1_mv", [P, NT, 2])
    std = mem.put("ln1_std", [P, NT, 2])
    ids = mem.put("token_ids", [P, TOP_K, NT, 2], I32)
    free_ids = mem.put("free_ids", [P, SLOT_BLOCKS, 2], I32)
    big = lambda n: mem.put(n, [P, NT, 16])
    score, sel, selm, t16, oh1, oh2, both, base, rank = (
        big(n) for n in ("score", "sel", "sel_in_group", "t16", "first_choice", "second_choice", "both", "base", "rank"))
    n_e = mem.put("n_e", [P, 16])
    hi = mem.put("hi", [P, NT, 4, 2])
    lo = mem.put("lo", [P, NT, 4, 2])
    g4 = mem.put("g4", [P, 3, NT, 4])
    t8 = mem.put("t8", [P, 6, NT])
    cmp_ = mem.put("block_compare", [P, 32, 16])
    e16 = mem.put("e16", [P, 4, 16])
    plan_f = mem.put("plan_f", [P, PLAN])
    h_in = [sem("h_in0"), sem("h_in1")]
    par_in = sem("route_in")
    m_made, resid, ln_stat, ln_aggr, ln_std, ln_rstd, xn = (sem(f"ln1_{n}") for n in (
        "m", "resid", "stat", "aggr", "std", "rstd", "xn"))
    xT_made, xT_kept, r_made, h1_mul, h1_done = (sem(n) for n in ("rt_xT_made", "rt_xT_kept", "rt_made", "h1_mul", "h1_done"))
    h1_out, free_out, ids_done, slots_out = sem("h1_out"), sem("slots_freed"), sem("ids_done"), sem("slots_out")
    scored, routed, counted, ranked = sem("scored"), sem("routed"), sem("counted"), sem("ranked")
    with ExitStack() as inner:
        mb = [inner.enter_context(nc.psum_tensor(f"m{b}", [P, HALF], F32)) for b in range(4)]
        xb = [inner.enter_context(nc.psum_tensor(f"rx{b}", [P, HALF], F32)) for b in range(2)]
        rbk = inner.enter_context(nc.psum_tensor("router_bank", [P, HALF], F32))
        cb = inner.enter_context(nc.psum_tensor("count_bank", [P, HALF], F32))
        with nc.Block() as block:
            @block.sync
            def _(sp):
                for k in range(4):
                    sp.dma_start(rows[:, k, :], rows4[k:k + 1, :].to_broadcast([P, D])).then_inc(par_in, 16)
                sp.dma_start(rw[:].rearrange("p k e -> p (k e)"), rw_d).then_inc(par_in, 16)
                sp.dma_start(rb[:], rb_d.to_broadcast([P, 16])).then_inc(par_in, 16)
                sp.dma_start(rc[:], route_d.to_broadcast([P, 80])).then_inc(par_in, 16)
                sp.wait_ge(ids_done, 2 * TOP_K + 2)
                sp.dma_start(slot_dram.rearrange("(p b) two -> p (b two)", p=P),
                             free_ids[:].rearrange("p b two -> p (b two)")).then_inc(free_out, 16)
                for i in range(NT):
                    if i >= 2:
                        sp.wait_ge(resid, 2 * (i - 1))
                    sp.dma_start(hb[:, i % 2, :], h_dram[i * P:(i + 1) * P, :]).then_inc(h_in[i % 2], 16)
                    if i >= 2:
                        sp.wait_ge(h1_done, i - 1)
                        sp.dma_start(h1_dram[(i - 2) * P:(i - 1) * P, :], h1[:, i - 2, :]).then_inc(h1_out, 16)
                for i in range(NT - 2, NT):
                    sp.wait_ge(h1_done, i + 1)
                    sp.dma_start(h1_dram[i * P:(i + 1) * P, :], h1[:, i, :]).then_inc(h1_out, 16)
                sp.wait_ge(h1_out, 16 * NT)

            @block.tensor
            def _(pe):
                def mix(i):
                    for half in range(2):
                        n = 2 * i + half
                        if n >= 4:
                            pe.wait_ge(resid, n - 3)
                        for k in range(ND):
                            mm = pe.matmul(mb[n % 4][:], mixT[:, k, i * P:(i + 1) * P],
                                           w_out[:, k, half * HALF:(half + 1) * HALF], start=k == 0, stop=k == ND - 1)
                        mm.then_inc(m_made, 1)

                def router(i):
                    pe.wait_ge(xn, i + 1)
                    if i:
                        pe.wait_ge(xT_kept, ND * i)
                    for d in range(ND):
                        mm = pe.transpose(xb[d // 4][:, (d % 4) * P:(d % 4 + 1) * P], r[:, i % 2, d * P:(d + 1) * P], C("ident"))
                    mm.then_inc(xT_made, 1)
                    pe.wait_ge(xT_kept, ND * (i + 1))
                    for d in range(ND):
                        mm = pe.matmul(rbk[:, i * 16:(i + 1) * 16], xT[:, d, :], rw[:, d, :], start=d == 0, stop=d == ND - 1)
                    mm.then_inc(r_made, 1)

                pe.wait_ge(w_out_in, 16)
                pe.wait_ge(par_in, 16 * 7)
                mix(0)
                mix(1)
                for i in range(NT):
                    if i + 2 < NT:
                        mix(i + 2)
                    router(i)
                pe.wait_ge(routed, ROUTED["both"])
                pe.matmul(cb[:, 0:P], C("key_before"), both[:].rearrange("p i e -> p (i e)"), start=True, stop=True)
                pe.matmul(cb[:, P:2 * P], C("ones"), both[:].rearrange("p i e -> p (i e)"), start=True, stop=True).then_inc(counted, 1)

            @block.scalar
            def _(act):
                for i in range(NT):
                    act.wait_ge(ln_aggr, i + 1)
                    act.activation(std[:, i, 0:1], mv[:, i, 1:2], ACT.Sqrt, bias=LN_EPS).then_inc(ln_std, 1)
                    act.wait_ge(xT_made, i + 1)
                    if i:
                        act.wait_ge(r_made, i)
                    for d in range(ND):
                        act.activation(xT[:, d, :], xb[d // 4][:, (d % 4) * P:(d % 4 + 1) * P], ACT.Identity,
                                       bias=C("ln1_b", d), scale=C("ln1_g", d)).then_inc(xT_kept, 1)
                act.wait_ge(r_made, NT)
                act.activation(score[:].rearrange("p i e -> p (i e)"), rbk[:, 0:P], ACT.Sigmoid).then_inc(scored, 1)

            @block.gpsimd
            def _(pool):
                for k in range(TOP_K):
                    pool.iota(ids[:, k, :, 0], pattern=[[P, NT]], base=0, channel_multiplier=1).then_inc(ids_done, 1)
                    pool.iota(ids[:, k, :, 1], pattern=[[P, NT]], base=k * T, channel_multiplier=1).then_inc(ids_done, 1)
                pool.memset(free_ids[:, :, 0], 0).then_inc(ids_done, 1)
                pool.memset(free_ids[:, :, 1], TOP_K * T).then_inc(ids_done, 1)
                pool.wait_ge(par_in, 16 * 7)
                for i in range(NT):
                    pool.wait_ge(xn, i + 1)
                    pool.tensor_tensor(h1[:, i, :], r[:, i % 2, :], rows[:, 0, :], ALU.mult).then_inc(h1_mul, 1)
                    pool.wait_ge(h1_mul, i + 1)
                    pool.tensor_tensor(h1[:, i, :], h1[:, i, :], rows[:, 1, :], ALU.add).then_inc(h1_done, 1)
                pool.wait_ge(free_out, 16)
                pool.wait_ge(routed, len(ROUTE_STEPS))
                for i in range(NT):
                    for k in range(TOP_K):
                        pool.indirect_dma_start(slot_dram, bass.IndirectOffsetOnAxis(ap=slots[:, k, i:i + 1], axis=0),
                                                ids[:, k, i, :], None).then_inc(slots_out, 16)
                pool.wait_ge(slots_out, 16 * NT * TOP_K)

            @block.vector
            def _(dve):
                dve.wait_ge(par_in, 16 * 7)
                for i in range(NT):
                    dve.wait_ge(h_in[i % 2], 16 * (i // 2 + 1))
                    if i >= 2:
                        dve.wait_ge(h1_mul, i - 1)
                        dve.wait_ge(xT_made, i - 1)
                    for half in range(2):
                        hs = slice(half * HALF, (half + 1) * HALF)
                        dve.wait_ge(m_made, 2 * i + half + 1)
                        dve.scalar_tensor_tensor(r[:, i % 2, hs], hb[:, i % 2, hs], ALPHA, mb[(2 * i + half) % 4][:],
                                                 ALU.mult, ALU.add).then_inc(resid, 1)
                        dve.wait_ge(resid, 2 * i + half + 1)
                        dve.bn_stats(stats[:, 6 * half:6 * half + 6], r[:, i % 2, hs]).then_inc(ln_stat, 1)
                    dve.wait_ge(ln_stat, 2 * i + 2)
                    dve.bn_aggr(mv[:, i, :], stats[:]).then_inc(ln_aggr, 1)
                    dve.wait_ge(ln_std, i + 1)
                    dve.reciprocal(std[:, i, 1:2], std[:, i, 0:1]).then_inc(ln_rstd, 1)
                    dve.wait_ge(ln_rstd, i + 1)
                    dve.tensor_scalar(r[:, i % 2, :], r[:, i % 2, :], mv[:, i, 0:1], std[:, i, 1:2],
                                      ALU.subtract, ALU.mult).then_inc(xn, 1)
                row = lambda n: rc[:, ROUTE[n][0]:ROUTE[n][0] + ROUTE[n][1]]
                per_token = lambda ap: bcast(ap, [1, NT], [0, 16])
                sel4 = sel[:].rearrange("p i (g e) -> p i g e", e=PER_GROUP)
                top, second, gsum = (g4[:, k, :, :] for k in range(3))
                gbest, m1, m2, w1, w2, wsum = (t8[:, k, :] for k in range(6))
                blocks, ends, starts, _ = (e16[:, k, :] for k in range(4))
                n = 0
                for name in ROUTE_STEPS:
                    if n:
                        dve.wait_ge(routed, n)
                    if name == "sel":
                        dve.wait_ge(scored, 1)
                        ins = dve.tensor_tensor(sel[:], score[:], bcast(rb[:], [0, NT], [1, 16]), ALU.add)
                    elif name == "hi":
                        ins = dve.tensor_tensor(hi[:], sel4[:, :, :, 0:2], sel4[:, :, :, 2:4], ALU.max)
                    elif name == "lo":
                        ins = dve.tensor_tensor(lo[:], sel4[:, :, :, 0:2], sel4[:, :, :, 2:4], ALU.min)
                    elif name == "top":
                        ins = dve.tensor_tensor(top, hi[:, :, :, 0], hi[:, :, :, 1], ALU.max)
                    elif name == "hi_min":
                        ins = dve.tensor_tensor(second, hi[:, :, :, 0], hi[:, :, :, 1], ALU.min)
                    elif name == "lo_max":
                        ins = dve.tensor_tensor(gsum, lo[:, :, :, 0], lo[:, :, :, 1], ALU.max)
                    elif name == "second":
                        ins = dve.tensor_tensor(second, second, gsum, ALU.max)
                    elif name == "gsum":
                        ins = dve.tensor_tensor(gsum, top, second, ALU.add)
                    elif name == "gmax":
                        ins = dve.tensor_reduce(gbest, gsum, AX, ALU.max)
                    elif name == "g_is":
                        ins = dve.tensor_tensor(top, gsum, bcast(gbest, [1, NT], [0, 4]), ALU.is_equal)
                    elif name == "g_cand":
                        ins = dve.scalar_tensor_tensor(top, top, -100.0, bcast(row("iota4"), [0, NT], [1, 4]), ALU.mult, ALU.add)
                    elif name == "g_index":
                        ins = dve.tensor_reduce(gbest, top, AX, ALU.min)
                    elif name == "g_index2":
                        ins = dve.tensor_scalar(gbest, gbest, 100.0, None, ALU.add)
                    elif name == "in_group":
                        ins = dve.tensor_tensor(t16[:], bcast(row("group16"), [0, NT], [1, 16]), per_token(gbest), ALU.is_equal)
                    elif name == "outside":
                        ins = dve.tensor_scalar(t16[:], t16[:], BIG, -BIG, ALU.mult, ALU.add)
                    elif name == "selm":
                        ins = dve.tensor_tensor(selm[:], sel[:], t16[:], ALU.add)
                    elif name in ("max1", "max2"):
                        ins = dve.tensor_reduce(m1 if name == "max1" else m2, selm[:], AX, ALU.max)
                    elif name in ("is1", "is2"):
                        ins = dve.tensor_tensor(t16[:], selm[:], per_token(m1 if name == "is1" else m2), ALU.is_equal)
                    elif name in ("cand1", "cand2"):
                        ins = dve.scalar_tensor_tensor(t16[:], t16[:], -100.0, bcast(row("iota16"), [0, NT], [1, 16]),
                                                       ALU.mult, ALU.add)
                    elif name in ("index1", "index2"):
                        ins = dve.tensor_reduce(m1 if name == "index1" else m2, t16[:], AX, ALU.min)
                    elif name in ("found1", "found2"):
                        m = m1 if name == "found1" else m2
                        ins = dve.tensor_scalar(m, m, 100.0, None, ALU.add)
                    elif name in ("hot1", "hot2"):
                        ins = dve.tensor_tensor(oh1[:] if name == "hot1" else oh2[:], bcast(row("iota16"), [0, NT], [1, 16]),
                                                per_token(m1 if name == "hot1" else m2), ALU.is_equal)
                    elif name == "without1":
                        ins = dve.scalar_tensor_tensor(selm[:], oh1[:], -2 * BIG, selm[:], ALU.mult, ALU.add)
                    elif name == "both":
                        ins = dve.tensor_tensor(both[:], oh1[:], oh2[:], ALU.add)
                    elif name in ("s1", "s2"):
                        ins = dve.tensor_tensor(t16[:], oh1[:] if name == "s1" else oh2[:], score[:], ALU.mult)
                    elif name in ("w1", "w2"):
                        ins = dve.tensor_reduce(w1 if name == "w1" else w2, t16[:], AX, ALU.add)
                    elif name == "wsum":
                        ins = dve.tensor_tensor(wsum, w1, w2, ALU.add)
                    elif name == "wrec":
                        ins = dve.reciprocal(wsum, wsum)
                    elif name in ("gate1", "gate2"):
                        k = int(name[4]) - 1
                        ins = dve.tensor_tensor(gates[:, k, :], (w1, w2)[k], wsum, ALU.mult)
                    elif name == "base0":
                        dve.wait_ge(counted, 1)
                        ins = dve.memset(base[:, 0, :], 0.0)
                    elif name[:4] == "base":
                        i = int(name[4:])
                        dst = n_e[:] if i == NT else base[:, i, :]
                        ins = dve.tensor_tensor(dst, base[:, i - 1, :], cb[:, P + 16 * (i - 1):P + 16 * i], ALU.add)
                    elif name == "rank":
                        ins = dve.tensor_tensor(rank[:], cb[:, 0:P].rearrange("p (i e) -> p i e", i=NT), base[:], ALU.add)
                    elif name == "edges":
                        ins = dve.tensor_tensor(cmp_[:, 0:16, 0:8], bcast(n_e[:], [1, 16], [0, 8]),
                                                bcast(row("edges"), [0, 16], [1, 8]), ALU.is_gt)
                    elif name == "blocks":
                        ins = dve.tensor_reduce(blocks, cmp_[:, 0:16, 0:8], AX, ALU.add)
                    elif name == "ends":
                        ins = dve.tensor_tensor_scan(ends, C("ones")[:, 0:16], blocks, 0.0, ALU.mult, ALU.add)
                    elif name == "starts":
                        ins = dve.tensor_tensor(starts, ends, blocks, ALU.subtract)
                    elif name == "start_slots":
                        ins = dve.tensor_scalar(starts, starts, float(P), None, ALU.mult)
                    elif name == "slot":
                        ins = dve.tensor_tensor(rank[:], rank[:], bcast(starts, [0, NT], [1, 16]), ALU.add)
                    elif name in ("slot1", "slot2"):
                        ins = dve.tensor_tensor(t16[:], rank[:], oh1[:] if name == "slot1" else oh2[:], ALU.mult)
                    elif name in ("sum1", "sum2"):
                        ins = dve.tensor_reduce(m1 if name == "sum1" else m2, t16[:], AX, ALU.add)
                    elif name in ("int1", "int2"):
                        k = int(name[3]) - 1
                        ins = dve.tensor_copy(slots[:, k, :], (m1, m2)[k])
                    elif name == "ended":
                        ins = dve.tensor_tensor(cmp_[:], bcast(row("blocks"), [1, 32], [0, 16]),
                                                bcast(ends, [0, 32], [1, 16]), ALU.is_ge)
                    elif name == "expert":
                        ins = dve.tensor_reduce(plan_f[:, 0:32], cmp_[:], AX, ALU.add)
                    elif name == "expert_max":
                        ins = dve.tensor_scalar(plan_f[:, 0:32], plan_f[:, 0:32], float(N_EXPERTS - 1), None, ALU.min)
                    elif name == "total":
                        ins = dve.tensor_scalar(plan_f[:, MAX_BLOCKS:MAX_BLOCKS + 1], ends[:, 15:16], float(-MIN_BLOCKS), None, ALU.add)
                    elif name == "plan_ends":
                        ins = dve.tensor_copy(plan_f[:, PLAN_ENDS:PLAN], ends)
                    elif name == "plan":
                        ins = dve.tensor_copy(plan[:], plan_f[0:1, :])
                    ins.then_inc(routed, 1)
                    n += 1


ROUTE_STEPS = ["sel", "hi", "lo", "top", "hi_min", "lo_max", "second", "gsum", "gmax", "g_is", "g_cand", "g_index",
               "g_index2", "in_group", "outside", "selm", "max1", "is1", "cand1", "index1", "found1", "hot1",
               "without1", "max2", "is2", "cand2", "index2", "found2", "hot2", "both", "s1", "w1", "s2", "w2", "wsum",
               "wrec", "gate1", "gate2", "base0", "base1", "base2", "base3", "base4", "base5", "base6", "base7",
               "base8", "rank", "edges", "blocks", "ends", "starts", "start_slots", "slot", "slot1", "sum1", "int1",
               "slot2", "sum2", "int2", "ended", "expert", "expert_max", "total", "plan_ends", "plan"]
ROUTED = {name: k + 1 for k, name in enumerate(ROUTE_STEPS)}


def experts(nc, ctx, h1_dram, slot_dram, y_dram, wgu_d, wd_d, out, C, K, mem):
    sem = lambda n: ctx.enter_context(nc.semaphore(n))
    h1, rows, gates, slots, plan = K["h1"], K["rows"], K["gates"], K["slots"], K["plan"]
    WG = mem.put("w_gate_up", [P, N_WBUF, ND, 2 * FF])
    WD = mem.put("w_down", [P, N_WBUF, 2, D])
    idx = mem.put("slot_ids", [P, SLOT_BLOCKS, 2], I32)
    idx_x = mem.put("gather_ids", [P, 2, 2], I32)
    idx_y = mem.put("scatter_ids", [P, 2, 2], I32)
    turn = mem.put("turn", [P, 1])
    xg = mem.put("slot_rows", [P, 2, D])
    xT = mem.put("slot_rows_T", [P, ND, P])
    sg = mem.put("silu_gate", [P, FF])
    ac = mem.put("act", [P, FF])
    aT = mem.put("act_T", [P, 2, P])
    y = mem.put("slot_out", [P, 2, D])
    w_in = [sem(f"expert_in{b}") for b in range(N_WBUF)]
    w_ready, stored = sem("weights_ready"), sem("blocks_stored")
    x_in, y_out = ([sem(f"{n}{b}") for b in range(2)] for n in ("xg_in", "y_out"))
    idx_in, idx_x_made, idx_y_made = sem("idx_in"), sem("idx_x_made"), sem("idx_y_made")
    gu_made, xT_made, d_made, aT_made = sem("gu_made"), sem("xg_T_made"), sem("down_made"), sem("act_T_made")
    xT_act, xT_dve, silu_done, act_done, aT_kept = (sem(n) for n in ("xT_kept_act", "xT_kept_dve", "silu_done", "act_done", "act_T_kept"))
    y_act, y_dve = sem("y_kept_act"), sem("y_kept_dve")
    trips = lambda eng: eng.snap((eng.value_load(plan[0:1, MAX_BLOCKS:MAX_BLOCKS + 1], min_val=0,
                                                 max_val=MAX_BLOCKS - MIN_BLOCKS) + 1) // 2 + MIN_BLOCKS // 2,
                                 min_val=MIN_BLOCKS // 2, max_val=MAX_BLOCKS // 2)

    def wait(eng, s, value):
        if not isinstance(value, int) or value > 0:
            eng.wait_ge(s, value)
    with ExitStack() as inner:
        gub = inner.enter_context(nc.psum_tensor("gu_bank", [P, HALF], F32))
        xb = [inner.enter_context(nc.psum_tensor(f"xg_bank{b}", [P, HALF], F32)) for b in range(2)]
        ab = inner.enter_context(nc.psum_tensor("act_bank", [P, HALF], F32))
        yb = [inner.enter_context(nc.psum_tensor(f"y_bank{b}", [P, HALF], F32)) for b in range(4)]
        with nc.Block() as block:
            @block.sync
            def _(sp):
                def load(e):
                    w = e % N_WBUF
                    sp.dma_start(WG[:, w, :, :].rearrange("p k f -> p (k f)"), wgu_d[e, :, :]).then_inc(w_in[w], 16)
                    sp.dma_start(WD[:, w, :, :].rearrange("p k f -> p (k f)"), wd_d[e, :, :]).then_inc(w_in[w], 16)

                def signal(e):
                    sp.wait_ge(w_in[e % N_WBUF], 32 * (e // N_WBUF + 1))
                    sp.nop().then_inc(w_ready, 1)

                for e in range(N_WBUF):
                    load(e)
                signal(0)
                for e in range(N_WBUF, N_EXPERTS):
                    signal(e - N_WBUF + 1)
                    at = PLAN_ENDS + e - N_WBUF
                    sp.wait_ge(stored, sp.value_load(plan[0:1, at:at + 1], min_val=0, max_val=MAX_BLOCKS) + 1)
                    load(e)
                for e in range(N_EXPERTS - N_WBUF + 1, N_EXPERTS):
                    signal(e)

            @block.gpsimd
            def _(pool):
                def gather(s, b, uses):
                    wait(pool, xT_made, s - 1)
                    wait(pool, x_in[b], 16 * uses)
                    pool.tensor_copy(idx_x[:, b, :], idx[:, bass.ds(s, 1), :].rearrange("p o two -> p (o two)")).then_inc(idx_x_made, 1)
                    pool.wait_ge(idx_x_made, s + 1)
                    pool.tensor_tensor(turn[:], C("ones")[:, 0:1], C("ones")[:, 0:1], ALU.add)
                    pool.indirect_dma_start(xg[:, b, :], None, h1_dram,
                                            bass.IndirectOffsetOnAxis(ap=idx_x[:, b, 0:1], axis=0)).then_inc(x_in[b], 16)

                def scatter(s, b, uses):
                    wait(pool, y_out[b], 16 * uses)
                    pool.tensor_copy(idx_y[:, b, :], idx[:, bass.ds(s, 1), :].rearrange("p o two -> p (o two)")).then_inc(idx_y_made, 1)
                    pool.wait_ge(idx_y_made, s + 1)
                    pool.wait_ge(y_act, s + 1)
                    pool.wait_ge(y_dve, s + 1)
                    wait(pool, y_out[1 - b], 16 * (uses + b))
                    pool.tensor_tensor(turn[:], C("ones")[:, 0:1], C("ones")[:, 0:1], ALU.add).then_inc(stored, 1)
                    pool.indirect_dma_start(y_dram, bass.IndirectOffsetOnAxis(ap=idx_y[:, b, 1:2], axis=0),
                                            y[:, b, :], None).then_inc(y_out[b], 16)

                pool.memset(turn[:], 0).then_inc(stored, 1)
                n = trips(pool)
                pool.dma_start(idx[:], slot_dram.rearrange("(b p) two -> p b two", p=P)).then_inc(idx_in, 16)
                pool.wait_ge(idx_in, 16)
                gather(0, 0, 0)
                gather(1, 1, 0)
                gather(2, 0, 1)
                def trip(q):
                    gather(2 * q + 1, 1, q)
                    scatter(2 * q - 2, 0, q - 1)
                    gather(2 * q + 2, 0, q + 1)
                    scatter(2 * q - 1, 1, q - 1)

                trip(1)
                with pool.Fori(2, n) as q:
                    trip(q)
                scatter(2 * n - 2, 0, n - 1)
                scatter(2 * n - 1, 1, n - 1)
                for b in range(2):
                    pool.wait_ge(y_out[b], 16 * n)

            @block.tensor
            def _(pe):
                def weights_of(s):
                    e = pe.value_load(plan[0:1, bass.ds(s, 1)], min_val=0, max_val=N_EXPERTS - 1)
                    pe.wait_ge(w_ready, e + 1)
                    return pe.snap(e % N_WBUF, min_val=0, max_val=N_WBUF - 1)

                def gate_up(q, b):
                    s = 2 * q + b
                    w = weights_of(s)
                    pe.wait_ge(xT_act, s + 1)
                    pe.wait_ge(xT_dve, s + 1)
                    wait(pe, act_done, s)
                    for k in range(ND):
                        mm = pe.matmul(gub[:], xT[:, k, :], WG[:, bass.ds(w, 1), k, :].rearrange("p o f -> p (o f)"), start=k == 0, stop=k == ND - 1)
                    mm.then_inc(gu_made, 1)

                def turn_x(q, b):
                    s = 2 * q + b
                    pe.wait_ge(x_in[b], 16 * (q + 1))
                    wait(pe, xT_act, s)
                    wait(pe, xT_dve, s)
                    for k in range(ND):
                        mm = pe.transpose(xb[k // 4][:, (k % 4) * P:(k % 4 + 1) * P], xg[:, b, k * P:(k + 1) * P], C("ident"))
                    mm.then_inc(xT_made, 1)

                def down(q, b):
                    s = 2 * q + b
                    w = weights_of(s)
                    pe.wait_ge(aT_kept, s + 1)
                    wait(pe, y_act, s - 1)
                    wait(pe, y_dve, s - 1)
                    for half in range(2):
                        for k in range(2):
                            mm = pe.matmul(yb[2 * b + half][:], aT[:, k, :], WD[:, bass.ds(w, 1), k, half * HALF:(half + 1) * HALF].rearrange("p o f -> p (o f)"),
                                           start=k == 0, stop=k == 1)
                    mm.then_inc(d_made, 1)

                def turn_act(q, b):
                    s = 2 * q + b
                    pe.wait_ge(act_done, s + 1)
                    wait(pe, aT_kept, s)
                    for k in range(2):
                        mm = pe.transpose(ab[:, k * P:(k + 1) * P], ac[:, k * P:(k + 1) * P], C("ident"))
                    mm.then_inc(aT_made, 1)

                n = trips(pe)
                turn_x(0, 0)
                gate_up(0, 0)
                turn_x(0, 1)
                turn_act(0, 0)
                gate_up(0, 1)
                turn_x(1, 0)
                down(0, 0)
                turn_act(0, 1)
                def trip(q):
                    gate_up(q, 0)
                    turn_x(q, 1)
                    down(q - 1, 1)
                    turn_act(q, 0)
                    gate_up(q, 1)
                    turn_x(q + 1, 0)
                    down(q, 0)
                    turn_act(q, 1)

                trip(1)
                with pe.Fori(2, n) as q:
                    trip(q)
                down(n - 1, 1)

            @block.scalar
            def _(act):
                def keep_xT(s):
                    act.wait_ge(xT_made, s + 1)
                    wait(act, gu_made, s)
                    act.copy(xT[:, 0:4, :].rearrange("p k t -> p (k t)"), xb[0][:]).then_inc(xT_act, 1)

                def silu(s):
                    act.wait_ge(gu_made, s + 1)
                    wait(act, act_done, s)
                    act.activation(sg[:], gub[:, 0:FF], ACT.Silu).then_inc(silu_done, 1)

                def keep_y(q, b):
                    s = 2 * q + b
                    act.wait_ge(d_made, s + 1)
                    wait(act, y_out[b], 16 * q)
                    act.copy(y[:, b, 0:HALF], yb[2 * b][:]).then_inc(y_act, 1)

                n = trips(act)
                keep_xT(0)
                silu(0)
                keep_xT(1)
                silu(1)
                keep_xT(2)
                keep_y(0, 0)
                def trip(q):
                    silu(2 * q)
                    keep_xT(2 * q + 1)
                    keep_y(q - 1, 1)
                    silu(2 * q + 1)
                    keep_xT(2 * q + 2)
                    keep_y(q, 0)

                trip(1)
                with act.Fori(2, n) as q:
                    trip(q)
                keep_y(n - 1, 1)

            @block.vector
            def _(dve):
                def keep_xT(s):
                    dve.wait_ge(xT_made, s + 1)
                    wait(dve, gu_made, s)
                    dve.tensor_copy(xT[:, 4:8, :].rearrange("p k t -> p (k t)"), xb[1][:]).then_inc(xT_dve, 1)

                def act_mul(s):
                    dve.wait_ge(silu_done, s + 1)
                    wait(dve, aT_made, s)
                    dve.tensor_tensor(ac[:], sg[:], gub[:, FF:2 * FF], ALU.mult).then_inc(act_done, 1)

                def keep_aT(s):
                    dve.wait_ge(aT_made, s + 1)
                    wait(dve, d_made, s)
                    dve.tensor_copy(aT[:].rearrange("p k t -> p (k t)"), ab[:, 0:2 * P]).then_inc(aT_kept, 1)

                def keep_y(q, b):
                    s = 2 * q + b
                    dve.wait_ge(d_made, s + 1)
                    wait(dve, y_out[b], 16 * q)
                    dve.tensor_copy(y[:, b, HALF:], yb[2 * b + 1][:]).then_inc(y_dve, 1)

                n = trips(dve)
                keep_xT(0)
                act_mul(0)
                keep_xT(1)
                keep_aT(0)
                act_mul(1)
                keep_xT(2)
                keep_y(0, 0)
                keep_aT(1)
                def trip(q):
                    act_mul(2 * q)
                    keep_xT(2 * q + 1)
                    keep_y(q - 1, 1)
                    keep_aT(2 * q)
                    act_mul(2 * q + 1)
                    keep_xT(2 * q + 2)
                    keep_y(q, 0)
                    keep_aT(2 * q + 1)

                trip(1)
                with dve.Fori(2, n) as q:
                    trip(q)
                keep_y(n - 1, 1)


def combine(nc, ctx, y_dram, out, K, mem):
    sem = lambda n: ctx.enter_context(nc.semaphore(n))
    h1, rows, gates, slots = K["h1"], K["rows"], K["gates"], K["slots"]
    yg = mem.put("gathered", [P, 2, TOP_K, D])
    f = mem.put("sum", [P, 2, D])
    stats = mem.put("ln2_stats", [P, 12])
    mv = mem.put("ln2_mv", [P, NT, 2])
    std = mem.put("ln2_std", [P, NT, 2])
    y_in = [[sem(f"yg_in{b}{k}") for k in range(2)] for b in range(2)]
    f_out = [sem("f_out0"), sem("f_out1")]
    chain, stat_done, ln_std, xn, mul_done, f_done = (sem(f"ln2_{n}") for n in ("chain", "stat", "std", "xn", "mul", "done"))
    STEPS = 7
    with nc.Block() as block:
        @block.gpsimd
        def _(pool):
            for i in range(NT):
                pool.wait_ge(xn, i + 1)
                pool.tensor_tensor(f[:, i % 2, :], f[:, i % 2, :], rows[:, 2, :], ALU.mult).then_inc(mul_done, 1)

        @block.scalar
        def _(act):
            for i in range(NT):
                act.wait_ge(stat_done, i + 1)
                act.activation(std[:, i, 0:1], mv[:, i, 1:2], ACT.Sqrt, bias=LN_EPS).then_inc(ln_std, 1)

        @block.sync
        def _(sp):
            def load(i):
                if i >= 2:
                    sp.wait_ge(chain, STEPS * (i - 2) + 3)
                for k in range(TOP_K):
                    sp.dma_start(yg[:, i % 2, k, :], y_dram[k * T + i * P:k * T + (i + 1) * P, :]
                                 ).then_inc(y_in[i % 2][k], 16)

            load(0)
            load(1)
            for i in range(NT):
                if i + 2 < NT:
                    load(i + 2)
                sp.wait_ge(f_done, i + 1)
                sp.dma_start(out[i * P:(i + 1) * P, :], f[:, i % 2, :]).then_inc(f_out[i % 2], 16)
            for s in f_out:
                sp.wait_ge(s, 16 * NT // 2)

        @block.vector
        def _(dve):
            def add_rows(i):
                dve.wait_ge(mul_done, i + 1)
                dve.tensor_tensor(f[:, i % 2, :], f[:, i % 2, :], rows[:, 3, :], ALU.add).then_inc(f_done, 1)

            n = 0
            for i in range(NT):
                b = i % 2
                for k in range(TOP_K):
                    dve.wait_ge(y_in[b][k], 16 * (i // 2 + 1))
                if i >= 2:
                    dve.wait_ge(f_out[b], 16 * (i // 2))
                for step in range(STEPS):
                    if step == 0:
                        ins = dve.tensor_scalar(f[:, b, :], yg[:, b, 0, :], gates[:, 0, i:i + 1], None, ALU.mult)
                    elif step == 1:
                        ins = dve.scalar_tensor_tensor(f[:, b, :], yg[:, b, 1, :], gates[:, 1, i:i + 1], f[:, b, :],
                                                       ALU.mult, ALU.add)
                    elif step == 2:
                        ins = dve.scalar_tensor_tensor(f[:, b, :], h1[:, i, :], ALPHA, f[:, b, :], ALU.mult, ALU.add)
                    elif step in (3, 4):
                        k = step - 3
                        ins = dve.bn_stats(stats[:, 6 * k:6 * k + 6], f[:, b, k * HALF:(k + 1) * HALF])
                    elif step == 5:
                        dve.bn_aggr(mv[:, i, :], stats[:]).then_inc(stat_done, 1)
                        if i:
                            add_rows(i - 1)
                        dve.wait_ge(ln_std, i + 1)
                        ins = dve.reciprocal(std[:, i, 1:2], std[:, i, 0:1])
                    else:
                        ins = dve.nop()
                    ins.then_inc(chain, 1)
                    n += 1
                    if step != 3:
                        dve.wait_ge(chain, n)
                dve.tensor_scalar(f[:, b, :], f[:, b, :], mv[:, i, 0:1], std[:, i, 1:2],
                                  ALU.subtract, ALU.mult).then_inc(xn, 1)
            add_rows(NT - 1)


INPUTS = ["x", "consts", "params", "masks", "ln_rows", "w_cm", "w_v", "up", "gate_up"]


def hybrid_decoder(nc, d, out, dbg=None, stop=None):
    h_dram = nc.dram_tensor("h_scratch", [T, D], F32).ap()
    toep_dram = nc.dram_tensor("toeplitz_scratch", [6, P, N_TOEPLITZ], F32).ap()
    h1_dram = nc.dram_tensor("h1_scratch", [T, D], F32).ap()
    slot_dram = nc.dram_tensor("slot_scratch", [SLOT_BLOCKS * P, 2], I32).ap()
    y_dram = nc.dram_tensor("y_scratch", [TOP_K * T + 1, D], F32).ap()
    qk_dram = nc.dram_tensor("qk_scratch", [N_CM - N_B, P, T], F32).ap()
    with ExitStack() as ctx:
        keep = Memory(nc, 17408)
        const_sb = keep.put("const_sb", [P, N_CONST])
        par_sb = keep.put("par_sb", [P, N_PC])
        mask_sb = keep.put("mask_sb", [P, (N_LEVELS + 1) * P], I32)

        def C(name, k=0, n=None):
            if name in CONST:
                at, width = CONST[name]
                return const_sb[:, at:at + width]
            at = PC[name][0] + k
            return par_sb[:, at:at + (n or 1)]

        early = keep.at
        v_tok = keep.put("v_tok", [P, NT, HALF])
        spent = keep.at
        pm = keep.put("mixed_channels", [P, N_B, T])
        R = {"AR": keep.put("ar", [P, 2, NT, 2, P]), "bt": keep.put("bt", [P, 2, T])}
        wv_at = keep.at
        R["bh"], R["kh"] = keep.put("bh", [P, 2, T]), keep.put("kh", [P, 2, T])
        R["wv"] = nc.alloc_sbuf_tensor_at("wv_sb", [P, ND, HALF], F32, offset=wv_at)
        R["g"], R["bonus"] = keep.put("gate", [P, 2, T]), keep.put("bonus", [P, 2, T])
        R["PT"] = keep.put("chunk_decay", [P, 2, NCH])
        zone = keep.at
        hT = keep.put("hT", [P, ND, T])
        mixT = nc.alloc_sbuf_tensor_at("mixT", [P, ND, T], F32, offset=zone)
        work = keep.at
        for name, other, tile in (("bh_tok", "yc", 0), ("kh_tok", "y2", 5)):
            R[name] = nc.alloc_sbuf_tensor_at(name, [P, NT, 256], F32, offset=zone + tile * 4 * T)
            R[other] = nc.alloc_sbuf_tensor_at(other, [P, 4, HALF], F32, offset=zone + tile * 4 * T)
        R["RT"] = nc.alloc_sbuf_tensor_at("r_total", [P, 2, 2, P], F32, offset=zone + 2 * 4 * T)
        R["S"] = nc.alloc_sbuf_tensor_at("state", [P, 2, 2, P], F32, offset=zone + 2 * 4 * T + 4 * 512)
        w_out = nc.alloc_sbuf_tensor_at("w_out", [P, ND, D], F32, offset=work)
        w_out_in = ctx.enter_context(nc.semaphore("w_out_in"))
        late = Memory(nc, early, zone)
        K = {"h1": late.put("h1", [P, NT, D]), "rows": late.put("ln_rows", [P, 4, D]),
             "gates": late.put("gates", [P, 2, NT]), "slots": late.put("slots", [P, 2, NT], I32),
             "plan": late.put("plan", [1, PLAN], I32)}
        stages = {
            "normalise": lambda: normalise_input(
                nc, ctx, d["x"], h_dram, d["ln_rows"], C,
                (const_sb, d["consts"], par_sb, d["params"], mask_sb, d["masks"]), pm, hT, Memory(nc, work)),
            "project": lambda: project(nc, ctx, d["w_cm"], d["w_v"], d["up"], d["gate_up"], qk_dram, C, hT, pm, v_tok,
                                       R, Memory(nc, work)),
            "rwkv": lambda: rwkv(nc, ctx, C, mask_sb, pm, R, mixT, Memory(nc, work)),
            "attend": lambda: attend(nc, ctx, d["w_out"], w_out, w_out_in, qk_dram, toep_dram, d["rel_bias"], d["bucket_hot"], d["sinks"], C, mask_sb,
                                     v_tok, mixT, Memory(nc, spent, zone)),
            "route": lambda: mix_and_route(nc, ctx, h_dram, h1_dram, slot_dram, d["ln_rows"][2:6, :], d["router_w"],
                                           d["router_bias"], d["route"], C, mixT, w_out, w_out_in, K,
                                           Memory(nc, late.at, zone)),
            "experts": lambda: experts(nc, ctx, h1_dram, slot_dram, y_dram, d["w_gate_up"], d["w_down"], out, C, K,
                                       Memory(nc, late.at)),
            "combine": lambda: combine(nc, ctx, y_dram, out, K, Memory(nc, late.at)),
        }
        for name, stage in stages.items():
            stage()
            if stop == name:
                break
        if dbg is not None:
            dbg(nc, ctx, dict(hT=hT, pm=pm, ob=mixT[:, 3:5, :], v_tok=v_tok, mixT=mixT, par_sb=par_sb, h_dram=h_dram, qk_dram=qk_dram, h1_dram=h1_dram, **R, **K), out)


def lay_out(v):
    f = lambda a: np.ascontiguousarray(a, dtype=np.float32)
    v = {k: np.asarray(a) for k, a in v.items()}
    col = lambda a: a.reshape(-1, P).T
    w = v["w_in"][0]
    b0, c0 = A_COLS, A_COLS + B_COLS
    b_tiles = [w[:, b0 + 768:b0 + 896], w[:, b0 + 896:b0 + 1024]]
    mu = v["shift_mu"][0]
    mus = [mu[768:896], mu[896:1024]]
    for g in range(2):
        for kind in range(3):
            at = 256 * kind + P * g
            b_tiles.append(w[:, b0 + at:b0 + at + P])
            mus.append(mu[at:at + P])
    c_tiles = [w[:, c0 + P * t:c0 + P * (t + 1)] for t in range(6)]
    a_tiles = [np.concatenate([w[:, HD * j:HD * (j + 1)], w[:, HD * (j + 3):HD * (j + 4)]], axis=1) for j in range(3)]
    a_tiles.append(w[:, 384:512])
    tiles = np.stack(b_tiles + c_tiles + a_tiles)
    w_v = np.concatenate([w[:, c0 + 768:c0 + 1152], w[:, 512:640]], axis=1)
    o = v["w_out"][0]
    w_out = np.concatenate([o[HD * (j + 3 * e):HD * (j + 3 * e + 1)] for j in range(3) for e in range(2)] + [o[384:]])
    params = [col(v["ln0_g"]), col(v["ln0_b"]), np.stack(mus, axis=1)]
    params += [col(v[n][0].reshape(-1)) for n in ("decay_w0", "iclr_a0", "k_k", "k_a", "r_k", "lnx_g", "lnx_b")]
    params += [col(v["ln1_g"][0]), col(v["ln1_b"][0])]
    params = np.concatenate(params, axis=1)
    params = np.concatenate([params, np.zeros((P, N_PC - params.shape[1]), np.float32)], axis=1)
    return {
        "x": f(v["x"][0]),
        "consts": f(np.concatenate(list(constants().values()), axis=1)),
        "params": f(params),
        "masks": np.ascontiguousarray(level_masks()),
        "ln_rows": f(np.stack([v["ln0_g"], v["ln0_b"], v["ln1_g"][0], v["ln1_b"][0], v["ln2_g"][0], v["ln2_b"][0]])),
        "route": routing_constants(),
        "router_w": f(v["router_w"].reshape(ND, P, 16).transpose(1, 0, 2).reshape(P, ND * 16)),
        "router_bias": f(v["router_bias"][None, :]),
        "w_out": f(w_out.reshape(ND, P, D).transpose(1, 0, 2).reshape(P, ND * D)),
        "w_gate_up": f(np.concatenate([v["w_gate"][0], v["w_up"][0]], axis=2).reshape(N_EXPERTS, ND, P, 2 * FF)
                       .transpose(0, 2, 1, 3).reshape(N_EXPERTS, P, ND * 2 * FF)),
        "w_down": f(v["w_down"][0].reshape(N_EXPERTS, 2, P, D).transpose(0, 2, 1, 3).reshape(N_EXPERTS, P, 2 * D)),
        "w_cm": f(tiles.reshape(N_CM, ND, P, P).transpose(0, 2, 1, 3).reshape(N_CM, P, ND * P)),
        "w_v": f(w_v.reshape(ND, P, HALF).transpose(1, 0, 2)),
        "up": f(np.concatenate([v["decay_up"][0], v["iclr_up"][0]])),
        "gate_up": f(v["gate_up"][0]),
        "rel_bias": f(v["rel_bias"]),
        "bucket_hot": f(bias_constants()),
        "sinks": f(v["sinks"]),
    }


def kernel(**inputs):
    import concourse.bacc as bacc
    from concourse.bass_utils import run_bass_kernel_spmd

    nc = bacc.Bacc("TRN2", target_bir_lowering=False, num_devices=1)
    arrays = lay_out(inputs)
    d = {name: nc.dram_tensor(name, a.shape, mybir.dt.from_np(a.dtype), kind="ExternalInput").ap()
         for name, a in arrays.items()}
    out = nc.dram_tensor("result", (T, D), F32, kind="ExternalOutput").ap()
    hybrid_decoder(nc, d, out)
    done = run_bass_kernel_spmd(nc, [arrays], core_ids=[0])
    return done.results[0]["result"].reshape(1, T, D)
```

```python
from contextlib import ExitStack

import numpy as np

import concourse.bass as bass
from concourse import mybir

F32 = mybir.dt.float32
I32 = mybir.dt.int32
F32R = mybir.dt.float32r
U32 = mybir.dt.uint32
ALU = mybir.AluOpType
ACT = mybir.ActivationFunctionType
AX = mybir.AxisListType.X

P = 128
T = 1024
D = 1024
NT, ND = T // P, D // P
HALF = 512
HD = 64
CH = 64
NCH = T // CH
A_COLS, B_COLS, C_COLS = 640, 1024, 1152
LN_EPS, GN_EPS = 1e-5, 64e-5
DECAY_SCALE = float(np.exp(-0.5))
ALPHA = 2 ** 0.25

XWXA, XG, R0, K0, V0, R1, K1, V1 = range(8)
N_B = 8
N_CM = 18
K_TILES = (3, 4, 5, 9)
N_BUCKETS, MAX_EXACT, MAX_DISTANCE, WINDOW = 32, 16, 128, 128
N_TOEPLITZ = 384
NEG = -1e30
CLAMP = 30.0

PC = {}
for _name, _n in (("ln0_g", 8), ("ln0_b", 8), ("mu", 8), ("w0", 2), ("a0", 2), ("k_k", 2), ("k_a", 2),
                  ("r_k", 2), ("lnx_g", 2), ("lnx_b", 2), ("ln1_g", 8), ("ln1_b", 8)):
    PC[_name] = sum(n for _, n in PC.values()), _n
N_PC = 56


def constants():
    i, j = np.arange(P)[:, None], np.arange(P)[None, :]
    same = (i // CH) == (j // CH)
    c = {
        "ident": i == j,
        "head_ones": same,
        "head_mean": same / HD,
        "level0": (i // 2 == j // 2) & (i % 2 == 0) & (j % 2 == 1),
        "suffix": -1.0 * (i >= j),
        "all_later": -np.ones((P, P)),
        "key_before": i < j,
        "ones": np.ones((P, P)),
    }
    s = np.arange(P)[:, None]
    cols = np.arange(512)
    chunk, kind, t = (cols // 64) % 2, (cols // 128) % 2, cols % 64
    c["chunk_mask"] = (s // CH == chunk) & ((s % CH < t) | ((kind == 1) & (s % CH == t)))
    return c


def bias_constants():
    dist = 255 - np.arange(N_TOEPLITZ)
    inside = (dist >= 0) & (dist < WINDOW)
    d = np.maximum(dist, 1).astype(np.float32)
    large = MAX_EXACT + (np.log(d / MAX_EXACT) / np.float32(np.log(MAX_DISTANCE / MAX_EXACT))
                         * (N_BUCKETS - MAX_EXACT)).astype(np.int32)
    bucket = np.where(dist < MAX_EXACT, dist, np.minimum(large, N_BUCKETS - 1))
    hot = (np.arange(N_BUCKETS)[:, None] == bucket[None, :]) & inside[None, :]
    outside = np.broadcast_to(np.where(inside, 0.0, NEG), (N_BUCKETS, N_TOEPLITZ))
    return np.concatenate([hot, outside], axis=1)


CONST = {}
_at = 0
for _name, _m in constants().items():
    CONST[_name] = (_at, _m.shape[1])
    _at += _m.shape[1]
N_CONST = _at


def level_masks():
    i, j = np.arange(P)[:, None], np.arange(P)[None, :]
    out = []
    for m in (2, 4, 8, 16, 32):
        out.append((i // (2 * m) == j // (2 * m)) & ((i // m) % 2 == 0) & ((j // m) % 2 == 1))
    out.append(i >= j)
    return np.concatenate(out, axis=1).astype(np.int32)


N_LEVELS = 5


class Memory:

    def __init__(self, nc, start, end=229344):
        self.nc, self.at, self.end = nc, start, end

    def put(self, name, shape, dtype=F32):
        t = self.nc.alloc_sbuf_tensor_at(name, shape, dtype, offset=self.at)
        size = 4 * int(np.prod(shape[1:]))
        self.at += -(-size // 32) * 32
        assert self.at <= self.end, (name, self.at)
        return t


def bcast(ap, *dims):
    return bass.AP(ap.tensor, ap.offset, [list(ap.ap[0])] + [list(d) for d in dims])


def normalise_input(nc, ctx, x, ln_rows, w_cm, C, params, x_sb, hT, H, mem):
    sem = lambda n: ctx.enter_context(nc.semaphore(n))
    gb = H["gb"]
    stats = mem.put("ln0_stats", [P, NT, 12])
    mv = mem.put("ln0_mv", [P, NT, 2])
    std = mem.put("ln0_std", [P, NT])
    rstd = mem.put("ln0_rstd", [P, NT])
    x_in = [sem(f"x_in{i}") for i in range(NT)]
    const_in = sem("const_in")
    stat, aggr, std_done, rstd_done = sem("ln0_stat"), sem("ln0_aggr"), sem("ln0_std"), sem("ln0_rstd")
    xT_done, hT_done = sem("xT_done"), sem("hT_done")
    xn_done, rows_in, w_in = H["xn_done"], H["rows_in"], H["w_in"]
    const_sb, const_d, par_sb, par_d, mask_sb, mask_d = params
    with ExitStack() as inner:
        bank = [inner.enter_context(nc.psum_tensor(f"xT{d}", [P, HALF], F32)) for d in range(ND)]
        with nc.Block() as block:
            @block.sync
            def _(sp):
                for i in range(NT):
                    sp.dma_start(x_sb[:, i, :], x[i * P:(i + 1) * P, :]).then_inc(x_in[i], 16)
                for t in range(2):
                    sp.dma_start(H["w_ring"][:, t, :], w_cm[t]).then_inc(w_in[t], 16)

            @block.scalar
            def _(act):
                act.dma_start(const_sb[:], const_d).then_inc(const_in, 16)
                act.dma_start(par_sb[:], par_d).then_inc(const_in, 16)
                act.dma_start(mask_sb[:], mask_d).then_inc(const_in, 16)
                for k in range(2):
                    act.dma_start(gb[:, k, :], ln_rows[k:k + 1, :].to_broadcast([P, D])).then_inc(rows_in, 16)
                act.wait_ge(const_in, 48)
                for half in range(2):
                    i0 = 4 * half
                    act.wait_ge(aggr, i0 + 4)
                    act.activation(std[:, i0:i0 + 4], mv[:, i0:i0 + 4, 1], ACT.Sqrt, bias=LN_EPS).then_inc(std_done, 1)
                    for d in range(ND):
                        act.wait_ge(xT_done, half * ND + d + 1)
                        act.activation(hT[:, d, half * HALF:(half + 1) * HALF], bank[d][:], ACT.Identity,
                                       bias=C("ln0_b", d), scale=C("ln0_g", d)).then_inc(hT_done, 1)

            @block.vector
            def _(dve):
                for half in range(2):
                    for i in range(4 * half, 4 * half + 4):
                        dve.wait_ge(x_in[i], 16)
                        for k in range(2):
                            dve.bn_stats(stats[:, i, 6 * k:6 * k + 6],
                                         x_sb[:, i, k * HALF:(k + 1) * HALF]).then_inc(stat, 1)
                        dve.wait_ge(stat, 2 * i + 2)
                        dve.bn_aggr(mv[:, i, :], stats[:, i, :]).then_inc(aggr, 1)
                    dve.wait_ge(std_done, half + 1)
                    dve.reciprocal(rstd[:, 4 * half:4 * half + 4], std[:, 4 * half:4 * half + 4]).then_inc(rstd_done, 1)
                    dve.wait_ge(rstd_done, half + 1)
                    for i in range(4 * half, 4 * half + 4):
                        dve.tensor_scalar(x_sb[:, i, :], x_sb[:, i, :], mv[:, i, 0:1], rstd[:, i:i + 1],
                                          ALU.subtract, ALU.mult).then_inc(xn_done, 1)

            @block.tensor
            def _(pe):
                pe.wait_ge(const_in, 48)
                for half in range(2):
                    pe.wait_ge(xn_done, 4 * half + 4)
                    for d in range(ND):
                        if half:
                            pe.wait_ge(hT_done, d + 1)
                        for j in range(4):
                            mm = pe.transpose(bank[d][:, j * P:(j + 1) * P],
                                              x_sb[:, 4 * half + j, d * P:(d + 1) * P], C("ident"))
                        mm.then_inc(xT_done, 1)


PREP = ["scan", "kk", "kk2", "norm0", "norm1", "kfac", "knew", "rk", "recip", "kkn", "bonus0", "bonus1",
        "at", "rt", "ba", "bt", "kt", "pt", "bh", "kh"]


def prep_at(g, name):
    return 1 + g * len(PREP) + PREP.index(name) + 1


def project(nc, ctx, w_cm, w_v, up_d, gate_d, qk_dram, h_dram, C, hT, pm, v_tok, R, H, mem):
    sem = lambda n: ctx.enter_context(nc.semaphore(n))
    AR, bt, bh, kh, gT, PT, bonus = (R[n] for n in ("AR", "bt", "bh", "kh", "g", "PT", "bonus"))
    wv_sb = R["wv"]
    w_ring, hb, gb, x_sb = H["w_ring"], H["hb"], H["gb"], H["x_sb"]
    praw = mem.put("praw", [P, T + 8])
    diff = mem.put("diff", [P, T])
    stage = mem.put("qk_stage", [P, 2, T])
    up_sb = mem.put("up_sb", [P, 256])
    gate_sb = mem.put("gate_sb", [P, 256])
    aT = mem.put("iclr", [P, 2, T])
    lw = mem.put("log_decay", [P, 2, T])
    Pe = mem.put("decay", [P, NCH, CH + 1])
    kk = mem.put("kk", [P, T])
    tmp = mem.put("prep_tmp", [P, T])
    scan_mask = mem.put("scan_mask", [P, NCH, CH])
    one_minus_ka = mem.put("one_minus_ka", [P, 8])
    Pinv, rn = praw, diff
    w_in = H["w_in"]
    h_mul, h_done, h_out = sem("h_mul"), sem("h_done"), [sem("h_out0"), sem("h_out1")]
    wv_in, up_in = sem("wv_in"), sem("up_in")
    proj_done, proj_out = sem("proj_done"), sem("proj_out")
    v_done, v_out = sem("v_done"), sem("v_out")
    prepared, mix_diff, mixed = sem("prep_consts"), sem("mix_diff"), sem("mixed")
    stored = [sem("qk_stored0"), sem("qk_stored1")]
    squashed = sem("squashed")
    lora_done, lora_out = sem("lora_done"), sem("lora_out")
    prep, exp_done, sqrt_done = sem("prep"), sem("exp_done"), sem("sqrt_done")
    head_sum = sem("head_sum")
    per_chunk = lambda ap: ap.rearrange("p (c t) -> p c t", c=NCH)
    per_tile = lambda ap: ap.rearrange("p (i c t) -> p i c t", i=NT, c=2)
    by_tile = lambda ap: ap.rearrange("p i (c t) -> p i c t", c=2)
    split = lambda ap: ap.rearrange("p (i c) t -> p i c t", c=2)

    with ExitStack() as inner:
        pb = [inner.enter_context(nc.psum_tensor(f"proj{b}", [P, HALF], F32)) for b in range(6)]
        sb = [inner.enter_context(nc.psum_tensor(f"small{b}", [P, HALF], F32)) for b in range(2)]
        with nc.Block() as block:
            @block.sync
            def _(sp):
                sp.dma_start(up_sb[:], up_d).then_inc(up_in, 16)
                sp.dma_start(gate_sb[:], gate_d).then_inc(up_in, 16)

                def store(u):
                    sp.wait_ge(proj_out, 2 * (N_B + u + 1))
                    sp.dma_start(qk_dram[u], stage[:, u % 2, :]).then_inc(stored[u % 2], 16)

                def store_h(i):
                    sp.wait_ge(h_done, i + 1)
                    sp.dma_start(h_dram[i * P:(i + 1) * P, :], hb[:, i % 2, :]).then_inc(h_out[i % 2], 16)

                for i in range(4):
                    store_h(i)
                for t in range(2, N_CM):
                    sp.wait_ge(proj_done, 2 * (t - 1))
                    sp.dma_start(w_ring[:, t % 2, :], w_cm[t]).then_inc(w_in[t % 2], 16)
                    if t == 2:
                        for i in range(4, NT):
                            store_h(i)
                    if t == 3:
                        sp.dma_start(wv_sb[:], w_v).then_inc(wv_in, 16)
                    if t >= N_B + 2:
                        store(t - N_B - 2)
                store(N_CM - N_B - 2)
                store(N_CM - N_B - 1)
                for s in stored:
                    sp.wait_ge(s, 16 * (N_CM - N_B) // 2)

            @block.gpsimd
            def _(pool):
                pool.wait_ge(H["rows_in"], 32)
                for i in range(NT):
                    pool.wait_ge(H["xn_done"], i + 1)
                    if i >= 2:
                        pool.wait_ge(h_out[i % 2], 16 * (i // 2))
                    pool.tensor_tensor(hb[:, i % 2, :], x_sb[:, i, :], gb[:, 0, :], ALU.mult).then_inc(h_mul, 1)
                    pool.wait_ge(h_mul, i + 1)
                    pool.tensor_tensor(hb[:, i % 2, :], hb[:, i % 2, :], gb[:, 1, :], ALU.add).then_inc(h_done, 1)

            @block.tensor
            def _(pe):
                def tile(t):
                    pe.wait_ge(w_in[t % 2], 16 * (t // 2 + 1))
                    for half in range(2):
                        n = 2 * t + half
                        if n >= 6:
                            pe.wait_ge(proj_out, n - 5)
                        for d in range(ND):
                            mm = pe.matmul(pb[n % 6][:], w_ring[:, t % 2, d * P:(d + 1) * P],
                                           hT[:, d, half * HALF:(half + 1) * HALF], start=d == 0, stop=d == ND - 1)
                        mm.then_inc(proj_done, 1)

                def head_sums(g, what, first):
                    pe.wait_ge(prep, prep_at(g, what))
                    for half in range(2):
                        if what == "rk":
                            pe.wait_ge(prep, prep_at(g, f"norm{half}"))
                        elif g:
                            pe.wait_ge(prep, prep_at(g - 1, f"bonus{half}"))
                        else:
                            pe.wait_ge(lora_out, 12)
                        pe.matmul(sb[half][:], C("head_ones"), tmp[:, half * HALF:(half + 1) * HALF],
                                  start=True, stop=True).then_inc(head_sum, 1)

                for t in range(N_B):
                    tile(t)
                pe.wait_ge(up_in, 32)
                pe.wait_ge(squashed, 2)
                n = 0
                for g in range(2):
                    cols = slice(g * P, (g + 1) * P)
                    for half in range(2):
                        hs = slice(half * HALF, (half + 1) * HALF)
                        for lhsT, rhs in ((up_sb[0:64, cols], pm[0:64, XWXA, hs]),
                                          (up_sb[64:128, cols], pm[64:128, XWXA, hs]),
                                          (gate_sb[:, cols], pm[:, XG, hs])):
                            if n >= 2:
                                pe.wait_ge(lora_out, n - 1)
                            pe.matmul(sb[n % 2][:], lhsT, rhs, start=True, stop=True).then_inc(lora_done, 1)
                            n += 1
                pe.wait_ge(wv_in, 16)
                for i in range(NT):
                    if i < 2:
                        pe.wait_ge(proj_out, 2 * N_B)
                    else:
                        pe.wait_ge(v_out, i - 1)
                    for d in range(ND):
                        mm = pe.matmul(pb[4 + i % 2][:], hT[:, d, i * P:(i + 1) * P], wv_sb[:, d, :],
                                       start=d == 0, stop=d == ND - 1)
                    mm.then_inc(v_done, 1)
                pe.wait_ge(v_out, NT)
                for t in range(N_B, N_CM):
                    tile(t)
                    if t in (8, 12):
                        head_sums((t - 8) // 4, "kk2", 0)
                    if t in (10, 14):
                        head_sums((t - 10) // 4, "rk", 0)

            @block.scalar
            def _(act):
                def copy_out(t):
                    for half in range(2):
                        n = 2 * t + half
                        act.wait_ge(proj_done, n + 1)
                        if t < N_B:
                            dst = praw[:, 1 + half * HALF:1 + (half + 1) * HALF]
                            if t and half == 0:
                                act.wait_ge(mixed, t)
                        else:
                            u = t - N_B
                            dst = stage[:, u % 2, half * HALF:(half + 1) * HALF]
                            if u >= 2 and half == 0:
                                act.wait_ge(stored[u % 2], 16 * (u // 2))
                        if t < N_B or t - N_B in K_TILES:
                            act.copy(dst, pb[n % 6][:]).then_inc(proj_out, 1)
                        else:
                            act.mul(dst, pb[n % 6][:], HD ** -0.5).then_inc(proj_out, 1)

                def decay_factors(g):
                    act.wait_ge(prep, prep_at(g, "scan"))
                    if g:
                        act.wait_ge(prep, prep_at(g - 1, "kh"))
                    else:
                        act.wait_ge(mixed, N_B)
                    act.activation(Pe[:, :, 1:], per_chunk(lw[:, g, :]), ACT.Exp, scale=-DECAY_SCALE).then_inc(exp_done, 1)
                    act.activation(Pinv[:, 0:T], lw[:, g, :], ACT.Exp, scale=DECAY_SCALE).then_inc(exp_done, 1)

                def norm(g):
                    act.wait_ge(prep, prep_at(g, "norm1"))
                    act.activation(rn[:], rn[:], ACT.Sqrt).then_inc(sqrt_done, 1)

                for t in range(N_B):
                    copy_out(t)
                    if t == 2:
                        act.wait_ge(mixed, 2)
                        act.activation(pm[0:64, XWXA, :], pm[0:64, XWXA, :], ACT.Tanh).then_inc(squashed, 1)
                        act.activation(pm[:, XG, :], pm[:, XG, :], ACT.Sigmoid).then_inc(squashed, 1)
                n = 0
                for g in range(2):
                    for half in range(2):
                        hs = slice(half * HALF, (half + 1) * HALF)
                        for k in range(3):
                            act.wait_ge(lora_done, n + 1)
                            if k == 0:
                                act.activation(lw[:, g, hs], sb[n % 2][:], ACT.Sigmoid, bias=C("w0", g)).then_inc(lora_out, 1)
                            elif k == 1:
                                act.activation(aT[:, g, hs], sb[n % 2][:], ACT.Sigmoid, bias=C("a0", g)).then_inc(lora_out, 1)
                            else:
                                act.copy(gT[:, g, hs], sb[n % 2][:]).then_inc(lora_out, 1)
                            n += 1
                for i in range(NT):
                    act.wait_ge(v_done, i + 1)
                    act.copy(v_tok[:, i, :], pb[4 + i % 2][:]).then_inc(v_out, 1)
                decay_factors(0)
                for t in range(N_B, N_CM):
                    copy_out(t)
                    if t in (8, 12):
                        norm((t - 8) // 4)
                    if t == 11:
                        decay_factors(1)

            @block.vector
            def _(dve):
                dve.memset(praw[:, 0:1], 0.0).then_inc(prepared, 1)
                dve.memset(scan_mask[:], 1.0).then_inc(prepared, 1)
                dve.memset(Pe[:, :, 0:1], 1.0).then_inc(prepared, 1)
                dve.wait_ge(prepared, 2)
                dve.memset(scan_mask[:, :, 0:1], 0.0).then_inc(prepared, 1)
                dve.tensor_scalar(one_minus_ka[:, 0:2], C("k_a", 0, 2), -1.0, 1.0, ALU.mult, ALU.add).then_inc(prepared, 1)
                dve.wait_ge(prepared, 5)
                for t in range(N_B):
                    dve.wait_ge(proj_out, 2 * t + 2)
                    dve.tensor_tensor(diff[:], praw[:, 0:T], praw[:, 1:T + 1], ALU.subtract).then_inc(mix_diff, 1)
                    dve.wait_ge(mix_diff, t + 1)
                    dve.wait_ge(h_mul, t + 1)
                    dve.scalar_tensor_tensor(pm[:, t, :], diff[:], C("mu", t), praw[:, 1:T + 1],
                                             ALU.mult, ALU.add).then_inc(mixed, 1)
                dve.wait_ge(mixed, N_B)
                dve.nop().then_inc(prep, 1)
                for g in range(2):
                    r, k, v = (pm[:, (R0, K0, V0)[j] if g == 0 else (R1, K1, V1)[j], :] for j in range(3))
                    after = lambda name: dve.wait_ge(prep, prep_at(g, name))
                    at_PT = bass.AP(PT, 0, [list(PT[:].ap[0]), [1, NCH], [0, CH]]) if g == 0 else \
                        bass.AP(PT, NCH, [list(PT[:].ap[0]), [1, NCH], [0, CH]])
                    dve.wait_ge(lora_out, 6 * (g + 1))
                    dve.tensor_tensor_scan(lw[:, g, :], scan_mask[:].rearrange("p c t -> p (c t)"), lw[:, g, :],
                                           0.0, ALU.mult, ALU.add).then_inc(prep, 1)
                    dve.tensor_scalar(kk[:], k, C("k_k", g), None, ALU.mult).then_inc(prep, 1)
                    after("kk")
                    dve.tensor_tensor(tmp[:], kk[:], kk[:], ALU.mult).then_inc(prep, 1)
                    for half in range(2):
                        dve.wait_ge(head_sum, 4 * g + half + 1)
                        dve.tensor_scalar(rn[:, half * HALF:(half + 1) * HALF], sb[half][:], 1e-24, None,
                                          ALU.max).then_inc(prep, 1)
                    dve.tensor_scalar(tmp[:], aT[:, g, :], C("k_a", g), one_minus_ka[:, g:g + 1],
                                      ALU.mult, ALU.add).then_inc(prep, 1)
                    after("kfac")
                    dve.tensor_tensor(k, k, tmp[:], ALU.mult).then_inc(prep, 1)
                    after("knew")
                    dve.scalar_tensor_tensor(tmp[:], r, C("r_k", g), k, ALU.mult, ALU.mult).then_inc(prep, 1)
                    dve.wait_ge(sqrt_done, g + 1)
                    dve.reciprocal(rn[:], rn[:]).then_inc(prep, 1)
                    after("recip")
                    dve.scalar_tensor_tensor(kk[:], kk[:], -1.0, rn[:], ALU.mult, ALU.mult).then_inc(prep, 1)
                    for half in range(2):
                        hs = slice(half * HALF, (half + 1) * HALF)
                        dve.wait_ge(head_sum, 4 * g + 2 + half + 1)
                        dve.tensor_tensor(bonus[:, g, hs], sb[half][:], v[:, hs], ALU.mult).then_inc(prep, 1)
                    dve.wait_ge(exp_done, 2 * g + 2)
                    after("kkn")
                    if g == 0:
                        for s in h_out:
                            dve.wait_ge(s, 16 * NT // 2)
                    dve.tensor_tensor(by_tile(AR[:, g, :, 0, :]), per_tile(kk[:]), split(Pe[:, :, 0:CH]), ALU.mult).then_inc(prep, 1)
                    dve.tensor_tensor(by_tile(AR[:, g, :, 1, :]), per_tile(r), split(Pe[:, :, 1:]), ALU.mult).then_inc(prep, 1)
                    dve.scalar_tensor_tensor(tmp[:], kk[:], -1.0, aT[:, g, :], ALU.mult, ALU.mult).then_inc(prep, 1)
                    after("ba")
                    dve.tensor_tensor(bt[:, g, :], tmp[:], Pinv[:, 0:T], ALU.mult).then_inc(prep, 1)
                    dve.tensor_tensor(k, k, Pinv[:, 0:T], ALU.mult).then_inc(prep, 1)
                    dve.tensor_copy(PT[:, g, :], Pe[:, :, CH]).then_inc(prep, 1)
                    dve.wait_ge(v_done, NT)
                    after("pt")
                    dve.tensor_tensor(per_chunk(bh[:, g, :]), per_chunk(bt[:, g, :]), at_PT, ALU.mult).then_inc(prep, 1)
                    dve.tensor_tensor(per_chunk(kh[:, g, :]), per_chunk(k), at_PT, ALU.mult).then_inc(prep, 1)


TURNS = [x for level in range(1, N_LEVELS + 1) for x in (f"T{level}", f"Y{level}", f"X{level}")][:-1]
MADE = ["turn", "A0", "A1", "A2", "A3", "AV", "X0", *TURNS, "GU", "RT", "MT"]
KEPT_ACT = ["a_tok", "bh_tok", "X0", *[x for x in TURNS if x[0] != "Y"], "GU"]
KEPT_DVE = ["kh_tok", "v_tok", "A0", "A1", "A2", "A3", "level0", "XT0", "AV",
            *[x for x in TURNS if x[0] == "Y"], "RT", "MT0", "MT1", "MT2", "MT3"]


def upto(steps, n, name):
    return n * len(steps) + steps.index(name) + 1


def rwkv(nc, ctx, qk_dram, qk, qk_in, C, masks, pm, R, mixT, mem):
    sem = lambda n: ctx.enter_context(nc.semaphore(n))
    AR, bt, bh, kh, gT, PT, bonus = (R[n] for n in ("AR", "bt", "bh", "kh", "g", "PT", "bonus"))
    XR = mem.put("x_rhs", [P, NT, 4, 2, HD])
    bh_tok = R["bh_tok"]
    kh_tok = R["kh_tok"]
    v_tok = mem.put("vb_tok", [P, NT, 256])
    Am = mem.put("chunk_products", [P, 2, 4, 512])
    XT = mem.put("inverse_T", [P, 2, 4, P])
    X = mem.put("inverse", [P, 2, 4, P])
    Tm = mem.put("inverse_step", [P, 2, 4, P])
    GU = mem.put("gu", [P, 2, 2, 4, HD])
    RT, S = R["RT"], R["S"]
    MT = mem.put("state_map", [P, 2, 4, P])
    made = [sem("made0"), sem("made1")]
    kept_act = [sem("kept_act0"), sem("kept_act1")]
    kept_dve = [sem("kept_dve0"), sem("kept_dve1")]
    z_done, s_done, y_done, y_out = sem("z_done"), sem("s_done"), sem("y_done"), sem("y_out")

    def cols4(ap):
        return ap.rearrange("p (h t) -> p h t", h=4)

    def part(st, hh, kind, ar):
        at = kind * 256 + ar * P
        return Am[:, st, hh, at:at + P]

    with ExitStack() as inner:
        bank = [inner.enter_context(nc.psum_tensor(f"rw{b}", [P, HALF], F32)) for b in range(8)]
        ybank, zbank = bank[6], bank[7]
        with nc.Block() as block:
            @block.sync
            def _(sp):
                for k in range(2):
                    sp.dma_start(qk[:, 0, k, :], qk_dram[3 * k]).then_inc(qk_in[0], 16)

            @block.tensor
            def _(pe):
                def step(name, st, i):
                    n = i // 2
                    B = bank[3 * st:3 * st + 3]
                    act_has = lambda x: pe.wait_ge(kept_act[st], upto(KEPT_ACT, n, x))
                    dve_has = lambda x: pe.wait_ge(kept_dve[st], upto(KEPT_DVE, n, x))
                    ts = slice(i * P, (i + 1) * P)
                    if name == "turn":
                        if n:
                            pe.wait_ge(kept_dve[st], n * len(KEPT_DVE))
                        for g in range(2):
                            pe.transpose(B[0][:, g * P:(g + 1) * P], AR[:, g, i, 0, :], C("ident"))
                            pe.transpose(B[0][:, (2 + g) * P:(3 + g) * P], bh[:, g, ts], C("ident"))
                            pe.transpose(B[1][:, g * P:(g + 1) * P], kh[:, g, ts], C("ident"))
                            mm = pe.transpose(B[1][:, (2 + g) * P:(3 + g) * P], pm[:, (V0, V1)[g], ts], C("ident"))
                    elif name[0] == "A" and name != "AV":
                        hh = int(name[1])
                        g, e = hh // 2, hh % 2
                        if hh == 0:
                            act_has("bh_tok")
                        elif hh == 1:
                            dve_has("v_tok")
                        elif hh == 3:
                            dve_has("A0")
                        ar = AR[e * HD:(e + 1) * HD, g, i, :, :].rearrange("p a t -> p (a t)")
                        dst = B[hh % 3]
                        pe.matmul(dst[:, 0:256], pm[e * HD:(e + 1) * HD, (K0, K1)[g], ts], ar, start=True, stop=True)
                        mm = pe.matmul(dst[:, 256:512], bt[e * HD:(e + 1) * HD, g, ts], ar, start=True, stop=True)
                    elif name == "AV":
                        dve_has("A3")
                        for hh in range(4):
                            mm = pe.matmul(B[1][:, hh * HD:(hh + 1) * HD], part(st, hh, 0, 0),
                                           v_tok[:, i, hh * HD:(hh + 1) * HD], start=True, stop=True)
                    elif name[0] == "X":
                        dve_has("XT0" if name == "X0" else f"Y{name[1]}")
                        for hh in range(4):
                            mm = pe.transpose(B[0][:, hh * P:(hh + 1) * P], XT[:, st, hh, :], C("ident"))
                    elif name[0] == "T":
                        act_has(f"X{int(name[1]) - 1}")
                        if name == "T1":
                            dve_has("AV")
                        for hh in range(4):
                            mm = pe.matmul(B[1][:, hh * P:(hh + 1) * P], part(st, hh, 1, 0), X[:, st, hh, :],
                                           start=True, stop=True)
                    elif name[0] == "Y":
                        act_has(f"T{name[1]}")
                        for hh in range(4):
                            mm = pe.matmul(B[2][:, hh * P:(hh + 1) * P], Tm[:, st, hh, :], XT[:, st, hh, :],
                                           start=True, stop=True)
                    elif name == "GU":
                        dve_has("Y5")
                        for hh in range(4):
                            mm = pe.matmul(B[1][:, hh * P:(hh + 1) * P], XT[:, st, hh, :], XR[:, i, hh, :, :],
                                           start=True, stop=True)
                    elif name == "RT":
                        act_has("GU")
                        for hh in range(4):
                            g, e = hh // 2, hh % 2
                            mm = pe.matmul(B[2][e * HD:(e + 1) * HD, g * P:(g + 1) * P], GU[:, st, 0, hh, :],
                                           part(st, hh, 1, 1), start=True, stop=True)
                    elif name == "MT":
                        for cc in range(2):
                            rows = slice(cc * CH, (cc + 1) * CH)
                            for g in range(2):
                                mm = pe.matmul(B[cc][:, g * P:(g + 1) * P], GU[rows, st, 0, 2 * g:2 * g + 2, :].rearrange("p h d -> p (h d)"),
                                               bh_tok[rows, i, g * P:(g + 1) * P], start=True, stop=True)
                    mm.then_inc(made[st], 1)

                def outputs_and_state(st, i):
                    n = i // 2
                    if i:
                        pe.wait_ge(y_out, i)
                    pe.wait_ge(kept_dve[st], upto(KEPT_DVE, n, "RT"))
                    for g in range(2):
                        for e in range(2):
                            hh = 2 * g + e
                            dst = ybank[e * HD:(e + 1) * HD, g * P:(g + 1) * P]
                            pe.matmul(dst, GU[:, st, 1, hh, :], part(st, hh, 1, 1), start=g == 0, stop=False,
                                      skip_group_check=True)
                            mm = pe.matmul(dst, v_tok[:, i, hh * HD:(hh + 1) * HD], part(st, hh, 0, 1),
                                           start=False, stop=i == 0, skip_group_check=True)
                    pe.wait_ge(kept_dve[st], upto(KEPT_DVE, n, "MT3"))
                    for cc in range(2):
                        c = 2 * i + cc
                        rows = slice(cc * CH, (cc + 1) * CH)
                        if c:
                            pe.wait_ge(s_done, c)
                            for g in range(2):
                                mm = pe.matmul(ybank[:, g * P + cc * CH:g * P + (cc + 1) * CH], S[:, c % 2, g, :],
                                               RT[:, st, g, cc * CH:(cc + 1) * CH], start=False, stop=True,
                                               skip_group_check=True)
                        if cc == 1:
                            mm.then_inc(y_done, 1)
                        if c == NCH - 1:
                            break
                        for g in range(2):
                            dst = zbank[:, g * P:(g + 1) * P]
                            pe.matmul(dst, bh_tok[rows, i, g * P:(g + 1) * P], GU[rows, st, 1, 2 * g:2 * g + 2, :].rearrange("p h d -> p (h d)"),
                                      start=g == 0, stop=False, skip_group_check=True)
                            mm = pe.matmul(dst, kh_tok[rows, i, g * P:(g + 1) * P], v_tok[rows, i, g * P:(g + 1) * P],
                                           start=False, stop=c == 0, skip_group_check=True)
                            if c:
                                mm = pe.matmul(dst, MT[:, st, 2 * cc + g, :], S[:, c % 2, g, :],
                                               start=False, stop=True, skip_group_check=True)
                        mm.then_inc(z_done, 1)

                for i in range(0, NT, 2):
                    for name in MADE:
                        for st in range(2):
                            step(name, st, i + st)
                    for st in range(2):
                        outputs_and_state(st, i + st)

            @block.scalar
            def _(act):
                def step(name, st, i):
                    n = i // 2
                    B = bank[3 * st:3 * st + 3]
                    done = kept_act[st]
                    act.wait_ge(made[st], upto(MADE, n, "turn" if name in ("a_tok", "bh_tok") else name))
                    if name == "a_tok":
                        act.copy(XR[:, i, :, 0, :], B[0][:, 0:256].rearrange("p (h d) -> p h d", h=4)).then_inc(done, 1)
                    elif name == "bh_tok":
                        act.copy(bh_tok[:, i, :], B[0][:, 256:512]).then_inc(done, 1)
                    elif name[0] == "X":
                        act.copy(X[:, st, :, :], cols4(B[0][:])).then_inc(done, 1)
                    elif name[0] == "T":
                        act.copy(Tm[:, st, :, :], cols4(B[1][:])).then_inc(done, 1)
                    else:
                        act.copy(GU[:, st, :, :, :].rearrange("p a h d -> p h a d"),
                                 B[1][:].rearrange("p (h a d) -> p h a d", h=4, a=2)).then_inc(done, 1)

                for i in range(0, NT, 2):
                    for name in KEPT_ACT:
                        for st in range(2):
                            step(name, st, i + st)
                    for st in range(2):
                        act.wait_ge(y_done, i + st + 1)
                        cols = slice((i + st) * P, (i + st + 1) * P)
                        for g in range(2):
                            ins = act.copy(mixT[:, 3 + g, cols], ybank[:, g * P:(g + 1) * P])
                        ins.then_inc(y_out, 1)

            @block.vector
            def _(dve):
                def step(name, st, i):
                    n = i // 2
                    B = bank[3 * st:3 * st + 3]
                    done = kept_dve[st]
                    was_made = lambda x: dve.wait_ge(made[st], upto(MADE, n, x))
                    own = lambda x: dve.wait_ge(done, upto(KEPT_DVE, n, x))
                    if name == "kh_tok":
                        was_made("turn")
                        dve.tensor_copy(kh_tok[:, i, :], B[1][:, 0:256]).then_inc(done, 1)
                    elif name == "v_tok":
                        dve.tensor_copy(v_tok[:, i, :], B[1][:, 256:512]).then_inc(done, 1)
                    elif name == "AV":
                        was_made("AV")
                        dve.tensor_copy(XR[:, i, :, 1, :],
                                        B[1][:, 0:256].rearrange("p (h d) -> p h d", h=4)).then_inc(done, 1)
                    elif name[0] == "A":
                        was_made(name)
                        if name == "A0" and i >= 2:
                            dve.wait_ge(y_done, i - 1)
                        dve.tensor_tensor(Am[:, st, int(name[1]), :], B[int(name[1]) % 3][:], C("chunk_mask"),
                                          ALU.mult).then_inc(done, 1)
                    elif name == "level0":
                        own("A3")
                        dve.tensor_tensor(XT[:, st, :, :], Am[:, st, :, 256:256 + P],
                                          bcast(C("level0"), [0, 4], [1, P]), ALU.mult).then_inc(done, 1)
                    elif name == "XT0":
                        own("level0")
                        dve.tensor_tensor(XT[:, st, :, :], XT[:, st, :, :], bcast(C("ident"), [0, 4], [1, P]),
                                          ALU.add).then_inc(done, 1)
                    elif name[0] == "Y":
                        was_made(name)
                        level = int(name[1]) - 1
                        dve.copy_predicated(XT[:, st, :, :], bcast(masks[:, level * P:(level + 1) * P], [0, 4], [1, P]),
                                            cols4(B[2][:])).then_inc(done, 1)
                    elif name == "RT":
                        was_made("RT")
                        dve.tensor_tensor(RT[:, st, :, :], B[2][:, 0:256].rearrange("p (g t) -> p g t", g=2),
                                          AR[:, :, i, 1, :], ALU.add).then_inc(done, 1)
                    else:
                        was_made("MT")
                        q = int(name[2])
                        cc, g = q // 2, q % 2
                        dve.scalar_tensor_tensor(MT[:, st, q, :], C("ident"), PT[:, g, 2 * i + cc:2 * i + cc + 1],
                                                 B[cc][:, g * P:(g + 1) * P], ALU.mult, ALU.add).then_inc(done, 1)

                for i in range(0, NT, 2):
                    for name in KEPT_DVE:
                        for st in range(2):
                            step(name, st, i + st)
                    for c in range(2 * i, min(2 * i + 4, NCH - 1)):
                        dve.wait_ge(z_done, c + 1)
                        dve.tensor_tensor(S[:, (c + 1) % 2, :, :], zbank[:, 0:256].rearrange("p (g v) -> p g v", g=2),
                                          bcast(C("head_ones"), [0, 2], [1, P]), ALU.mult).then_inc(s_done, 1)


UNITS = [(h, qg, kb) for h in range(6) for qg in range(2) for kb in range(4 * qg + 3, -1, -1)]


GN_FIRST, GN_EVERY, GN_LAGS = 6, 12, 8


def attend(nc, ctx, w_out_d, w_out, w_out_in, qk_dram, toep_dram, rel_d, hot_d, sinks_d, C, masks, v_tok, mixT, R, qk, qk_in, mem, upper):
    sem = lambda n: ctx.enter_context(nc.semaphore(n))
    start = mem.at
    mem.at += 4 * 4 * T
    ring = 4
    ex = upper.put("exp_z", [P, ring, HALF])
    sp = mem.put("softplus", [P, ring, HALF])
    w = mem.put("weights", [P, ring, HALF])
    acc = mem.put("later_softplus", [P, 3, HALF])
    late_end = mem.at
    zeros = mem.put("zeros", [P, P])
    qa = mem.put("window_qk", [P, 4, T])
    rel = mem.put("rel_bias", [32, 8])
    hot = mem.put("bucket_one_hot", [32, 2, N_TOEPLITZ])
    toep = mem.put("toeplitz_rows", [8, N_TOEPLITZ])
    bias = mem.put("bias", [P, 6, 256])
    sink = mem.put("sink", [P, 8])
    late = Memory(nc, start, late_end)
    L = late.put("logits", [P, 2, 6, 256])
    Pr = late.put("probs", [P, 2, 6, 256])
    PrT = late.put("probs_T", [P, 2, 12, P])
    st = late.put("softmax_stats", [P, 2, 6, 8])
    yc, y2 = mem.put("y_centred", [P, HALF]), mem.put("y_squared", [P, HALF])
    mean_done, centred, squared, var_done, log_var, gn_rstd, gn_scaled, gn_gain, gn_bonus, gn_done = (
        sem(f"gn_{n}") for n in ("mean", "centred", "squared", "var", "log_var", "rstd", "scaled", "gain", "bonus", "done"))
    qa_in, rel_in = sem("qa_in"), sem("rel_in")
    z_done, e_done, l_done = (sem(f"sb_{n}") for n in ("z", "exp", "log"))
    sp_step = sem("sb_softplus")
    RAW, MASKED = -1, 0
    sp_at = lambda u, step: 2 * (u + 1) + step
    acc_done, s_done, w_raw, w_done, av_done, o_out = (sem(f"sb_{n}") for n in ("acc", "s", "w_raw", "w", "av", "o"))
    zero_done, toep_made, toep_kept, toep_out, bias_in = (sem(n) for n in ("zero_done", "toep_made", "toep_kept", "toep_out", "bias_in"))
    l_made, l_kept, stat, stat2, p_done, p_norm, pT_made, pT_kept, o_made, o_kept = (
        sem(f"win_{n}") for n in ("l_made", "l_kept", "stat", "stat2", "p", "p_norm", "pT_made", "pT_kept", "o_made", "o_kept"))

    groups = [(h, qg) for h in range(6) for qg in range(2)]
    diag = [kb >= 4 * qg for _, qg, kb in UNITS]
    first = [kb == 4 * qg + 3 for _, qg, kb in UNITS]
    last = [kb == 0 for _, _, kb in UNITS]
    place = [4 * qg + 3 - kb for _, qg, kb in UNITS]
    c0 = [max(0, (kb - 4 * qg) * P) for _, qg, kb in UNITS]
    N = len(UNITS)
    diags = [sum(diag[:u + 1]) for u in range(N)]
    adds = [sum(not x for x in last[:u + 1]) for u in range(N)]
    group_of = [groups.index((h, qg)) for h, qg, _ in UNITS]

    norm_at = {GN_FIRST + GN_EVERY * v + lag: (lag, v) for v in range(4) for lag in range(GN_LAGS)}

    def norm_part(v):
        g, half = v // 2, v % 2
        hs = slice(half * HALF, (half + 1) * HALF)
        return g, hs, mixT[:, 3 + g, hs]

    NZ = 5
    with ExitStack() as inner:
        gb = inner.enter_context(nc.psum_tensor("norm_bank", [P, HALF], F32))
        zb = [inner.enter_context(nc.psum_tensor(f"z{b}", [P, HALF], F32)) for b in range(NZ)]
        ob = [inner.enter_context(nc.psum_tensor(f"o{b}", [P, HALF], F32)) for b in range(2)]
        tb = zb[NZ - 1]
        with nc.Block() as block:
            @block.sync
            def _(sp_):
                sp_.dma_start(rel[:, 0:6], rel_d).then_inc(rel_in, 16)
                sp_.dma_start(hot[:].rearrange("p a m -> p (a m)"), hot_d).then_inc(rel_in, 16)
                sp_.dma_start(sink[:, 0:6], sinks_d.to_broadcast([P, 6])).then_inc(rel_in, 16)
                for t in range(3):
                    if t == 2:
                        sp_.wait_ge(av_done, 24)
                    if t:
                        sp_.dma_start(qk[:, t % 2, 0, :], qk_dram[t]).then_inc(qk_in[t % 2], 16)
                        sp_.dma_start(qk[:, t % 2, 1, :], qk_dram[3 + t]).then_inc(qk_in[t % 2], 16)
                    if t == 1:
                        for k in range(4):
                            sp_.dma_start(qa[:, k, :], qk_dram[6 + k]).then_inc(qa_in, 16)
                        sp_.wait_ge(toep_kept, 1)
                        sp_.dma_start(toep_dram, toep[0:6, :].unsqueeze(1).to_broadcast([6, P, N_TOEPLITZ])).then_inc(toep_out, 16)
                        sp_.wait_ge(toep_out, 16)
                        sp_.dma_start(bias[:], bass.AP(toep_dram.tensor, 127, [[N_TOEPLITZ - 1, P], [P * N_TOEPLITZ, 6], [1, 256]])
                                      ).then_inc(bias_in, 16)
                        sp_.dma_start(w_out[:].rearrange("p k d -> p (k d)"), w_out_d).then_inc(w_out_in, 16)

            @block.tensor
            def _(pe):
                def scores(u):
                    h, qg, kb = UNITS[u]
                    rows, t = slice((h % 2) * HD, (h % 2 + 1) * HD), h // 2
                    pe.wait_ge(qk_in[t % 2], 32 * (t // 2 + 1))
                    if u >= NZ:
                        pe.wait_ge(w_raw, u - NZ + 1)
                    elif u == NZ - 1:
                        pe.wait_ge(toep_kept, 1)
                    pe.matmul(zb[u % NZ][:, c0[u]:], qk[rows, t % 2, 1, kb * P:(kb + 1) * P],
                              qk[rows, t % 2, 0, qg * HALF + c0[u]:(qg + 1) * HALF],
                              start=True, stop=True).then_inc(z_done, 1)

                def suffix(u):
                    pe.wait_ge(sp_step, sp_at(u, MASKED))
                    mm = pe.matmul(zb[u % NZ][:, c0[u]:], C("suffix"), sp[:, u % ring, c0[u]:], start=False, stop=True,
                                   skip_group_check=True)
                    if not first[u]:
                        pe.wait_ge(acc_done, 2 * adds[u - 1])
                        from_ = c0[u] + P if diag[u] else 0
                        mm = pe.matmul(zb[u % NZ][:, from_:], C("all_later"), acc[:, adds[u - 1] % 3, from_:],
                                       start=False, stop=True, skip_group_check=True)
                    mm.then_inc(s_done, 1)

                def values(u):
                    h, qg, kb = UNITS[u]
                    g = group_of[u]
                    pe.wait_ge(w_done, u + 1)
                    if first[u] and g >= 2:
                        pe.wait_ge(o_out, g - 1)
                    rows = slice((h % 2) * HD, (h % 2 + 1) * HD)
                    pe.matmul(ob[g % 2][rows, c0[u]:], v_tok[:, kb, h * HD:(h + 1) * HD], w[:, u % ring, c0[u]:],
                              start=first[u], stop=last[u], skip_group_check=True).then_inc(av_done, 1)

                def norm(lag, v):
                    if lag == 0:
                        pe.matmul(gb[:], C("head_mean"), norm_part(v)[2], start=True, stop=True).then_inc(mean_done, 1)
                    elif lag == 2:
                        pe.wait_ge(squared, v + 1)
                        pe.wait_ge(centred, v + 1)
                        pe.matmul(gb[:], C("head_mean"), y2[:], start=True, stop=True).then_inc(var_done, 1)

                scores(0)
                scores(1)
                pe.wait_ge(rel_in, 48)
                pe.matmul(tb[0:6, 0:N_TOEPLITZ], rel[:, 0:6], hot[:, 0, :], start=True, stop=True).then_inc(toep_made, 1)
                for u in range(N + 2):
                    if u in norm_at:
                        norm(*norm_at[u])
                    if u + 2 < N:
                        scores(u + 2)
                    if u and u - 1 < N:
                        suffix(u - 1)
                    if u >= 2:
                        values(u - 2)

            @block.scalar
            def _(act):
                def weights(u):
                    act.wait_ge(s_done, u + 1)
                    if u >= ring:
                        act.wait_ge(av_done, u - ring + 1)
                    act.activation(w[:, u % ring, c0[u]:], zb[u % NZ][:, c0[u]:], ACT.Exp).then_inc(w_raw, 1)

                def norm(lag, v):
                    if lag == 1:
                        act.wait_ge(centred, v + 1)
                        act.activation(y2[:], yc[:], ACT.Square).then_inc(squared, 1)
                    elif lag == 3:
                        act.wait_ge(var_done, v + 1)
                        act.activation(y2[:], gb[:], ACT.Ln, bias=GN_EPS).then_inc(log_var, 1)
                        act.wait_ge(log_var, v + 1)
                        act.activation(y2[:], y2[:], ACT.Exp, scale=-0.5).then_inc(gn_rstd, 1)
                    elif lag == 5:
                        act.wait_ge(gn_scaled, v + 1)
                        g = norm_part(v)[0]
                        act.activation(yc[:], yc[:], ACT.Identity, bias=C("lnx_b", g), scale=C("lnx_g", g)).then_inc(gn_gain, 1)

                act.preload_act_table_set("natural_log_exp_and_others")
                for u in range(N + 2):
                    if u in norm_at:
                        norm(*norm_at[u])
                    if u < N:
                        act.wait_ge(z_done, u + 1)
                        if u >= ring:
                            act.wait_ge(sp_step, sp_at(u - ring, RAW))
                        b = ex[:, u % ring, c0[u]:]
                        act.activation(b, zb[u % NZ][:, c0[u]:], ACT.Exp).then_inc(e_done, 1)
                        act.wait_ge(e_done, u + 1)
                        act.activation(b, b, ACT.Ln, bias=1.0).then_inc(l_done, 1)
                    if u >= 2:
                        weights(u - 2)

            @block.vector
            def _(dve):
                dve.memset(zeros[:], 0.0).then_inc(zero_done, 1)
                dve.wait_ge(zero_done, 1)
                for u in range(N + 2):
                    if u == 1:
                        dve.wait_ge(toep_made, 1)
                        dve.tensor_tensor(toep[0:6, :], tb[0:6, 0:N_TOEPLITZ], hot[0:6, 1, :], ALU.add).then_inc(toep_kept, 1)
                    if norm_at.get(u, (1, 0))[0] == 0:
                        v = norm_at[u][1]
                        dve.wait_ge(mean_done, v + 1)
                        if v:
                            dve.wait_ge(gn_done, v)
                        dve.tensor_tensor(yc[:], norm_part(v)[2], gb[:], ALU.subtract).then_inc(centred, 1)
                    if u < N:
                        dve.wait_ge(l_done, u + 1)
                        if u >= ring:
                            dve.wait_ge(s_done, u - ring + 1)
                            dve.wait_ge(acc_done, 2 * adds[u - ring])
                        d = slice(c0[u], c0[u] + P)
                        dve.scalar_tensor_tensor(sp[:, u % ring, c0[u]:], ex[:, u % ring, c0[u]:], CLAMP,
                                                 zb[u % NZ][:, c0[u]:], ALU.min, ALU.max).then_inc(sp_step, 1)
                        dve.wait_ge(sp_step, sp_at(u, RAW))
                        if diag[u]:
                            dve.tensor_tensor(sp[:, u % ring, d], sp[:, u % ring, d], C("key_before"),
                                              ALU.mult).then_inc(sp_step, 1)
                            dve.wait_ge(sp_step, sp_at(u, MASKED))
                        else:
                            dve.nop().then_inc(sp_step, 1)
                    if u >= 2:
                        v = u - 2
                        dve.wait_ge(w_raw, v + 1)
                        if diag[v]:
                            dve.copy_predicated(w[:, v % ring, c0[v]:c0[v] + P], masks[:, N_LEVELS * P:(N_LEVELS + 1) * P],
                                                zeros[:]).then_inc(w_done, 1)
                        else:
                            dve.nop().then_inc(w_done, 1)
                        if last[v]:
                            h, qg, _ = UNITS[v]
                            g = group_of[v]
                            rows = slice((h % 2) * HD, (h % 2 + 1) * HD)
                            dve.wait_ge(av_done, v + 1)
                            dve.tensor_copy(mixT[rows, 5 + h // 2, qg * HALF:(qg + 1) * HALF], ob[g % 2][rows, :]
                                            ).then_inc(o_out, 1)

            @block.gpsimd
            def _(pool):
                def norm(lag, v):
                    g, hs, y = norm_part(v)
                    if lag == 4:
                        pool.wait_ge(gn_rstd, v + 1)
                        pool.tensor_tensor(yc[:], yc[:], y2[:], ALU.mult).then_inc(gn_scaled, 1)
                    elif lag == 6:
                        pool.wait_ge(gn_gain, v + 1)
                        pool.tensor_tensor(yc[:], yc[:], R["bonus"][:, g, hs], ALU.add).then_inc(gn_bonus, 1)
                    elif lag == 7:
                        pool.wait_ge(gn_bonus, v + 1)
                        pool.tensor_tensor(y, yc[:], R["g"][:, g, hs], ALU.mult).then_inc(gn_done, 1)

                for u in range(N):
                    if u in norm_at:
                        norm(*norm_at[u])
                    if last[u]:
                        continue
                    pool.wait_ge(sp_step, sp_at(u, MASKED))
                    k, c = place[u], c0[u]
                    if k >= 1:
                        pool.wait_ge(acc_done, 2 * adds[u - 1])
                    if u >= 2:
                        pool.wait_ge(s_done, u - 1)
                    new, old, here = acc[:, adds[u] % 3, :], acc[:, adds[u - 1] % 3, :], sp[:, u % ring, :]
                    if diag[u]:
                        pool.tensor_copy(new[:, c:c + P], here[:, c:c + P]).then_inc(acc_done, 1 if k else 2)
                        c += P
                    if k:
                        pool.tensor_tensor(new[:, c:], old[:, c:], here[:, c:], ALU.add).then_inc(acc_done, 1 if diag[u] else 2)

    with ExitStack() as inner:
        lb = inner.enter_context(nc.psum_tensor("logit_banks", [P, 4 * HALF], F32))
        pTb = inner.enter_context(nc.psum_tensor("prob_banks", [P, 3 * HALF], F32))
        ob = inner.enter_context(nc.psum_tensor("out_bank", [P, HALF], F32))
        blocks = lambda n: (1,) if n == 0 else (0, 1)
        keys = [slice(P, 256) if n == 0 else slice(0, 256) for n in range(NT)]
        with nc.Block() as block:
            @block.tensor
            def _(pe):
                pe.wait_ge(qa_in, 64)

                def logits(n):
                    if n:
                        pe.wait_ge(l_kept, n)
                    lo = keys[n].start
                    for e in range(2):
                        rows = slice(e * HD, (e + 1) * HD)
                        for j in range(3):
                            at = e * 2 * HALF + j * 256
                            mm = pe.matmul(lb[:, at + lo:at + 256], qa[rows, j, n * P:(n + 1) * P],
                                           qa[rows, 3, (n - 1) * P + lo:(n + 1) * P], start=True, stop=True)
                    mm.then_inc(l_made, 1)

                def turn(n):
                    pe.wait_ge(p_norm, n + 1)
                    if n:
                        pe.wait_ge(pT_kept, n)
                    for h in range(6):
                        for kb in blocks(n):
                            mm = pe.transpose(pTb[:, (2 * h + kb) * P:(2 * h + kb + 1) * P],
                                              Pr[:, n % 2, h, kb * P:(kb + 1) * P], C("ident"))
                    mm.then_inc(pT_made, 1)

                def outputs(n):
                    pe.wait_ge(pT_kept, n + 1)
                    if n:
                        pe.wait_ge(o_kept, n)
                    for h in range(6):
                        e, j = h // 3, h % 3
                        for kb in blocks(n):
                            mm = pe.matmul(ob[e * HD:(e + 1) * HD, j * P:(j + 1) * P],
                                           v_tok[:, n - 1 + kb, 384 + e * HD:384 + (e + 1) * HD], PrT[:, n % 2, 2 * h + kb, :],
                                           start=kb == blocks(n)[0], stop=kb == 1)
                    mm.then_inc(o_made, 1)

                logits(0)
                logits(1)
                for n in range(NT + 1):
                    if n + 2 < NT:
                        logits(n + 2)
                    if n:
                        outputs(n - 1)
                    if n < NT:
                        turn(n)

            @block.scalar
            def _(act):
                def exponentials(n):
                    b = n % 2
                    act.wait_ge(stat, 4 * (n + 1))
                    if n >= 2:
                        act.wait_ge(pT_made, n - 1)
                    for h in range(6):
                        act.activation(Pr[:, b, h, keys[n]], L[:, b, h, keys[n]], ACT.Exp, bias=st[:, b, 1, h:h + 1],
                                       accum_out=st[:, b, 2, h:h + 1])
                    act.activation(st[:, b, 3, 0:6], st[:, b, 3, 0:6], ACT.Exp).then_inc(p_done, 1)

                exponentials(0)
                for n in range(NT):
                    if n + 1 < NT:
                        exponentials(n + 1)
                    act.wait_ge(pT_made, n + 1)
                    if n >= 2:
                        act.wait_ge(o_made, n - 1)
                    if n == 0:
                        act.copy(PrT[:, 0, :, :].rearrange("p (h k) q -> p h k q", k=2)[:, :, 1, :],
                                 pTb[:].rearrange("p (h k q) -> p h k q", h=6, k=2)[:, :, 1, :]).then_inc(pT_kept, 1)
                    else:
                        act.copy(PrT[:, n % 2, :, :].rearrange("p a q -> p (a q)"), pTb[:]).then_inc(pT_kept, 1)

            @block.vector
            def _(dve):
                def row(n, j):
                    return st[:, n % 2, j, 0:6]

                def logits(n):
                    b, k = n % 2, keys[n]
                    dve.wait_ge(l_made, n + 1)
                    if n >= 2:
                        dve.wait_ge(p_done, n - 1)
                    logit = lb[:].rearrange("p (e x) -> p e x", e=2)[:, :, 0:768].rearrange("p e (j k) -> p e j k", j=3)
                    dve.tensor_tensor(L[:, b, :, :].rearrange("p (e j) k -> p e j k", e=2)[:, :, :, k], logit[:, :, :, k],
                                      bias[:].rearrange("p (e j) k -> p e j k", e=2)[:, :, :, k], ALU.add).then_inc(l_kept, 1)
                    dve.wait_ge(l_kept, n + 1)
                    dve.tensor_reduce(row(n, 0), L[:, b, :, k], AX, ALU.max).then_inc(stat, 1)
                    dve.wait_ge(stat, 4 * n + 1)
                    dve.tensor_tensor(row(n, 0), row(n, 0), sink[:, 0:6], ALU.max).then_inc(stat, 1)
                    dve.wait_ge(stat, 4 * n + 2)
                    dve.tensor_scalar(row(n, 1), row(n, 0), -1.0, None, ALU.mult).then_inc(stat, 1)
                    dve.wait_ge(stat, 4 * n + 3)
                    dve.tensor_tensor(row(n, 3), sink[:, 0:6], row(n, 1), ALU.add).then_inc(stat, 1)

                def normalise(n):
                    b, k = n % 2, keys[n]
                    dve.wait_ge(p_done, n + 1)
                    dve.tensor_tensor(row(n, 4), row(n, 2), row(n, 3), ALU.add).then_inc(stat2, 1)
                    dve.wait_ge(stat2, 2 * n + 1)
                    dve.reciprocal(row(n, 5), row(n, 4)).then_inc(stat2, 1)
                    dve.wait_ge(stat2, 2 * n + 2)
                    dve.tensor_tensor(Pr[:, b, :, k], Pr[:, b, :, k], bcast(row(n, 5), [1, 6], [0, k.stop - k.start]),
                                      ALU.mult).then_inc(p_norm, 1)

                dve.wait_ge(bias_in, 16)
                dve.wait_ge(rel_in, 48)
                logits(0)
                for n in range(NT + 1):
                    if n + 1 < NT:
                        logits(n + 1)
                    if n < NT:
                        normalise(n)
                    if n:
                        dve.wait_ge(o_made, n)
                        dve.tensor_copy(mixT[:, 0:3, (n - 1) * P:n * P],
                                        ob[:, 0:3 * P].rearrange("p (j q) -> p j q", j=3)).then_inc(o_kept, 1)


N_EXPERTS, N_GROUPS, PER_GROUP, TOP_K, FF = 16, 4, 4, 2, 256
MAX_BLOCKS = TOP_K * T // P + N_EXPERTS - 1 + 1
MIN_BLOCKS = TOP_K * T // P
PLAN_ENDS = MAX_BLOCKS + 1
PLAN = PLAN_ENDS + N_EXPERTS
EXPERTS_AT = 108672
W_COLS = 2 * ND * FF + 2 * D
N_WBUF = 3
SPARE_ROW = TOP_K * T
SLOT_BLOCKS = MAX_BLOCKS + 1
BIG = 1e30

ROUTE = {"iota16": (0, 16), "group16": (16, 16), "iota4": (32, 4), "edges": (36, 8), "blocks": (48, 33),
         "iota16_far": (84, 16), "iota4_far": (100, 4), "places": (104, P)}
N_ROUTE = 104 + P
FAR = 100.0


def routing_constants():
    c = np.zeros((1, N_ROUTE), np.float32)
    c[0, 0:16] = np.arange(16)
    c[0, 16:32] = np.arange(16) // PER_GROUP
    c[0, 32:36] = np.arange(4)
    c[0, 36:44] = np.arange(8) * P
    c[0, 48:81] = np.arange(33)
    c[0, 84:100] = np.arange(16) + FAR
    c[0, 100:104] = np.arange(4) + FAR
    c[0, 104:] = np.arange(P)
    return c


def mix_and_route(nc, ctx, wgu_d, wd_d, h_dram, h1_dram, rows4, rw_d, rb_d, route_d, C, mixT, w_out, w_out_in, K, mem):
    sem = lambda n: ctx.enter_context(nc.semaphore(n))
    h1, rows, gates, slots, plan = K["h1"], K["rows"], K["gates"], K["slots"], K["plan"]
    hb_at = mem.at
    hb = mem.put("h_in", [P, 2, D])
    r_at = mem.at
    r = mem.put("residual", [P, 2, D])
    xT = mem.put("h1_T", [P, ND, P])
    rw = mem.put("router_w", [P, ND, 16])
    rb = mem.put("router_bias", [P, 16])
    rc = mem.put("route_consts", [P, N_ROUTE])
    stats = mem.put("ln1_stats", [P, 12])
    mv = mem.put("ln1_mv", [P, NT, 2])
    std = mem.put("ln1_std", [P, NT, 2])
    ids = mem.put("token_ids", [P, TOP_K, NT, 2], I32)
    ids_f = mem.put("ids_f", [P, TOP_K, NT, 2])
    where_i = mem.put("where_i", [P, 2, TOP_K, NT], I32)
    where = mem.put("where", [P, 2, TOP_K, NT])
    at_place = nc.alloc_sbuf_tensor_at("at_place", [P, TOP_K * NT, P], F32, offset=hb_at)
    in_block = nc.alloc_sbuf_tensor_at("in_block", [P, TOP_K * NT, SLOT_BLOCKS], F32, offset=r_at)
    block_ids = nc.alloc_sbuf_tensor_at("block_ids", [P, TOP_K * NT, SLOT_BLOCKS, 2], F32,
                                        offset=r_at + 4 * TOP_K * NT * SLOT_BLOCKS)
    big = lambda n: mem.put(n, [P, NT, 16])
    score, sel, selm, t16, oh1, oh2, both, base, rank = (
        big(n) for n in ("score", "sel", "sel_in_group", "t16", "first_choice", "second_choice", "both", "base", "rank"))
    n_e = mem.put("n_e", [P, 16])
    hi = mem.put("hi", [P, NT, 4, 2])
    lo = mem.put("lo", [P, NT, 4, 2])
    g4 = mem.put("g4", [P, 3, NT, 4])
    t8 = mem.put("t8", [P, 6, NT])
    cmp_ = mem.put("block_compare", [P, 32, 16])
    e16 = mem.put("e16", [P, 4, 16])
    plan_f = mem.put("plan_f", [P, PLAN])
    h_in = [sem("h_in0"), sem("h_in1")]
    par_in = sem("route_in")
    m_made, resid, ln_stat, ln_aggr, ln_std, ln_rstd, xn = (sem(f"ln1_{n}") for n in (
        "m", "resid", "stat", "aggr", "std", "rstd", "xn"))
    xT_made, xT_kept, r_made, h1_mul, h1_done = (sem(n) for n in ("rt_xT_made", "rt_xT_kept", "rt_made", "h1_mul", "h1_done"))
    h1_out, ids_done, ids_summed = sem("h1_out"), sem("ids_done"), sem("ids_summed")
    scored, routed, counted, ranked = sem("scored"), sem("routed"), sem("counted"), sem("ranked")
    with ExitStack() as inner:
        mb = [inner.enter_context(nc.psum_tensor(f"m{b}", [P, HALF], F32)) for b in range(4)]
        xb = [inner.enter_context(nc.psum_tensor(f"rx{b}", [P, HALF], F32)) for b in range(2)]
        rbk = inner.enter_context(nc.psum_tensor("router_bank", [P, HALF], F32))
        cb = inner.enter_context(nc.psum_tensor("count_bank", [P, HALF], F32))
        with nc.Block() as block:
            @block.sync
            def _(sp):
                def load_h(i):
                    sp.dma_start(hb[:, i % 2, :], h_dram[i * P:(i + 1) * P, :]).then_inc(h_in[i % 2], 16)

                for i in range(2):
                    load_h(i)
                for k in range(4):
                    sp.dma_start(rows[:, k, :], rows4[k:k + 1, :].to_broadcast([P, D])).then_inc(par_in, 16)
                sp.dma_start(rw[:].rearrange("p k e -> p (k e)"), rw_d).then_inc(par_in, 16)
                sp.dma_start(rb[:], rb_d.to_broadcast([P, 16])).then_inc(par_in, 16)
                sp.dma_start(rc[:], route_d.to_broadcast([P, N_ROUTE])).then_inc(par_in, 16)
                for i in range(2, NT):
                    sp.wait_ge(resid, 2 * (i - 1))
                    load_h(i)
                    sp.wait_ge(h1_done, i - 1)
                    sp.dma_start(h1_dram[(i - 2) * P:(i - 1) * P, :], h1[:, i - 2, :]).then_inc(h1_out, 16)
                for i in range(NT - 2, NT):
                    sp.wait_ge(h1_done, i + 1)
                    sp.dma_start(h1_dram[i * P:(i + 1) * P, :], h1[:, i, :]).then_inc(h1_out, 16)
                for e in range(2):
                    load_expert(sp, e, K, wgu_d, wd_d)
                sp.wait_ge(h1_out, 16 * NT)

            @block.tensor
            def _(pe):
                def mix(i, between=None):
                    for half in range(2):
                        if half and between is not None:
                            router(between)
                        n = 2 * i + half
                        if n >= 4:
                            pe.wait_ge(resid, n - 3)
                        for k in range(ND):
                            mm = pe.matmul(mb[n % 4][:], mixT[:, k, i * P:(i + 1) * P],
                                           w_out[:, k, half * HALF:(half + 1) * HALF], start=k == 0, stop=k == ND - 1)
                        mm.then_inc(m_made, 1)

                def turn(i):
                    pe.wait_ge(xn, i + 1)
                    if i:
                        pe.wait_ge(xT_kept, ND * i)
                    for d in range(ND):
                        mm = pe.transpose(xb[d // 4][:, (d % 4) * P:(d % 4 + 1) * P], r[:, i % 2, d * P:(d + 1) * P], C("ident"))
                    mm.then_inc(xT_made, 1)

                def router(i):
                    pe.wait_ge(xT_kept, ND * (i + 1))
                    for d in range(ND):
                        mm = pe.matmul(rbk[:, i * 16:(i + 1) * 16], xT[:, d, :], rw[:, d, :], start=d == 0, stop=d == ND - 1)
                    mm.then_inc(r_made, 1)

                pe.wait_ge(w_out_in, 16)
                mix(0)
                mix(1)
                pe.wait_ge(par_in, 16 * 7)
                for i in range(NT):
                    if i + 2 < NT:
                        mix(i + 2, i - 1 if i else None)
                    elif i:
                        router(i - 1)
                    turn(i)
                router(NT - 1)
                pe.wait_ge(routed, ROUTED["both"])
                pe.matmul(cb[:, 0:P], C("key_before"), both[:].rearrange("p i e -> p (i e)"), start=True, stop=True)
                pe.matmul(cb[:, P:2 * P], C("ones"), both[:].rearrange("p i e -> p (i e)"), start=True, stop=True).then_inc(counted, 1)
                pe.wait_ge(routed, ROUTED["at_place"])
                for n in range(TOP_K * NT):
                    mm = pe.matmul(rbk[:, 0:2 * SLOT_BLOCKS], at_place[:, n, :], block_ids[:, n, :, :].rearrange("p b c -> p (b c)"),
                                   start=n == 0, stop=n == TOP_K * NT - 1)
                mm.then_inc(ids_summed, 1)

            @block.scalar
            def _(act):
                for i in range(NT):
                    act.wait_ge(ln_aggr, i + 1)
                    act.activation(std[:, i, 0:1], mv[:, i, 1:2], ACT.Sqrt, bias=LN_EPS).then_inc(ln_std, 1)
                    act.wait_ge(xT_made, i + 1)
                    if i:
                        act.wait_ge(r_made, i)
                    for d in range(ND):
                        act.activation(xT[:, d, :], xb[d // 4][:, (d % 4) * P:(d % 4 + 1) * P], ACT.Identity,
                                       bias=C("ln1_b", d), scale=C("ln1_g", d)).then_inc(xT_kept, 1)
                act.wait_ge(r_made, NT)
                act.activation(score[:].rearrange("p i e -> p (i e)"), rbk[:, 0:P], ACT.Sigmoid).then_inc(scored, 1)

            @block.gpsimd
            def _(pool):
                for k in range(TOP_K):
                    pool.iota(ids[:, k, :, 0], pattern=[[P, NT]], base=0, channel_multiplier=1).then_inc(ids_done, 1)
                    pool.iota(ids[:, k, :, 1], pattern=[[P, NT]], base=k * T - SPARE_ROW, channel_multiplier=1).then_inc(ids_done, 1)
                pool.wait_ge(par_in, 16 * 7)
                for i in range(NT):
                    pool.wait_ge(xn, i + 1)
                    pool.tensor_tensor(h1[:, i, :], r[:, i % 2, :], rows[:, 0, :], ALU.mult).then_inc(h1_mul, 1)
                    pool.wait_ge(h1_mul, i + 1)
                    pool.tensor_tensor(h1[:, i, :], h1[:, i, :], rows[:, 1, :], ALU.add).then_inc(h1_done, 1)

            @block.vector
            def _(dve):
                for i in range(NT):
                    dve.wait_ge(h_in[i % 2], 16 * (i // 2 + 1))
                    if i >= 2:
                        dve.wait_ge(h1_mul, i - 1)
                        dve.wait_ge(xT_made, i - 1)
                    for half in range(2):
                        hs = slice(half * HALF, (half + 1) * HALF)
                        dve.wait_ge(m_made, 2 * i + half + 1)
                        dve.scalar_tensor_tensor(r[:, i % 2, hs], hb[:, i % 2, hs], ALPHA, mb[(2 * i + half) % 4][:],
                                                 ALU.mult, ALU.add).then_inc(resid, 1)
                        dve.wait_ge(resid, 2 * i + half + 1)
                        dve.bn_stats(stats[:, 6 * half:6 * half + 6], r[:, i % 2, hs]).then_inc(ln_stat, 1)
                    dve.wait_ge(ln_stat, 2 * i + 2)
                    dve.bn_aggr(mv[:, i, :], stats[:]).then_inc(ln_aggr, 1)
                    dve.wait_ge(ln_std, i + 1)
                    dve.reciprocal(std[:, i, 1:2], std[:, i, 0:1]).then_inc(ln_rstd, 1)
                    dve.wait_ge(ln_rstd, i + 1)
                    dve.tensor_scalar(r[:, i % 2, :], r[:, i % 2, :], mv[:, i, 0:1], std[:, i, 1:2],
                                      ALU.subtract, ALU.mult).then_inc(xn, 1)
                row = lambda n: rc[:, ROUTE[n][0]:ROUTE[n][0] + ROUTE[n][1]]
                per_token = lambda ap: bcast(ap, [1, NT], [0, 16])
                sel4 = sel[:].rearrange("p i (g e) -> p i g e", e=PER_GROUP)
                top, second, gsum = (g4[:, k, :, :] for k in range(3))
                gbest, m1, m2, w1, w2, wsum = (t8[:, k, :] for k in range(6))
                blocks, ends, starts, _ = (e16[:, k, :] for k in range(4))
                dve.wait_ge(par_in, 16 * 7)
                flat = lambda ap: ap.rearrange("p k i -> p (k i)")
                summed = rbk[:, 0:2 * SLOT_BLOCKS].rearrange("p (b c) -> p b c", c=2)
                n = 0
                for name in ROUTE_STEPS:
                    if n:
                        dve.wait_ge(routed, n)
                    if name == "sel":
                        dve.wait_ge(scored, 1)
                        ins = dve.tensor_tensor(sel[:], score[:], bcast(rb[:], [0, NT], [1, 16]), ALU.add)
                    elif name == "hi":
                        ins = dve.tensor_tensor(hi[:], sel4[:, :, :, 0:2], sel4[:, :, :, 2:4], ALU.max)
                    elif name == "lo":
                        ins = dve.tensor_tensor(lo[:], sel4[:, :, :, 0:2], sel4[:, :, :, 2:4], ALU.min)
                    elif name == "top":
                        ins = dve.tensor_tensor(top, hi[:, :, :, 0], hi[:, :, :, 1], ALU.max)
                    elif name == "hi_min":
                        ins = dve.tensor_tensor(second, hi[:, :, :, 0], hi[:, :, :, 1], ALU.min)
                    elif name == "lo_max":
                        ins = dve.tensor_tensor(gsum, lo[:, :, :, 0], lo[:, :, :, 1], ALU.max)
                    elif name == "second":
                        ins = dve.tensor_tensor(second, second, gsum, ALU.max)
                    elif name == "gsum":
                        ins = dve.tensor_tensor(gsum, top, second, ALU.add)
                    elif name == "gmax":
                        ins = dve.tensor_reduce(gbest, gsum, AX, ALU.max)
                    elif name == "g_is":
                        ins = dve.tensor_tensor(top, gsum, bcast(gbest, [1, NT], [0, 4]), ALU.is_equal)
                    elif name == "g_cand":
                        ins = dve.scalar_tensor_tensor(top, top, -FAR, bcast(row("iota4_far"), [0, NT], [1, 4]), ALU.mult, ALU.add)
                    elif name == "g_index":
                        ins = dve.tensor_reduce(gbest, top, AX, ALU.min)
                    elif name == "in_group":
                        ins = dve.tensor_tensor(t16[:], bcast(row("group16"), [0, NT], [1, 16]), per_token(gbest), ALU.is_equal)
                    elif name == "outside":
                        ins = dve.tensor_scalar(t16[:], t16[:], BIG, -BIG, ALU.mult, ALU.add)
                    elif name == "selm":
                        ins = dve.tensor_tensor(selm[:], sel[:], t16[:], ALU.add)
                    elif name in ("max1", "max2"):
                        ins = dve.tensor_reduce(m1 if name == "max1" else m2, selm[:], AX, ALU.max)
                    elif name in ("is1", "is2"):
                        ins = dve.tensor_tensor(t16[:], selm[:], per_token(m1 if name == "is1" else m2), ALU.is_equal)
                    elif name in ("cand1", "cand2"):
                        ins = dve.scalar_tensor_tensor(t16[:], t16[:], -FAR, bcast(row("iota16_far"), [0, NT], [1, 16]),
                                                       ALU.mult, ALU.add)
                    elif name in ("index1", "index2"):
                        ins = dve.tensor_reduce(m1 if name == "index1" else m2, t16[:], AX, ALU.min)
                    elif name in ("hot1", "hot2"):
                        ins = dve.tensor_tensor(oh1[:] if name == "hot1" else oh2[:], bcast(row("iota16"), [0, NT], [1, 16]),
                                                per_token(m1 if name == "hot1" else m2), ALU.is_equal)
                    elif name == "without1":
                        ins = dve.scalar_tensor_tensor(selm[:], oh1[:], -2 * BIG, selm[:], ALU.mult, ALU.add)
                    elif name == "both":
                        ins = dve.tensor_tensor(both[:], oh1[:], oh2[:], ALU.add)
                    elif name in ("s1", "s2"):
                        ins = dve.tensor_tensor(t16[:], oh1[:] if name == "s1" else oh2[:], score[:], ALU.mult)
                    elif name in ("w1", "w2"):
                        ins = dve.tensor_reduce(w1 if name == "w1" else w2, t16[:], AX, ALU.add)
                    elif name == "wsum":
                        ins = dve.tensor_tensor(wsum, w1, w2, ALU.add)
                    elif name == "wrec":
                        ins = dve.reciprocal(wsum, wsum)
                    elif name in ("gate1", "gate2"):
                        k = int(name[4]) - 1
                        ins = dve.tensor_tensor(gates[:, k, :], (w1, w2)[k], wsum, ALU.mult)
                    elif name == "base0":
                        dve.wait_ge(counted, 1)
                        ins = dve.memset(base[:, 0, :], 0.0)
                    elif name[:4] == "base":
                        i = int(name[4:])
                        dst = n_e[:] if i == NT else base[:, i, :]
                        ins = dve.tensor_tensor(dst, base[:, i - 1, :], cb[:, P + 16 * (i - 1):P + 16 * i], ALU.add)
                    elif name == "rank":
                        ins = dve.tensor_tensor(rank[:], cb[:, 0:P].rearrange("p (i e) -> p i e", i=NT), base[:], ALU.add)
                    elif name == "edges":
                        ins = dve.tensor_tensor(cmp_[:, 0:16, 0:8], bcast(n_e[:], [1, 16], [0, 8]),
                                                bcast(row("edges"), [0, 16], [1, 8]), ALU.is_gt)
                    elif name == "blocks":
                        ins = dve.tensor_reduce(blocks, cmp_[:, 0:16, 0:8], AX, ALU.add)
                    elif name == "ends":
                        ins = dve.tensor_tensor_scan(ends, C("ones")[:, 0:16], blocks, 0.0, ALU.mult, ALU.add)
                    elif name == "starts":
                        ins = dve.tensor_tensor(starts, ends, blocks, ALU.subtract)
                    elif name == "start_slots":
                        ins = dve.tensor_scalar(starts, starts, float(P), None, ALU.mult)
                    elif name == "slot":
                        ins = dve.tensor_tensor(rank[:], rank[:], bcast(starts, [0, NT], [1, 16]), ALU.add)
                    elif name in ("slot1", "slot2"):
                        ins = dve.tensor_tensor(t16[:], rank[:], oh1[:] if name == "slot1" else oh2[:], ALU.mult)
                    elif name in ("sum1", "sum2"):
                        ins = dve.tensor_reduce(m1 if name == "sum1" else m2, t16[:], AX, ALU.add)
                    elif name in ("int1", "int2"):
                        k = int(name[3]) - 1
                        ins = dve.tensor_copy(slots[:, k, :], (m1, m2)[k])
                    elif name == "ended":
                        ins = dve.tensor_tensor(cmp_[:], bcast(row("blocks")[:, 0:32], [1, 32], [0, 16]),
                                                bcast(ends, [0, 32], [1, 16]), ALU.is_ge)
                    elif name == "expert":
                        ins = dve.tensor_reduce(plan_f[:, 0:32], cmp_[:], AX, ALU.add)
                    elif name == "expert_max":
                        ins = dve.tensor_scalar(plan_f[:, 0:32], plan_f[:, 0:32], float(N_EXPERTS - 1), None, ALU.min)
                    elif name == "total":
                        ins = dve.tensor_scalar(plan_f[:, MAX_BLOCKS:MAX_BLOCKS + 1], ends[:, 15:16], float(-MIN_BLOCKS), None, ALU.add)
                    elif name == "plan_ends":
                        ins = dve.tensor_copy(plan_f[:, PLAN_ENDS:PLAN], ends)
                    elif name == "plan":
                        ins = dve.tensor_copy(plan[:], plan_f[0:1, :])
                    elif name == "ids_f":
                        dve.wait_ge(ids_done, 2 * TOP_K)
                        ins = dve.tensor_copy(ids_f[:], ids[:])
                    elif name == "block":
                        ins = dve.tensor_scalar(where_i[:, 0, :, :], slots[:], P.bit_length() - 1, None, ALU.logical_shift_right)
                    elif name == "place":
                        ins = dve.tensor_scalar(where_i[:, 1, :, :], slots[:], P - 1, None, ALU.bitwise_and)
                    elif name == "where":
                        ins = dve.tensor_copy(where[:], where_i[:])
                    elif name == "at_place":
                        ins = dve.tensor_tensor(at_place[:], bcast(row("places"), [0, TOP_K * NT], [1, P]),
                                                bcast(flat(where[:, 1, :, :]), [1, TOP_K * NT], [0, P]), ALU.is_equal)
                    elif name == "in_block":
                        dve.wait_ge(h1_mul, NT)
                        dve.wait_ge(xT_made, NT)
                        ins = dve.tensor_tensor(in_block[:], bcast(row("blocks"), [0, TOP_K * NT], [1, SLOT_BLOCKS]),
                                                bcast(flat(where[:, 0, :, :]), [1, TOP_K * NT], [0, SLOT_BLOCKS]), ALU.is_equal)
                    elif name in ("block_ids0", "block_ids1"):
                        c = int(name[-1])
                        each = ids_f[:].rearrange("p k i c -> p (k i) c")[:, :, c]
                        ins = dve.tensor_tensor(block_ids[:, :, :, c], in_block[:], bcast(each, [2, TOP_K * NT], [0, SLOT_BLOCKS]),
                                                ALU.mult)
                    elif name == "slot_ids0":
                        dve.wait_ge(ids_summed, 1)
                        ins = dve.tensor_copy(K["ids"][:, :, 0], summed[:, :, 0])
                    elif name == "slot_ids1":
                        ins = dve.tensor_scalar(K["ids"][:, :, 1], summed[:, :, 1], float(SPARE_ROW), None, ALU.add)
                    ins.then_inc(routed, 1)
                    n += 1


ROUTE_STEPS = ["sel", "hi", "lo", "top", "hi_min", "lo_max", "second", "gsum", "gmax", "g_is", "g_cand", "g_index",
               "in_group", "outside", "selm", "max1", "is1", "cand1", "index1", "hot1",
               "without1", "max2", "is2", "cand2", "index2", "hot2", "both", "s1", "w1", "s2", "w2", "wsum",
               "wrec", "gate1", "gate2", "base0", "base1", "base2", "base3", "base4", "base5", "base6", "base7",
               "base8", "rank", "edges", "blocks", "ends", "starts", "start_slots", "slot", "slot1", "sum1", "int1",
               "slot2", "sum2", "int2", "ids_f", "block", "place", "where", "in_block", "block_ids0", "block_ids1", "at_place",
               "ended", "expert", "expert_max", "total", "plan_ends", "plan", "slot_ids0", "slot_ids1"]
ROUTED = {name: k + 1 for k, name in enumerate(ROUTE_STEPS)}


def weight_buffer(e):
    return 2 * e % N_WBUF


def load_expert(eng, e, K, wgu_d, wd_d):
    w = weight_buffer(e)
    n = 2 * ND * FF
    eng.dma_start(K["experts"][:, w, 0:n], wgu_d[e, :, :]).then_inc(K["experts_in"][w], 16)
    eng.dma_start(K["experts"][:, w, n:n + 2 * D], wd_d[e, :, :]).then_inc(K["experts_in"][w], 16)


def experts(nc, ctx, h1_dram, y_dram, wgu_d, wd_d, out, C, K, mem):
    sem = lambda n: ctx.enter_context(nc.semaphore(n))
    h1, rows, gates, slots, plan = K["h1"], K["rows"], K["gates"], K["slots"], K["plan"]
    W = K["experts"]
    WG = W[:, :, 0:2 * ND * FF].rearrange("p w (k f) -> p w k f", k=ND)
    WD = W[:, :, 2 * ND * FF:2 * ND * FF + 2 * D].rearrange("p w (k f) -> p w k f", k=2)
    w_in = K["experts_in"]
    idx = K["ids"]
    idx_x = mem.put("gather_ids", [P, 2, 2], I32)
    idx_y = mem.put("scatter_ids", [P, 2, 2], I32)
    turn = mem.put("turn", [P, 1])
    xg = mem.put("slot_rows", [P, 2, D])
    xT = mem.put("slot_rows_T", [P, ND, P])
    sg = mem.put("silu_gate", [P, FF])
    ac = mem.put("act", [P, FF])
    aT = mem.put("act_T", [P, 2, P])
    y = mem.put("slot_out", [P, 2, D])
    w_ready, stored = sem("weights_ready"), sem("blocks_stored")
    x_in, y_out = ([sem(f"{n}{b}") for b in range(2)] for n in ("xg_in", "y_out"))
    idx_x_made, idx_y_made = sem("idx_x_made"), sem("idx_y_made")
    gu_made, xT_made, d_made, aT_made = sem("gu_made"), sem("xg_T_made"), sem("down_made"), sem("act_T_made")
    xT_act, xT_dve, silu_done, act_done, aT_kept = (sem(n) for n in ("xT_kept_act", "xT_kept_dve", "silu_done", "act_done", "act_T_kept"))
    y_act, y_dve = sem("y_kept_act"), sem("y_kept_dve")
    trips = lambda eng: eng.snap((eng.value_load(plan[0:1, MAX_BLOCKS:MAX_BLOCKS + 1], min_val=0,
                                                 max_val=MAX_BLOCKS - MIN_BLOCKS) + 1) // 2 + MIN_BLOCKS // 2,
                                 min_val=MIN_BLOCKS // 2, max_val=MAX_BLOCKS // 2)

    def wait(eng, s, value):
        if not isinstance(value, int) or value > 0:
            eng.wait_ge(s, value)
    with ExitStack() as inner:
        gub = inner.enter_context(nc.psum_tensor("gu_bank", [P, HALF], F32))
        xb = [inner.enter_context(nc.psum_tensor(f"xg_bank{b}", [P, HALF], F32)) for b in range(2)]
        ab = inner.enter_context(nc.psum_tensor("act_bank", [P, HALF], F32))
        yb = [inner.enter_context(nc.psum_tensor(f"y_bank{b}", [P, HALF], F32)) for b in range(4)]
        with nc.Block() as block:
            @block.sync
            def _(sp):
                load = lambda e: load_expert(sp, e, K, wgu_d, wd_d)

                def signal(e):
                    sp.wait_ge(w_in[weight_buffer(e)], 32 * (e // N_WBUF + 1))
                    sp.nop().then_inc(w_ready, 1)

                for b in range(2):
                    sp.wait_ge(x_in[b], 16)
                load(2)
                signal(0)
                for e in range(N_WBUF, N_EXPERTS):
                    signal(e - N_WBUF + 1)
                    at = PLAN_ENDS + e - N_WBUF
                    sp.wait_ge(stored, sp.value_load(plan[0:1, at:at + 1], min_val=0, max_val=MAX_BLOCKS) + 1)
                    load(e)
                for e in range(N_EXPERTS - N_WBUF + 1, N_EXPERTS):
                    signal(e)

            @block.gpsimd
            def _(pool):
                def gather(s, b, uses):
                    wait(pool, xT_made, s - 1)
                    wait(pool, x_in[b], 16 * uses)
                    pool.tensor_copy(idx_x[:, b, :], idx[:, bass.ds(s, 1), :].rearrange("p o two -> p (o two)")).then_inc(idx_x_made, 1)
                    pool.wait_ge(idx_x_made, s + 1)
                    pool.tensor_tensor(turn[:], C("ones")[:, 0:1], C("ones")[:, 0:1], ALU.add)
                    pool.indirect_dma_start(xg[:, b, :], None, h1_dram,
                                            bass.IndirectOffsetOnAxis(ap=idx_x[:, b, 0:1], axis=0)).then_inc(x_in[b], 16)

                def scatter(s, b, uses):
                    wait(pool, y_out[b], 16 * uses)
                    pool.tensor_copy(idx_y[:, b, :], idx[:, bass.ds(s, 1), :].rearrange("p o two -> p (o two)")).then_inc(idx_y_made, 1)
                    pool.wait_ge(idx_y_made, s + 1)
                    pool.wait_ge(y_act, s + 1)
                    pool.wait_ge(y_dve, s + 1)
                    wait(pool, y_out[1 - b], 16 * (uses + b))
                    pool.tensor_tensor(turn[:], C("ones")[:, 0:1], C("ones")[:, 0:1], ALU.add).then_inc(stored, 1)
                    pool.indirect_dma_start(y_dram, bass.IndirectOffsetOnAxis(ap=idx_y[:, b, 1:2], axis=0),
                                            y[:, b, :], None).then_inc(y_out[b], 16)

                pool.memset(turn[:], 0).then_inc(stored, 1)
                n = trips(pool)
                gather(0, 0, 0)
                gather(1, 1, 0)
                gather(2, 0, 1)
                def trip(q):
                    gather(2 * q + 1, 1, q)
                    scatter(2 * q - 2, 0, q - 1)
                    gather(2 * q + 2, 0, q + 1)
                    scatter(2 * q - 1, 1, q - 1)

                trip(1)
                with pool.Fori(2, n) as q:
                    trip(q)
                scatter(2 * n - 2, 0, n - 1)
                scatter(2 * n - 1, 1, n - 1)
                for b in range(2):
                    pool.wait_ge(y_out[b], 16 * n)

            @block.tensor
            def _(pe):
                def weights_of(s):
                    e = pe.value_load(plan[0:1, bass.ds(s, 1)], min_val=0, max_val=N_EXPERTS - 1)
                    pe.wait_ge(w_ready, e + 1)
                    return pe.snap((e * 2) % N_WBUF, min_val=0, max_val=N_WBUF - 1)

                def gate_up(q, b):
                    s = 2 * q + b
                    w = weights_of(s)
                    pe.wait_ge(xT_act, s + 1)
                    pe.wait_ge(xT_dve, s + 1)
                    wait(pe, act_done, s)
                    for k in range(ND):
                        mm = pe.matmul(gub[:], xT[:, k, :], WG[:, bass.ds(w, 1), k, :].rearrange("p o f -> p (o f)"), start=k == 0, stop=k == ND - 1)
                    mm.then_inc(gu_made, 1)

                def turn_x(q, b):
                    s = 2 * q + b
                    pe.wait_ge(x_in[b], 16 * (q + 1))
                    wait(pe, xT_act, s)
                    wait(pe, xT_dve, s)
                    for k in range(ND):
                        mm = pe.transpose(xb[k // 4][:, (k % 4) * P:(k % 4 + 1) * P], xg[:, b, k * P:(k + 1) * P], C("ident"))
                    mm.then_inc(xT_made, 1)

                def down(q, b):
                    s = 2 * q + b
                    w = weights_of(s)
                    pe.wait_ge(aT_kept, s + 1)
                    wait(pe, y_act, s - 1)
                    wait(pe, y_dve, s - 1)
                    for half in range(2):
                        for k in range(2):
                            mm = pe.matmul(yb[2 * b + half][:], aT[:, k, :], WD[:, bass.ds(w, 1), k, half * HALF:(half + 1) * HALF].rearrange("p o f -> p (o f)"),
                                           start=k == 0, stop=k == 1)
                    mm.then_inc(d_made, 1)

                def turn_act(q, b):
                    s = 2 * q + b
                    pe.wait_ge(act_done, s + 1)
                    wait(pe, aT_kept, s)
                    for k in range(2):
                        mm = pe.transpose(ab[:, k * P:(k + 1) * P], ac[:, k * P:(k + 1) * P], C("ident"))
                    mm.then_inc(aT_made, 1)

                n = trips(pe)
                turn_x(0, 0)
                gate_up(0, 0)
                turn_x(0, 1)
                turn_act(0, 0)
                gate_up(0, 1)
                turn_x(1, 0)
                down(0, 0)
                turn_act(0, 1)
                def trip(q):
                    gate_up(q, 0)
                    turn_x(q, 1)
                    down(q - 1, 1)
                    turn_act(q, 0)
                    gate_up(q, 1)
                    turn_x(q + 1, 0)
                    down(q, 0)
                    turn_act(q, 1)

                trip(1)
                with pe.Fori(2, n) as q:
                    trip(q)
                down(n - 1, 1)

            @block.scalar
            def _(act):
                def keep_xT(s):
                    act.wait_ge(xT_made, s + 1)
                    wait(act, gu_made, s)
                    act.copy(xT[:, 0:4, :].rearrange("p k t -> p (k t)"), xb[0][:]).then_inc(xT_act, 1)

                def silu(s):
                    act.wait_ge(gu_made, s + 1)
                    wait(act, act_done, s)
                    act.activation(sg[:], gub[:, 0:FF], ACT.Silu).then_inc(silu_done, 1)

                def keep_y(q, b):
                    s = 2 * q + b
                    act.wait_ge(d_made, s + 1)
                    wait(act, y_out[b], 16 * q)
                    act.copy(y[:, b, 0:HALF], yb[2 * b][:]).then_inc(y_act, 1)

                n = trips(act)
                keep_xT(0)
                silu(0)
                keep_xT(1)
                silu(1)
                keep_xT(2)
                keep_y(0, 0)
                def trip(q):
                    silu(2 * q)
                    keep_xT(2 * q + 1)
                    keep_y(q - 1, 1)
                    silu(2 * q + 1)
                    keep_xT(2 * q + 2)
                    keep_y(q, 0)

                trip(1)
                with act.Fori(2, n) as q:
                    trip(q)
                keep_y(n - 1, 1)

            @block.vector
            def _(dve):
                def keep_xT(s):
                    dve.wait_ge(xT_made, s + 1)
                    wait(dve, gu_made, s)
                    dve.tensor_copy(xT[:, 4:8, :].rearrange("p k t -> p (k t)"), xb[1][:]).then_inc(xT_dve, 1)

                def act_mul(s):
                    dve.wait_ge(silu_done, s + 1)
                    wait(dve, aT_made, s)
                    dve.tensor_tensor(ac[:], sg[:], gub[:, FF:2 * FF], ALU.mult).then_inc(act_done, 1)

                def keep_aT(s):
                    dve.wait_ge(aT_made, s + 1)
                    wait(dve, d_made, s)
                    dve.tensor_copy(aT[:].rearrange("p k t -> p (k t)"), ab[:, 0:2 * P]).then_inc(aT_kept, 1)

                def keep_y(q, b):
                    s = 2 * q + b
                    dve.wait_ge(d_made, s + 1)
                    wait(dve, y_out[b], 16 * q)
                    dve.tensor_copy(y[:, b, HALF:], yb[2 * b + 1][:]).then_inc(y_dve, 1)

                n = trips(dve)
                keep_xT(0)
                act_mul(0)
                keep_xT(1)
                keep_aT(0)
                act_mul(1)
                keep_xT(2)
                keep_y(0, 0)
                keep_aT(1)
                def trip(q):
                    act_mul(2 * q)
                    keep_xT(2 * q + 1)
                    keep_y(q - 1, 1)
                    keep_aT(2 * q)
                    act_mul(2 * q + 1)
                    keep_xT(2 * q + 2)
                    keep_y(q, 0)
                    keep_aT(2 * q + 1)

                trip(1)
                with dve.Fori(2, n) as q:
                    trip(q)
                keep_y(n - 1, 1)


def combine(nc, ctx, y_dram, out, K, mem):
    sem = lambda n: ctx.enter_context(nc.semaphore(n))
    h1, rows, gates = K["h1"], K["rows"], K["gates"]
    R = 3
    yg = mem.put("y_rows", [P, R, TOP_K, D])
    f = mem.put("sum", [P, R, D])
    o = mem.put("normed", [P, R, D])
    stats = mem.put("ln2_stats", [P, NT, 12])
    mv = mem.put("ln2_mv", [P, NT, 2])
    std = mem.put("ln2_std", [P, NT, 4])
    y_in = [sem(f"y_in{b}") for b in range(R)]
    o_out = [sem(f"o_out{b}") for b in range(R)]
    y1_done, y2_done, f_done, stat, aggr, dev, inv, shift, xn, gain, bias_pool, bias_dve = (
        sem(f"ln2_{n}") for n in ("y1", "y2", "f", "stat", "aggr", "dev", "inv", "shift", "xn", "gain",
                                  "bias_pool", "bias_dve"))
    with nc.Block() as block:
        @block.sync
        def _(sp):
            def load(i):
                if i >= R:
                    sp.wait_ge(y2_done, i - R + 1)
                for k in range(TOP_K):
                    sp.dma_start(yg[:, i % R, k, :], y_dram[k * T + i * P:k * T + (i + 1) * P, :]
                                 ).then_inc(y_in[i % R], 16)

            for i in range(R):
                load(i)
            for i in range(NT):
                if i + R < NT:
                    load(i + R)
                sp.wait_ge(bias_pool, i + 1)
                sp.wait_ge(bias_dve, i + 1)
                sp.dma_start(out[i * P:(i + 1) * P, :], o[:, i % R, :]).then_inc(o_out[i % R], 16)
            for b in range(R):
                sp.wait_ge(o_out[b], 16 * len(range(b, NT, R)))

        @block.scalar
        def _(act):
            def first(i):
                act.wait_ge(y_in[i % R], 32 * (i // R + 1))
                if i >= R:
                    act.wait_ge(xn, i - R + 1)
                act.activation(f[:, i % R, :], yg[:, i % R, 0, :], ACT.Copy, scale=gates[:, 0, i:i + 1]).then_inc(y1_done, 1)

            first(0)
            for i in range(NT):
                if i + 1 < NT:
                    first(i + 1)
                act.wait_ge(aggr, i + 1)
                act.activation(std[:, i, 0:1], mv[:, i, 1:2], ACT.Sqrt, bias=LN_EPS).then_inc(dev, 1)
                act.wait_ge(shift, i + 1)
                if i >= R:
                    act.wait_ge(o_out[i % R], 16 * (i // R))
                act.activation(o[:, i % R, :], f[:, i % R, :], ACT.Identity, bias=std[:, i, 2:3],
                               scale=std[:, i, 1:2]).then_inc(xn, 1)

        @block.gpsimd
        def _(pool):
            for i in range(NT):
                b = i % R
                pool.wait_ge(xn, i + 1)
                pool.tensor_tensor(o[:, b, :], o[:, b, :], rows[:, 2, :], ALU.mult).then_inc(gain, 1)
                pool.wait_ge(gain, i + 1)
                pool.tensor_tensor(o[:, b, HALF:], o[:, b, HALF:], rows[:, 3, HALF:], ALU.add).then_inc(bias_pool, 1)

        @block.vector
        def _(dve):
            def add_bias(i):
                dve.wait_ge(gain, i + 1)
                dve.tensor_tensor(o[:, i % R, 0:HALF], o[:, i % R, 0:HALF], rows[:, 3, 0:HALF], ALU.add).then_inc(bias_dve, 1)

            for i in range(NT):
                b = i % R
                dve.wait_ge(y1_done, i + 1)
                dve.scalar_tensor_tensor(f[:, b, :], yg[:, b, 1, :], gates[:, 1, i:i + 1], f[:, b, :],
                                         ALU.mult, ALU.add).then_inc(y2_done, 1)
                dve.wait_ge(y2_done, i + 1)
                dve.scalar_tensor_tensor(f[:, b, :], h1[:, i, :], ALPHA, f[:, b, :], ALU.mult, ALU.add).then_inc(f_done, 1)
                dve.wait_ge(f_done, i + 1)
                for k in range(2):
                    dve.bn_stats(stats[:, i, 6 * k:6 * k + 6], f[:, b, k * HALF:(k + 1) * HALF]).then_inc(stat, 1)
                dve.wait_ge(stat, 2 * i + 2)
                dve.bn_aggr(mv[:, i, :], stats[:, i, :]).then_inc(aggr, 1)
                if i >= 2:
                    add_bias(i - 2)
                dve.wait_ge(dev, i + 1)
                dve.reciprocal(std[:, i, 1:2], std[:, i, 0:1]).then_inc(inv, 1)
                dve.wait_ge(inv, i + 1)
                dve.scalar_tensor_tensor(std[:, i, 2:3], mv[:, i, 0:1], -1.0, std[:, i, 1:2],
                                         ALU.mult, ALU.mult).then_inc(shift, 1)
            add_bias(NT - 2)
            add_bias(NT - 1)


def hybrid_decoder(nc, d, out, dbg=None, stop=None):
    h_dram = nc.dram_tensor("h_scratch", [T, D], F32).ap()
    toep_dram = nc.dram_tensor("toeplitz_scratch", [6, P, N_TOEPLITZ], F32).ap()
    h1_dram = nc.dram_tensor("h1_scratch", [T, D], F32).ap()
    y_dram = nc.dram_tensor("y_scratch", [SPARE_ROW + 1, D], F32).ap()
    qk_dram = nc.dram_tensor("qk_scratch", [N_CM - N_B, P, T], F32).ap()
    with ExitStack() as ctx:
        keep = Memory(nc, 17408)
        const_sb = keep.put("const_sb", [P, N_CONST])
        par_sb = keep.put("par_sb", [P, N_PC])
        mask_sb = keep.put("mask_sb", [P, (N_LEVELS + 1) * P], I32)

        def C(name, k=0, n=None):
            if name in CONST:
                at, width = CONST[name]
                return const_sb[:, at:at + width]
            at = PC[name][0] + k
            return par_sb[:, at:at + (n or 1)]

        early = keep.at
        v_tok = keep.put("v_tok", [P, NT, HALF])
        spent = keep.at
        pm = keep.put("mixed_channels", [P, N_B, T])
        R = {"AR": keep.put("ar", [P, 2, NT, 2, P]), "bt": keep.put("bt", [P, 2, T])}
        wv_at = keep.at
        R["bh"], R["kh"] = keep.put("bh", [P, 2, T]), keep.put("kh", [P, 2, T])
        R["wv"] = nc.alloc_sbuf_tensor_at("wv_sb", [P, ND, HALF], F32, offset=wv_at)
        gate_at = keep.at
        R["g"], R["bonus"] = keep.put("gate", [P, 2, T]), keep.put("bonus", [P, 2, T])
        R["PT"] = keep.put("chunk_decay", [P, 2, NCH])
        zone = keep.at
        hT = keep.put("hT", [P, ND, T])
        mixT = nc.alloc_sbuf_tensor_at("mixT", [P, ND, T], F32, offset=zone)
        work = keep.at
        for name, tile in (("bh_tok", 0), ("kh_tok", 5)):
            R[name] = nc.alloc_sbuf_tensor_at(name, [P, NT, 256], F32, offset=zone + tile * 4 * T)
        R["RT"] = nc.alloc_sbuf_tensor_at("r_total", [P, 2, 2, P], F32, offset=zone + 2 * 4 * T)
        R["S"] = nc.alloc_sbuf_tensor_at("state", [P, 2, 2, P], F32, offset=zone + 2 * 4 * T + 4 * 512)
        w_out = nc.alloc_sbuf_tensor_at("w_out", [P, ND, D], F32, offset=work)
        w_out_in = ctx.enter_context(nc.semaphore("w_out_in"))
        qk = nc.alloc_sbuf_tensor_at("qk_ahead", [P, 2, 2, T], F32, offset=spent)
        qk_in = [ctx.enter_context(nc.semaphore(f"qk_in{b}")) for b in range(2)]
        ar_at = spent + 4 * N_B * T
        H = {"x_sb": pm, "w_ring": nc.alloc_sbuf_tensor_at("w_ring", [P, 2, ND * P], F32, offset=work),
             "hb": nc.alloc_sbuf_tensor_at("h_rows", [P, 2, D], F32, offset=ar_at),
             "gb": nc.alloc_sbuf_tensor_at("ln0_rows", [P, 2, D], F32, offset=ar_at + 8 * D)}
        for name in ("xn_done", "rows_in"):
            H[name] = ctx.enter_context(nc.semaphore(name))
        H["w_in"] = [ctx.enter_context(nc.semaphore(f"w_in{b}")) for b in range(2)]
        after_ring = work + 8 * ND * P
        late = Memory(nc, early, zone)
        K = {"h1": late.put("h1", [P, NT, D]), "rows": late.put("ln_rows", [P, 4, D]),
             "gates": late.put("gates", [P, 2, NT]), "slots": late.put("slots", [P, 2, NT], I32),
             "plan": late.put("plan", [1, PLAN], I32), "ids": late.put("slot_ids", [P, SLOT_BLOCKS, 2], I32)}
        first = EXPERTS_AT
        step = (work + 4 * ND * D - first) // 8 * 4
        assert late.at < first and first + 4 * W_COLS <= zone and first + 2 * step + 4 * W_COLS <= 229344
        K["experts"] = bass.AP(nc.alloc_sbuf_tensor_at("expert_weights", [P, (2 * step) // 4 + W_COLS], F32, offset=first), 0,
                               [[(2 * step) // 4 + W_COLS, P], [step // 4, N_WBUF], [1, W_COLS]])
        K["experts_in"] = [ctx.enter_context(nc.semaphore(f"expert_in{b}")) for b in range(N_WBUF)]
        stages = {
            "normalise": lambda: normalise_input(
                nc, ctx, d["x"], d["ln_rows"], d["w_cm"], C,
                (const_sb, d["consts"], par_sb, d["params"], mask_sb, d["masks"]), pm, hT, H, Memory(nc, after_ring)),
            "project": lambda: project(nc, ctx, d["w_cm"], d["w_v"], d["up"], d["gate_up"], qk_dram, h_dram, C, hT,
                                       pm, v_tok, R, H, Memory(nc, after_ring)),
            "rwkv": lambda: rwkv(nc, ctx, qk_dram, qk, qk_in, C, mask_sb, pm, R, mixT, Memory(nc, work)),
            "attend": lambda: attend(nc, ctx, d["w_out"], w_out, w_out_in, qk_dram, toep_dram, d["rel_bias"], d["bucket_hot"], d["sinks"], C, mask_sb,
                                     v_tok, mixT, R, qk, qk_in, Memory(nc, spent, gate_at), Memory(nc, work + 4 * ND * D)),
            "route": lambda: mix_and_route(nc, ctx, d["w_gate_up"], d["w_down"], h_dram, h1_dram, d["ln_rows"][2:6, :], d["router_w"],
                                           d["router_bias"], d["route"], C, mixT, w_out, w_out_in, K,
                                           Memory(nc, late.at, first)),
            "experts": lambda: experts(nc, ctx, h1_dram, y_dram, d["w_gate_up"], d["w_down"], out, C, K,
                                       Memory(nc, late.at, first)),
            "combine": lambda: combine(nc, ctx, y_dram, out, K, Memory(nc, late.at)),
        }
        for name, stage in stages.items():
            stage()
            if stop == name:
                break
        if dbg is not None:
            dbg(nc, ctx, dict(hT=hT, pm=pm, ob=mixT[:, 3:5, :], v_tok=v_tok, mixT=mixT, par_sb=par_sb, h_dram=h_dram, qk_dram=qk_dram, h1_dram=h1_dram, **R, **K), out)


def lay_out(v):
    f = lambda a: np.ascontiguousarray(a, dtype=np.float32)
    v = {k: np.asarray(a) for k, a in v.items()}
    col = lambda a: a.reshape(-1, P).T
    w = v["w_in"][0]
    b0, c0 = A_COLS, A_COLS + B_COLS
    b_tiles = [w[:, b0 + 768:b0 + 896], w[:, b0 + 896:b0 + 1024]]
    mu = v["shift_mu"][0]
    mus = [mu[768:896], mu[896:1024]]
    for g in range(2):
        for kind in range(3):
            at = 256 * kind + P * g
            b_tiles.append(w[:, b0 + at:b0 + at + P])
            mus.append(mu[at:at + P])
    c_tiles = [w[:, c0 + P * t:c0 + P * (t + 1)] for t in range(6)]
    a_tiles = [np.concatenate([w[:, HD * j:HD * (j + 1)], w[:, HD * (j + 3):HD * (j + 4)]], axis=1) for j in range(3)]
    a_tiles.append(w[:, 384:512])
    tiles = np.stack(b_tiles + c_tiles + a_tiles)
    w_v = np.concatenate([w[:, c0 + 768:c0 + 1152], w[:, 512:640]], axis=1)
    o = v["w_out"][0]
    w_out = np.concatenate([o[HD * (j + 3 * e):HD * (j + 3 * e + 1)] for j in range(3) for e in range(2)] + [o[384:]])
    params = [col(v["ln0_g"]), col(v["ln0_b"]), np.stack(mus, axis=1)]
    params += [col(v[n][0].reshape(-1)) for n in ("decay_w0", "iclr_a0", "k_k", "k_a", "r_k", "lnx_g", "lnx_b")]
    params += [col(v["ln1_g"][0]), col(v["ln1_b"][0])]
    params = np.concatenate(params, axis=1)
    params = np.concatenate([params, np.zeros((P, N_PC - params.shape[1]), np.float32)], axis=1)
    return {
        "x": f(v["x"][0]),
        "consts": f(np.concatenate(list(constants().values()), axis=1)),
        "params": f(params),
        "masks": np.ascontiguousarray(level_masks()),
        "ln_rows": f(np.stack([v["ln0_g"], v["ln0_b"], v["ln1_g"][0], v["ln1_b"][0], v["ln2_g"][0], v["ln2_b"][0]])),
        "route": routing_constants(),
        "router_w": f(v["router_w"].reshape(ND, P, 16).transpose(1, 0, 2).reshape(P, ND * 16)),
        "router_bias": f(v["router_bias"][None, :]),
        "w_out": f(w_out.reshape(ND, P, D).transpose(1, 0, 2).reshape(P, ND * D)),
        "w_gate_up": f(np.concatenate([v["w_gate"][0], v["w_up"][0]], axis=2).reshape(N_EXPERTS, ND, P, 2 * FF)
                       .transpose(0, 2, 1, 3).reshape(N_EXPERTS, P, ND * 2 * FF)),
        "w_down": f(v["w_down"][0].reshape(N_EXPERTS, 2, P, D).transpose(0, 2, 1, 3).reshape(N_EXPERTS, P, 2 * D)),
        "w_cm": f(tiles.reshape(N_CM, ND, P, P).transpose(0, 2, 1, 3).reshape(N_CM, P, ND * P)),
        "w_v": f(w_v.reshape(ND, P, HALF).transpose(1, 0, 2)),
        "up": f(np.concatenate([v["decay_up"][0], v["iclr_up"][0]])),
        "gate_up": f(v["gate_up"][0]),
        "rel_bias": f(v["rel_bias"]),
        "bucket_hot": f(bias_constants()),
        "sinks": f(v["sinks"]),
    }


def kernel(**inputs):
    import concourse.bacc as bacc
    from concourse.bass_utils import run_bass_kernel_spmd

    nc = bacc.Bacc("TRN2", target_bir_lowering=False, num_devices=1)
    arrays = lay_out(inputs)
    d = {name: nc.dram_tensor(name, a.shape, mybir.dt.from_np(a.dtype), kind="ExternalInput").ap()
         for name, a in arrays.items()}
    out = nc.dram_tensor("result", (T, D), F32, kind="ExternalOutput").ap()
    hybrid_decoder(nc, d, out)
    done = run_bass_kernel_spmd(nc, [arrays], core_ids=[0])
    return done.results[0]["result"].reshape(1, T, D)
```

```python
from contextlib import ExitStack

import numpy as np

import concourse.bass as bass
from concourse import mybir

F32 = mybir.dt.float32
I32 = mybir.dt.int32
F32R = mybir.dt.float32r
U32 = mybir.dt.uint32
ALU = mybir.AluOpType
ACT = mybir.ActivationFunctionType
AX = mybir.AxisListType.X

P = 128
T = 1024
D = 1024
NT, ND = T // P, D // P
HALF = 512
HD = 64
CH = 64
NCH = T // CH
A_COLS, B_COLS, C_COLS = 640, 1024, 1152
LN_EPS, GN_EPS = 1e-5, 64e-5
DECAY_SCALE = float(np.exp(-0.5))
ALPHA = 2 ** 0.25

XWXA, XG, R0, K0, V0, R1, K1, V1 = range(8)
N_SPLIT = 7
N_B = 8
N_CM = 18
K_TILES = (3, 4, 5, 9)
N_BUCKETS, MAX_EXACT, MAX_DISTANCE, WINDOW = 32, 16, 128, 128
N_TOEPLITZ = 384
NEG = -1e30
CLAMP = 30.0

PC = {}
for _name, _n in (("ln0_g", 8), ("ln0_b", 8), ("mu", 8), ("w0", 2), ("a0", 2), ("k_k", 2), ("k_a", 2),
                  ("r_k", 2), ("lnx_g", 2), ("lnx_b", 2), ("ln1_g", 8), ("ln1_b", 8)):
    PC[_name] = sum(n for _, n in PC.values()), _n
N_PC = 56


def constants():
    i, j = np.arange(P)[:, None], np.arange(P)[None, :]
    same = (i // CH) == (j // CH)
    c = {
        "ident": i == j,
        "head_ones": same,
        "head_mean": same / HD,
        "level0": (i // 2 == j // 2) & (i % 2 == 0) & (j % 2 == 1),
        "suffix": -1.0 * (i >= j),
        "all_later": -np.ones((P, P)),
        "key_before": i < j,
        "ones": np.ones((P, P)),
    }
    s = np.arange(P)[:, None]
    cols = np.arange(512)
    chunk, kind, t = (cols // 64) % 2, (cols // 128) % 2, cols % 64
    c["chunk_mask"] = (s // CH == chunk) & ((s % CH < t) | ((kind == 1) & (s % CH == t)))
    return c


def bias_constants():
    dist = 255 - np.arange(N_TOEPLITZ)
    inside = (dist >= 0) & (dist < WINDOW)
    d = np.maximum(dist, 1).astype(np.float32)
    large = MAX_EXACT + (np.log(d / MAX_EXACT) / np.float32(np.log(MAX_DISTANCE / MAX_EXACT))
                         * (N_BUCKETS - MAX_EXACT)).astype(np.int32)
    bucket = np.where(dist < MAX_EXACT, dist, np.minimum(large, N_BUCKETS - 1))
    hot = (np.arange(N_BUCKETS)[:, None] == bucket[None, :]) & inside[None, :]
    outside = np.broadcast_to(np.where(inside, 0.0, NEG), (N_BUCKETS, N_TOEPLITZ))
    return np.concatenate([hot, outside], axis=1)


CONST = {}
_at = 0
for _name, _m in constants().items():
    CONST[_name] = (_at, _m.shape[1])
    _at += _m.shape[1]
N_CONST = _at


def level_masks():
    i, j = np.arange(P)[:, None], np.arange(P)[None, :]
    out = []
    for m in (2, 4, 8, 16, 32):
        out.append((i // (2 * m) == j // (2 * m)) & ((i // m) % 2 == 0) & ((j // m) % 2 == 1))
    out.append(i >= j)
    return np.concatenate(out, axis=1).astype(np.int32)


N_LEVELS = 5


class Memory:

    def __init__(self, nc, start, end=229344):
        self.nc, self.at, self.end = nc, start, end

    def put(self, name, shape, dtype=F32):
        t = self.nc.alloc_sbuf_tensor_at(name, shape, dtype, offset=self.at)
        size = 4 * int(np.prod(shape[1:]))
        self.at += -(-size // 32) * 32
        assert self.at <= self.end, (name, self.at)
        return t


def bcast(ap, *dims):
    return bass.AP(ap.tensor, ap.offset, [list(ap.ap[0])] + [list(d) for d in dims])


def split_w_high(act, t, H, tiles=ND):
    n = tiles * P
    act.copy(H["w_hi"][:, t % 2, 0:n], H["w_ring"][:, t % 2, 0:n]).then_inc(H["w_hi_made"], 1)


def split_w_low(eng, t, H, tiles=ND):
    b, n = t % 2, tiles * P
    eng.wait_ge(H["w_hi_made"], t + 1)
    eng.tensor_tensor(H["w_lo"][:, b, 0:n], H["w_ring"][:, b, 0:n], H["w_hi"][:, b, 0:n].bitcast(F32),
                      ALU.subtract).then_inc(H["w_lo_made"], 1)


def split_h_high(act, half, hT, H):
    for d in range(ND):
        hs = slice(half * HALF, (half + 1) * HALF)
        act.copy(H["hT_hi"][:, d, hs], hT[:, d, hs]).then_inc(H["h_hi"], 1)


def split_h_low(dve, half, hT, H):
    for d in range(ND):
        hs = slice(half * HALF, (half + 1) * HALF)
        dve.wait_ge(H["h_hi"], half * ND + d + 1)
        dve.tensor_tensor(H["hT_lo"][:, d, hs], hT[:, d, hs], H["hT_hi"][:, d, hs].bitcast(F32),
                          ALU.subtract).then_inc(H["h_lo"], 1)


def normalise_input(nc, ctx, x, ln_rows, w_cm, C, params, x_sb, hT, H, mem):
    sem = lambda n: ctx.enter_context(nc.semaphore(n))
    gb = H["gb"]
    stats = mem.put("ln0_stats", [P, NT, 12])
    mv = mem.put("ln0_mv", [P, NT, 2])
    std = mem.put("ln0_std", [P, NT])
    rstd = mem.put("ln0_rstd", [P, NT])
    x_in = [sem(f"x_in{i}") for i in range(NT // 2)]
    const_in = sem("const_in")
    stat, aggr, std_done, rstd_done = sem("ln0_stat"), sem("ln0_aggr"), sem("ln0_std"), sem("ln0_rstd")
    xT_done, hT_done = sem("xT_done"), sem("hT_done")
    xn_done, rows_in, w_in = H["xn_done"], H["rows_in"], H["w_in"]
    const_sb, const_d, par_sb, par_d, mask_sb, mask_d = params
    with ExitStack() as inner:
        bank = [inner.enter_context(nc.psum_tensor(f"xT{d}", [P, HALF], F32)) for d in range(ND)]
        with nc.Block() as block:
            @block.sync
            def _(sp):
                for i in range(NT):
                    sp.dma_start(x_sb[:, i, :], x[i * P:(i + 1) * P, :]).then_inc(x_in[i // 2], 16)
                for t in range(2):
                    sp.dma_start(H["w_ring"][:, t, :], w_cm[t]).then_inc(w_in[t], 16)

            @block.scalar
            def _(act):
                act.dma_start(const_sb[:], const_d).then_inc(const_in, 16)
                act.dma_start(par_sb[:], par_d).then_inc(const_in, 16)
                act.dma_start(mask_sb[:], mask_d).then_inc(const_in, 16)
                for k in range(2):
                    act.dma_start(gb[:, k, :], ln_rows[k:k + 1, :].to_broadcast([P, D])).then_inc(rows_in, 16)
                act.wait_ge(const_in, 48)
                def deviation(half):
                    i0 = 4 * half
                    act.wait_ge(aggr, i0 + 4)
                    act.activation(std[:, i0:i0 + 4], mv[:, i0:i0 + 4, 1], ACT.Sqrt, bias=LN_EPS).then_inc(std_done, 1)

                def keep_h(half):
                    for d in range(ND):
                        act.wait_ge(xT_done, half * ND + d + 1)
                        act.activation(hT[:, d, half * HALF:(half + 1) * HALF], bank[d][:], ACT.Identity,
                                       bias=C("ln0_b", d), scale=C("ln0_g", d)).then_inc(hT_done, 1)

                deviation(0)
                keep_h(0)
                deviation(1)
                for t in range(2):
                    act.wait_ge(w_in[t], 16)
                    split_w_high(act, t, H)
                act.wait_ge(hT_done, ND)
                split_h_high(act, 0, hT, H)
                keep_h(1)

            @block.vector
            def _(dve):
                for half in range(2):
                    for i in range(4 * half, 4 * half + 4):
                        dve.wait_ge(x_in[i // 2], 32)
                        for k in range(2):
                            dve.bn_stats(stats[:, i, 6 * k:6 * k + 6],
                                         x_sb[:, i, k * HALF:(k + 1) * HALF]).then_inc(stat, 1)
                        dve.wait_ge(stat, 2 * i + 2)
                        dve.bn_aggr(mv[:, i, :], stats[:, i, :]).then_inc(aggr, 1)
                    dve.wait_ge(std_done, half + 1)
                    dve.reciprocal(rstd[:, 4 * half:4 * half + 4], std[:, 4 * half:4 * half + 4]).then_inc(rstd_done, 1)
                    dve.wait_ge(rstd_done, half + 1)
                    for i in range(4 * half, 4 * half + 4):
                        dve.tensor_scalar(x_sb[:, i, :], x_sb[:, i, :], mv[:, i, 0:1], rstd[:, i:i + 1],
                                          ALU.subtract, ALU.mult).then_inc(xn_done, 1)
                for t in range(2):
                    split_w_low(dve, t, H)
                split_h_low(dve, 0, hT, H)

            @block.tensor
            def _(pe):
                pe.wait_ge(const_in, 48)
                for half in range(2):
                    pe.wait_ge(xn_done, 4 * half + 4)
                    for d in range(ND):
                        if half:
                            pe.wait_ge(hT_done, d + 1)
                        for j in range(4):
                            mm = pe.transpose(bank[d][:, j * P:(j + 1) * P],
                                              x_sb[:, 4 * half + j, d * P:(d + 1) * P], C("ident"))
                        mm.then_inc(xT_done, 1)


PREP = ["scan", "kk", "kk2", "norm0", "norm1", "kfac", "knew", "rk", "recip", "kkn", "bonus0", "bonus1",
        "at", "rt", "ba", "bt", "kt", "pt", "bh", "kh"]


def prep_at(g, name):
    return 1 + g * len(PREP) + PREP.index(name) + 1


def project(nc, ctx, w_cm, w_v, up_d, gate_d, qk_dram, h_dram, C, hT, pm, v_tok, R, H, mem, mem2):
    sem = lambda n: ctx.enter_context(nc.semaphore(n))
    AR, bt, bh, kh, gT, PT, bonus = (R[n] for n in ("AR", "bt", "bh", "kh", "g", "PT", "bonus"))
    wv_sb = R["wv"]
    w_ring, w_hi, w_lo, hb, gb, x_sb, hT_hi, hT_lo = (
        H[n] for n in ("w_ring", "w_hi", "w_lo", "hb", "gb", "x_sb", "hT_hi", "hT_lo"))
    wv_hi, wv_lo = R["wv_hi"], R["wv_lo"]
    one_minus_ka = mem.put("one_minus_ka", [P, 8])
    praw = mem.put("praw", [P, T + 8])
    diff = mem.put("diff", [P, T])
    Pe = nc.alloc_sbuf_tensor_at("decay", [P, NCH, CH + 1], F32, offset=mem.at)
    assert mem.at + 4 * NCH * (CH + 1) <= mem.end
    up_sb = mem.put("up_sb", [P, 256])
    gate_sb = mem.put("gate_sb", [P, 256])
    aT = bt
    lw = [AR[:, g, 0:NT // 2, :, :].rearrange("p i a t -> p (i a t)") for g in range(2)]
    stage = mem2.put("qk_stage", [P, 2, HALF])
    kk = nc.alloc_sbuf_tensor_at("kk", [P, T], F32, offset=R["bh_at"] + 4 * T)
    tmp = nc.alloc_sbuf_tensor_at("prep_tmp", [P, T], F32, offset=R["kh_at"] + 4 * T)
    scan_mask = nc.alloc_sbuf_tensor_at("scan_mask", [P, NCH, CH], F32, offset=R["ar_at"] + 12 * T)
    w_hi_made, w_lo_made, wv_split, restored = H["w_hi_made"], H["w_lo_made"], sem("wv_split"), sem("h_restored")
    Pinv, rn = praw, diff
    w_in = H["w_in"]
    h_step, h_out = sem("h_step"), [sem("h_out0"), sem("h_out1")]
    wv_in, up_in = sem("wv_in"), sem("up_in")
    proj_done, proj_out = sem("proj_done"), sem("proj_out")
    v_done, v_out = sem("v_done"), sem("v_out")
    prepared, mix_diff, mixed = sem("prep_consts"), sem("mix_diff"), sem("mixed")
    stored = H["qk_stored"]
    squashed = sem("squashed")
    lora_done, lora_out = sem("lora_done"), sem("lora_out")
    prep, exp_done, sqrt_done = sem("prep"), sem("exp_done"), sem("sqrt_done")
    head_sum = sem("head_sum")
    per_chunk = lambda ap: ap.rearrange("p (c t) -> p c t", c=NCH)
    per_tile = lambda ap: ap.rearrange("p (i c t) -> p i c t", i=NT, c=2)
    by_tile = lambda ap: ap.rearrange("p i (c t) -> p i c t", c=2)
    split = lambda ap: ap.rearrange("p (i c) t -> p i c t", c=2)

    with ExitStack() as inner:
        pb = [inner.enter_context(nc.psum_tensor(f"proj{b}", [P, HALF], F32)) for b in range(6)]
        sb = [inner.enter_context(nc.psum_tensor(f"small{b}", [P, HALF], F32)) for b in range(2)]
        with nc.Block() as block:
            @block.sync
            def _(sp):
                sp.dma_start(up_sb[:], up_d).then_inc(up_in, 16)
                sp.dma_start(gate_sb[:], gate_d).then_inc(up_in, 16)

                def store(u):
                    for half in range(2):
                        sp.wait_ge(proj_out, 2 * (N_B + u) + half + 1)
                        sp.dma_start(qk_dram[u][:, half * HALF:(half + 1) * HALF], stage[:, half, :]).then_inc(stored[half], 16)

                def store_h(i):
                    sp.wait_ge(h_step, 2 * (i + 1))
                    sp.dma_start(h_dram[i * P:(i + 1) * P, :], hb[:, i % 2, :]).then_inc(h_out[i % 2], 16)

                for i in range(2):
                    store_h(i)
                for t in range(2, N_CM):
                    sp.wait_ge(proj_done, 2 * (t - 1))
                    sp.dma_start(w_ring[:, t % 2, :], w_cm[t]).then_inc(w_in[t % 2], 16)
                    for i in {2: (2, 3, 4), 3: (5, 6), 4: (7,)}.get(t, ()):
                        store_h(i)
                    if t == 3:
                        sp.dma_start(wv_sb[:], w_v).then_inc(wv_in, 16)
                    if t >= N_B + 2:
                        store(t - N_B - 2)
                store(N_CM - N_B - 2)
                store(N_CM - N_B - 1)

            @block.gpsimd
            def _(pool):
                pool.wait_ge(H["rows_in"], 32)
                for i in range(NT):
                    pool.wait_ge(H["xn_done"], i + 1)
                    if i >= 2:
                        pool.wait_ge(h_out[i % 2], 16 * (i // 2))
                    pool.tensor_tensor(hb[:, i % 2, :], x_sb[:, i, :], gb[:, 0, :], ALU.mult).then_inc(h_step, 1)
                    pool.wait_ge(h_step, 2 * i + 1)
                    pool.tensor_tensor(hb[:, i % 2, :], hb[:, i % 2, :], gb[:, 1, :], ALU.add).then_inc(h_step, 1)
                for t in range(N_B, N_CM):
                    pool.wait_ge(w_hi_made, t + 1)
                    pool.wait_ge(w_lo_made, t)
                    split_w_low(pool, t, H, N_SPLIT)

            @block.tensor
            def _(pe):
                def tile(t):
                    pe.wait_ge(w_hi_made, t + 1)
                    pe.wait_ge(w_lo_made, t + 1)
                    parts = [(w_hi, hT_hi), (w_hi, hT_lo), (w_lo, hT_hi)]
                    if t < N_B:
                        terms = [parts] * ND
                    else:
                        pe.wait_ge(w_in[t % 2], 16 * (t // 2 + 1))
                        terms = [parts] * N_SPLIT + [[(w_ring, hT)]] * (ND - N_SPLIT)
                    for half in range(2):
                        n = 2 * t + half
                        if t == 0:
                            pe.wait_ge(H["h_lo"], ND * (half + 1))
                        if n >= 6:
                            pe.wait_ge(proj_out, n - 5)
                        for d in range(ND):
                            if t == N_B and half == 0 and d == N_SPLIT:
                                pe.wait_ge(restored, ND - N_SPLIT)
                            for k, (w, h) in enumerate(terms[d]):
                                mm = pe.matmul(pb[n % 6][:], w[:, t % 2, d * P:(d + 1) * P],
                                               h[:, d, half * HALF:(half + 1) * HALF],
                                               start=d == 0 and k == 0, stop=d == ND - 1 and k == len(terms[d]) - 1)
                        mm.then_inc(proj_done, 1)

                def head_sums(g, what, first):
                    pe.wait_ge(prep, prep_at(g, what))
                    for half in range(2):
                        if what == "rk":
                            pe.wait_ge(prep, prep_at(g, f"norm{half}"))
                        elif g:
                            pe.wait_ge(prep, prep_at(g - 1, f"bonus{half}"))
                        else:
                            pe.wait_ge(lora_out, 12)
                        pe.matmul(sb[half][:], C("head_ones"), tmp[:, half * HALF:(half + 1) * HALF],
                                  start=True, stop=True).then_inc(head_sum, 1)

                for t in range(N_B):
                    tile(t)
                pe.wait_ge(wv_split, 2)
                for i in range(NT):
                    if i < 2:
                        pe.wait_ge(proj_out, 2 * N_B)
                    else:
                        pe.wait_ge(v_out, i - 1)
                    for d in range(ND):
                        for k, (h, w) in enumerate(((hT_hi, wv_hi), (hT_hi, wv_lo), (hT_lo, wv_hi))):
                            mm = pe.matmul(pb[4 + i % 2][:], h[:, d, i * P:(i + 1) * P], w[:, d, :],
                                           start=d == 0 and k == 0, stop=d == ND - 1 and k == 2)
                    mm.then_inc(v_done, 1)
                pe.wait_ge(up_in, 32)
                pe.wait_ge(squashed, 2)
                n = 0
                for g in range(2):
                    cols = slice(g * P, (g + 1) * P)
                    for half in range(2):
                        hs = slice(half * HALF, (half + 1) * HALF)
                        for lhsT, rhs in ((up_sb[0:64, cols], pm[0:64, XWXA, hs]),
                                          (up_sb[64:128, cols], pm[64:128, XWXA, hs]),
                                          (gate_sb[:, cols], pm[:, XG, hs])):
                            if n >= 2:
                                pe.wait_ge(lora_out, n - 1)
                            pe.matmul(sb[n % 2][:], lhsT, rhs, start=True, stop=True).then_inc(lora_done, 1)
                            n += 1
                pe.wait_ge(v_out, NT)
                for t in range(N_B, N_CM):
                    tile(t)
                    if t in (8, 12):
                        head_sums((t - 8) // 4, "kk2", 0)
                    if t in (10, 14):
                        head_sums((t - 10) // 4, "rk", 0)

            @block.scalar
            def _(act):
                def copy_out(t):
                    for half in range(2):
                        n = 2 * t + half
                        act.wait_ge(proj_done, n + 1)
                        if t < N_B:
                            dst = praw[:, 1 + half * HALF:1 + (half + 1) * HALF]
                            if t and half == 0:
                                act.wait_ge(mixed, t)
                        else:
                            u = t - N_B
                            dst = stage[:, half, :]
                            if u:
                                act.wait_ge(stored[half], 16 * u)
                        if t < N_B or t - N_B in K_TILES:
                            act.copy(dst, pb[n % 6][:]).then_inc(proj_out, 1)
                        else:
                            act.mul(dst, pb[n % 6][:], HD ** -0.5).then_inc(proj_out, 1)

                def decay_factors(g):
                    act.wait_ge(prep, prep_at(g, "scan"))
                    if g:
                        act.wait_ge(prep, prep_at(g - 1, "kh"))
                    else:
                        act.wait_ge(mixed, N_B)
                    act.activation(Pe[:, :, 1:], per_chunk(lw[g]), ACT.Exp, scale=-DECAY_SCALE).then_inc(exp_done, 1)
                    act.activation(Pinv[:, 0:T], lw[g], ACT.Exp, scale=DECAY_SCALE).then_inc(exp_done, 1)

                def norm(g):
                    act.wait_ge(prep, prep_at(g, "norm1"))
                    act.activation(rn[:], rn[:], ACT.Sqrt).then_inc(sqrt_done, 1)

                def next_high(t):
                    act.wait_ge(w_in[t % 2], 16 * (t // 2 + 2))
                    act.wait_ge(proj_done, 2 * (t + 1))
                    split_w_high(act, t + 2, H, ND if t + 2 < N_B else N_SPLIT)

                split_h_high(act, 1, hT, H)
                for t in range(N_B):
                    copy_out(t)
                    next_high(t)
                    if t == 5:
                        act.wait_ge(wv_in, 16)
                        for b in range(2):
                            act.wait_ge(h_out[b], 16 * NT // 2)
                        act.copy(wv_hi[:].rearrange("p k d -> p (k d)"),
                                 wv_sb[:].rearrange("p k d -> p (k d)")).then_inc(wv_split, 1)
                    if t == 2:
                        act.wait_ge(mixed, 2)
                        act.activation(pm[0:64, XWXA, :], pm[0:64, XWXA, :], ACT.Tanh).then_inc(squashed, 1)
                        act.activation(pm[:, XG, :], pm[:, XG, :], ACT.Sigmoid).then_inc(squashed, 1)
                for i in range(NT):
                    act.wait_ge(v_done, i + 1)
                    act.copy(v_tok[:, i, :], pb[4 + i % 2][:]).then_inc(v_out, 1)
                n = 0
                for g in range(2):
                    for half in range(2):
                        hs = slice(half * HALF, (half + 1) * HALF)
                        for k in range(3):
                            act.wait_ge(lora_done, n + 1)
                            if k == 0:
                                act.activation(lw[g][:, hs], sb[n % 2][:], ACT.Sigmoid, bias=C("w0", g)).then_inc(lora_out, 1)
                            elif k == 1:
                                act.activation(aT[:, g, hs], sb[n % 2][:], ACT.Sigmoid, bias=C("a0", g)).then_inc(lora_out, 1)
                            else:
                                act.copy(gT[:, g, hs], sb[n % 2][:]).then_inc(lora_out, 1)
                            n += 1
                decay_factors(0)
                for t in range(N_B, N_CM):
                    copy_out(t)
                    if t + 2 < N_CM:
                        next_high(t)
                    if t in (8, 12):
                        norm((t - 8) // 4)
                    if t == 11:
                        decay_factors(1)

            @block.vector
            def _(dve):
                dve.memset(praw[:, 0:1], 0.0).then_inc(prepared, 1)
                dve.tensor_scalar(one_minus_ka[:, 0:2], C("k_a", 0, 2), -1.0, 1.0, ALU.mult, ALU.add).then_inc(prepared, 1)
                dve.wait_ge(prepared, 2)

                split_h_low(dve, 1, hT, H)
                for t in range(N_B):
                    if 0 < t < N_B - 1:
                        split_w_low(dve, t + 1, H)
                    if t == 6:
                        dve.wait_ge(wv_split, 1)
                        dve.tensor_tensor(wv_lo[:], wv_sb[:], wv_hi[:].bitcast(F32), ALU.subtract).then_inc(wv_split, 1)
                    dve.wait_ge(proj_out, 2 * t + 2)
                    dve.tensor_tensor(diff[:], praw[:, 0:T], praw[:, 1:T + 1], ALU.subtract).then_inc(mix_diff, 1)
                    dve.wait_ge(mix_diff, t + 1)
                    dve.wait_ge(h_step, 2 * t + 1)
                    dve.scalar_tensor_tensor(pm[:, t, :], diff[:], C("mu", t), praw[:, 1:T + 1],
                                             ALU.mult, ALU.add).then_inc(mixed, 1)
                dve.wait_ge(mixed, N_B)
                dve.wait_ge(v_done, NT)
                for d in range(N_SPLIT, ND):
                    dve.tensor_tensor(hT[:, d, :], hT_lo[:, d, :].bitcast(F32), hT_hi[:, d, :].bitcast(F32), ALU.add).then_inc(restored, 1)
                dve.wait_ge(restored, ND - N_SPLIT)
                dve.memset(scan_mask[:], 1.0).then_inc(prepared, 1)
                dve.wait_ge(prepared, 3)
                dve.memset(scan_mask[:, :, 0:1], 0.0).then_inc(prepared, 1)
                dve.wait_ge(prepared, 4)
                dve.nop().then_inc(prep, 1)
                for g in range(2):
                    r, k, v = (pm[:, (R0, K0, V0)[j] if g == 0 else (R1, K1, V1)[j], :] for j in range(3))
                    after = lambda name: dve.wait_ge(prep, prep_at(g, name))
                    at_PT = bass.AP(PT, 0, [list(PT[:].ap[0]), [1, NCH], [0, CH]]) if g == 0 else \
                        bass.AP(PT, NCH, [list(PT[:].ap[0]), [1, NCH], [0, CH]])
                    dve.wait_ge(lora_out, 6 * (g + 1))
                    dve.tensor_tensor_scan(lw[g], scan_mask[:].rearrange("p c t -> p (c t)"), lw[g],
                                           0.0, ALU.mult, ALU.add).then_inc(prep, 1)
                    dve.tensor_scalar(kk[:], k, C("k_k", g), None, ALU.mult).then_inc(prep, 1)
                    after("kk")
                    dve.tensor_tensor(tmp[:], kk[:], kk[:], ALU.mult).then_inc(prep, 1)
                    for half in range(2):
                        dve.wait_ge(head_sum, 4 * g + half + 1)
                        dve.tensor_scalar(rn[:, half * HALF:(half + 1) * HALF], sb[half][:], 1e-24, None,
                                          ALU.max).then_inc(prep, 1)
                    dve.tensor_scalar(tmp[:], aT[:, g, :], C("k_a", g), one_minus_ka[:, g:g + 1],
                                      ALU.mult, ALU.add).then_inc(prep, 1)
                    after("kfac")
                    dve.tensor_tensor(k, k, tmp[:], ALU.mult).then_inc(prep, 1)
                    after("knew")
                    dve.scalar_tensor_tensor(tmp[:], r, C("r_k", g), k, ALU.mult, ALU.mult).then_inc(prep, 1)
                    dve.wait_ge(sqrt_done, g + 1)
                    dve.reciprocal(rn[:], rn[:]).then_inc(prep, 1)
                    after("recip")
                    dve.scalar_tensor_tensor(kk[:], kk[:], -1.0, rn[:], ALU.mult, ALU.mult).then_inc(prep, 1)
                    for half in range(2):
                        hs = slice(half * HALF, (half + 1) * HALF)
                        dve.wait_ge(head_sum, 4 * g + 2 + half + 1)
                        dve.tensor_tensor(bonus[:, g, hs], sb[half][:], v[:, hs], ALU.mult).then_inc(prep, 1)
                    dve.wait_ge(exp_done, 2 * g + 2)
                    after("kkn")
                    if g == 0:
                        for s in h_out:
                            dve.wait_ge(s, 16 * NT // 2)
                        dve.memset(Pe[:, :, 0:1], 1.0).then_inc(prepared, 1)
                        dve.wait_ge(prepared, 5)
                    dve.tensor_tensor(by_tile(AR[:, g, :, 0, :]), per_tile(kk[:]), split(Pe[:, :, 0:CH]), ALU.mult).then_inc(prep, 1)
                    dve.tensor_tensor(by_tile(AR[:, g, :, 1, :]), per_tile(r), split(Pe[:, :, 1:]), ALU.mult).then_inc(prep, 1)
                    dve.scalar_tensor_tensor(tmp[:], kk[:], -1.0, aT[:, g, :], ALU.mult, ALU.mult).then_inc(prep, 1)
                    after("ba")
                    dve.tensor_tensor(bt[:, g, :], tmp[:], Pinv[:, 0:T], ALU.mult).then_inc(prep, 1)
                    dve.tensor_tensor(k, k, Pinv[:, 0:T], ALU.mult).then_inc(prep, 1)
                    dve.tensor_copy(PT[:, g, :], Pe[:, :, CH]).then_inc(prep, 1)
                    dve.wait_ge(v_done, NT)
                    after("pt")
                    dve.tensor_tensor(per_chunk(bh[:, g, :]), per_chunk(bt[:, g, :]), at_PT, ALU.mult).then_inc(prep, 1)
                    dve.tensor_tensor(per_chunk(kh[:, g, :]), per_chunk(k), at_PT, ALU.mult).then_inc(prep, 1)


TURNS = [x for level in range(1, N_LEVELS + 1) for x in (f"T{level}", f"Y{level}", f"X{level}")][:-1]
MADE = ["turn", "A0", "A1", "A2", "A3", "AV", "X0", *TURNS, "GU", "RT", "MT"]
TILE = [*MADE, "Y", "C0", "C1"]


def in_order():
    behind = 3.5
    return [x for _, *x in sorted((i // 2 * len(TILE) + k + behind * (i % 2), name, i % 2, i)
                                  for i in range(NT) for k, name in enumerate(TILE))]


KEPT_ACT = ["a_tok", "bh_tok", "X0", *[x for x in TURNS if x[0] != "Y"], "GU"]
KEPT_DVE = ["kh_tok", "v_tok", "A0", "A1", "A2", "A3", "level0", "XT0", "AV",
            *[x for x in TURNS if x[0] == "Y"], "RT", "MT0", "MT1", "MT2", "MT3"]


def upto(steps, n, name):
    return n * len(steps) + steps.index(name) + 1


def rwkv(nc, ctx, qk_dram, stored, qk, qk_in, C, masks, pm, R, mixT, mem):
    sem = lambda n: ctx.enter_context(nc.semaphore(n))
    AR, bt, bh, kh, gT, PT, bonus = (R[n] for n in ("AR", "bt", "bh", "kh", "g", "PT", "bonus"))
    XR = mem.put("x_rhs", [P, NT, 4, 2, HD])
    bh_tok = R["bh_tok"]
    kh_tok = R["kh_tok"]
    v_tok = mem.put("vb_tok", [P, NT, 256])
    Am = mem.put("chunk_products", [P, 2, 4, 512])
    XT = mem.put("inverse_T", [P, 2, 4, P])
    X = mem.put("inverse", [P, 2, 4, P])
    Tm = mem.put("inverse_step", [P, 2, 4, P])
    GU = mem.put("gu", [P, 2, 2, 4, HD])
    RT, S = R["RT"], R["S"]
    MT = mem.put("state_map", [P, 2, 4, P])
    made = [sem("made0"), sem("made1")]
    kept_act = [sem("kept_act0"), sem("kept_act1")]
    kept_dve = [sem("kept_dve0"), sem("kept_dve1")]
    z_done, s_done, y_done, y_out = sem("z_done"), sem("s_done"), sem("y_done"), sem("y_out")

    def cols4(ap):
        return ap.rearrange("p (h t) -> p h t", h=4)

    def part(st, hh, kind, ar):
        at = kind * 256 + ar * P
        return Am[:, st, hh, at:at + P]

    with ExitStack() as inner:
        bank = [inner.enter_context(nc.psum_tensor(f"rw{b}", [P, HALF], F32)) for b in range(8)]
        ybank, zbank = bank[6], bank[7]
        with nc.Block() as block:
            @block.sync
            def _(sp):
                for s in stored:
                    sp.wait_ge(s, 16 * (N_CM - N_B))
                for k in range(2):
                    sp.dma_start(qk[:, 0, k, :], qk_dram[3 * k]).then_inc(qk_in[0], 16)

            @block.tensor
            def _(pe):
                def step(name, st, i):
                    n = i // 2
                    B = bank[3 * st:3 * st + 3]
                    act_has = lambda x: pe.wait_ge(kept_act[st], upto(KEPT_ACT, n, x))
                    dve_has = lambda x: pe.wait_ge(kept_dve[st], upto(KEPT_DVE, n, x))
                    ts = slice(i * P, (i + 1) * P)
                    if name == "turn":
                        if n:
                            pe.wait_ge(kept_dve[st], n * len(KEPT_DVE))
                        for g in range(2):
                            pe.transpose(B[0][:, g * P:(g + 1) * P], AR[:, g, i, 0, :], C("ident"))
                            pe.transpose(B[0][:, (2 + g) * P:(3 + g) * P], bh[:, g, ts], C("ident"))
                            pe.transpose(B[1][:, g * P:(g + 1) * P], kh[:, g, ts], C("ident"))
                            mm = pe.transpose(B[1][:, (2 + g) * P:(3 + g) * P], pm[:, (V0, V1)[g], ts], C("ident"))
                    elif name[0] == "A" and name != "AV":
                        hh = int(name[1])
                        g, e = hh // 2, hh % 2
                        if hh == 0:
                            act_has("bh_tok")
                        elif hh == 1:
                            dve_has("v_tok")
                        elif hh == 3:
                            dve_has("A0")
                        ar = AR[e * HD:(e + 1) * HD, g, i, :, :].rearrange("p a t -> p (a t)")
                        dst = B[hh % 3]
                        pe.matmul(dst[:, 0:256], pm[e * HD:(e + 1) * HD, (K0, K1)[g], ts], ar, start=True, stop=True)
                        mm = pe.matmul(dst[:, 256:512], bt[e * HD:(e + 1) * HD, g, ts], ar, start=True, stop=True)
                    elif name == "AV":
                        dve_has("A3")
                        for hh in range(4):
                            mm = pe.matmul(B[1][:, hh * HD:(hh + 1) * HD], part(st, hh, 0, 0),
                                           v_tok[:, i, hh * HD:(hh + 1) * HD], start=True, stop=True)
                    elif name[0] == "X":
                        dve_has("XT0" if name == "X0" else f"Y{name[1]}")
                        for hh in range(4):
                            mm = pe.transpose(B[0][:, hh * P:(hh + 1) * P], XT[:, st, hh, :], C("ident"))
                    elif name[0] == "T":
                        act_has(f"X{int(name[1]) - 1}")
                        if name == "T1":
                            dve_has("AV")
                        for hh in range(4):
                            mm = pe.matmul(B[1][:, hh * P:(hh + 1) * P], part(st, hh, 1, 0), X[:, st, hh, :],
                                           start=True, stop=True)
                    elif name[0] == "Y":
                        act_has(f"T{name[1]}")
                        for hh in range(4):
                            mm = pe.matmul(B[2][:, hh * P:(hh + 1) * P], Tm[:, st, hh, :], XT[:, st, hh, :],
                                           start=True, stop=True)
                    elif name == "GU":
                        dve_has("Y5")
                        for hh in range(4):
                            mm = pe.matmul(B[1][:, hh * P:(hh + 1) * P], XT[:, st, hh, :], XR[:, i, hh, :, :],
                                           start=True, stop=True)
                    elif name == "RT":
                        act_has("GU")
                        for hh in range(4):
                            g, e = hh // 2, hh % 2
                            mm = pe.matmul(B[2][e * HD:(e + 1) * HD, g * P:(g + 1) * P], GU[:, st, 0, hh, :],
                                           part(st, hh, 1, 1), start=True, stop=True)
                    elif name == "MT":
                        for cc in range(2):
                            rows = slice(cc * CH, (cc + 1) * CH)
                            for g in range(2):
                                mm = pe.matmul(B[cc][:, g * P:(g + 1) * P], GU[rows, st, 0, 2 * g:2 * g + 2, :].rearrange("p h d -> p (h d)"),
                                               bh_tok[rows, i, g * P:(g + 1) * P], start=True, stop=True)
                    mm.then_inc(made[st], 1)

                def outputs(st, i):
                    n = i // 2
                    if i:
                        pe.wait_ge(y_out, i)
                    pe.wait_ge(kept_dve[st], upto(KEPT_DVE, n, "RT"))
                    for g in range(2):
                        for e in range(2):
                            hh = 2 * g + e
                            dst = ybank[e * HD:(e + 1) * HD, g * P:(g + 1) * P]
                            pe.matmul(dst, GU[:, st, 1, hh, :], part(st, hh, 1, 1), start=g == 0, stop=False,
                                      skip_group_check=True)
                            mm = pe.matmul(dst, v_tok[:, i, hh * HD:(hh + 1) * HD], part(st, hh, 0, 1),
                                           start=False, stop=i == 0, skip_group_check=True)

                def state(st, i, cc):
                    n = i // 2
                    c = 2 * i + cc
                    rows = slice(cc * CH, (cc + 1) * CH)
                    pe.wait_ge(kept_dve[st], upto(KEPT_DVE, n, "MT3"))
                    if c:
                        pe.wait_ge(s_done, c)
                        for g in range(2):
                            mm = pe.matmul(ybank[:, g * P + cc * CH:g * P + (cc + 1) * CH], S[:, c % 2, g, :],
                                           RT[:, st, g, cc * CH:(cc + 1) * CH], start=False, stop=True,
                                           skip_group_check=True)
                    if cc == 1:
                        mm.then_inc(y_done, 1)
                    if c == NCH - 1:
                        return
                    for g in range(2):
                        dst = zbank[:, g * P:(g + 1) * P]
                        pe.matmul(dst, bh_tok[rows, i, g * P:(g + 1) * P], GU[rows, st, 1, 2 * g:2 * g + 2, :].rearrange("p h d -> p (h d)"),
                                  start=g == 0, stop=False, skip_group_check=True)
                        mm = pe.matmul(dst, kh_tok[rows, i, g * P:(g + 1) * P], v_tok[rows, i, g * P:(g + 1) * P],
                                       start=False, stop=c == 0, skip_group_check=True)
                        if c:
                            mm = pe.matmul(dst, MT[:, st, 2 * cc + g, :], S[:, c % 2, g, :],
                                           start=False, stop=True, skip_group_check=True)
                    mm.then_inc(z_done, 1)

                for name, st, i in in_order():
                    if name == "Y":
                        outputs(st, i)
                    elif name in ("C0", "C1"):
                        state(st, i, int(name[1]))
                    else:
                        step(name, st, i)

            @block.scalar
            def _(act):
                def step(name, st, i):
                    n = i // 2
                    B = bank[3 * st:3 * st + 3]
                    done = kept_act[st]
                    act.wait_ge(made[st], upto(MADE, n, "turn" if name in ("a_tok", "bh_tok") else name))
                    if name == "a_tok":
                        act.copy(XR[:, i, :, 0, :], B[0][:, 0:256].rearrange("p (h d) -> p h d", h=4)).then_inc(done, 1)
                    elif name == "bh_tok":
                        act.copy(bh_tok[:, i, :], B[0][:, 256:512]).then_inc(done, 1)
                    elif name[0] == "X":
                        act.copy(X[:, st, :, :], cols4(B[0][:])).then_inc(done, 1)
                    elif name[0] == "T":
                        act.copy(Tm[:, st, :, :], cols4(B[1][:])).then_inc(done, 1)
                    else:
                        act.copy(GU[:, st, :, :, :].rearrange("p a h d -> p h a d"),
                                 B[1][:].rearrange("p (h a d) -> p h a d", h=4, a=2)).then_inc(done, 1)

                for name, st, i in in_order():
                    if name == "C1":
                        act.wait_ge(y_done, i + 1)
                        cols = slice(i * P, (i + 1) * P)
                        for g in range(2):
                            ins = act.copy(mixT[:, 3 + g, cols], ybank[:, g * P:(g + 1) * P])
                        ins.then_inc(y_out, 1)
                    for own in KEPT_ACT:
                        if name == ("turn" if own in ("a_tok", "bh_tok") else own):
                            step(own, st, i)

            @block.vector
            def _(dve):
                def step(name, st, i):
                    n = i // 2
                    B = bank[3 * st:3 * st + 3]
                    done = kept_dve[st]
                    was_made = lambda x: dve.wait_ge(made[st], upto(MADE, n, x))
                    own = lambda x: dve.wait_ge(done, upto(KEPT_DVE, n, x))
                    if name == "kh_tok":
                        was_made("turn")
                        dve.tensor_copy(kh_tok[:, i, :], B[1][:, 0:256]).then_inc(done, 1)
                    elif name == "v_tok":
                        dve.tensor_copy(v_tok[:, i, :], B[1][:, 256:512]).then_inc(done, 1)
                    elif name == "AV":
                        was_made("AV")
                        dve.tensor_copy(XR[:, i, :, 1, :],
                                        B[1][:, 0:256].rearrange("p (h d) -> p h d", h=4)).then_inc(done, 1)
                    elif name[0] == "A":
                        was_made(name)
                        if name == "A0" and i >= 2:
                            dve.wait_ge(y_done, i - 1)
                        if name == "A0" and i == 0:
                            for s in stored:
                                dve.wait_ge(s, 16 * (N_CM - N_B))
                        dve.tensor_tensor(Am[:, st, int(name[1]), :], B[int(name[1]) % 3][:], C("chunk_mask"),
                                          ALU.mult).then_inc(done, 1)
                    elif name == "level0":
                        own("A3")
                        dve.tensor_tensor(XT[:, st, :, :], Am[:, st, :, 256:256 + P],
                                          bcast(C("level0"), [0, 4], [1, P]), ALU.mult).then_inc(done, 1)
                    elif name == "XT0":
                        own("level0")
                        dve.tensor_tensor(XT[:, st, :, :], XT[:, st, :, :], bcast(C("ident"), [0, 4], [1, P]),
                                          ALU.add).then_inc(done, 1)
                    elif name[0] == "Y":
                        was_made(name)
                        level = int(name[1]) - 1
                        dve.copy_predicated(XT[:, st, :, :], bcast(masks[:, level * P:(level + 1) * P], [0, 4], [1, P]),
                                            cols4(B[2][:])).then_inc(done, 1)
                    elif name == "RT":
                        was_made("RT")
                        dve.tensor_tensor(RT[:, st, :, :], B[2][:, 0:256].rearrange("p (g t) -> p g t", g=2),
                                          AR[:, :, i, 1, :], ALU.add).then_inc(done, 1)
                    else:
                        was_made("MT")
                        q = int(name[2])
                        cc, g = q // 2, q % 2
                        dve.scalar_tensor_tensor(MT[:, st, q, :], C("ident"), PT[:, g, 2 * i + cc:2 * i + cc + 1],
                                                 B[cc][:, g * P:(g + 1) * P], ALU.mult, ALU.add).then_inc(done, 1)

                source = {"kh_tok": "turn", "v_tok": "turn", "level0": "A3", "XT0": "A3",
                          **{f"MT{k}": "MT" for k in range(4)}}
                for name, st, i in in_order():
                    for own in KEPT_DVE:
                        if name == source.get(own, own):
                            step(own, st, i)
                    if name in ("C0", "C1") and 2 * i + int(name[1]) < NCH - 1:
                        c = 2 * i + int(name[1])
                        dve.wait_ge(z_done, c + 1)
                        dve.tensor_tensor(S[:, (c + 1) % 2, :, :], zbank[:, 0:256].rearrange("p (g v) -> p g v", g=2),
                                          bcast(C("head_ones"), [0, 2], [1, P]), ALU.mult).then_inc(s_done, 1)


UNITS = [(h, qg, kb) for h in range(6) for qg in range(2) for kb in range(4 * qg + 3, -1, -1)]


GN_FIRST, GN_EVERY, GN_LAGS = 6, 12, 8


def attend(nc, ctx, w_out_d, w_out, w_out_in, qk_dram, toep_dram, rel_d, hot_d, sinks_d, C, masks, v_tok, mixT, R, qk, qk_in, mem, upper):
    sem = lambda n: ctx.enter_context(nc.semaphore(n))
    start = mem.at
    mem.at += 4 * 4 * T
    ring = 4
    ex = upper.put("exp_z", [P, ring, HALF])
    sp = mem.put("softplus", [P, ring, HALF])
    w = mem.put("weights", [P, ring, HALF])
    acc = mem.put("later_softplus", [P, 3, HALF])
    late_end = mem.at
    zeros = mem.put("zeros", [P, P])
    qa = mem.put("window_qk", [P, 4, T])
    rel = mem.put("rel_bias", [32, 8])
    hot = mem.put("bucket_one_hot", [32, 2, N_TOEPLITZ])
    toep = mem.put("toeplitz_rows", [8, N_TOEPLITZ])
    bias = mem.put("bias", [P, 6, 256])
    sink = mem.put("sink", [P, 8])
    late = Memory(nc, start, late_end)
    L = late.put("logits", [P, 2, 6, 256])
    Pr = late.put("probs", [P, 2, 6, 256])
    PrT = late.put("probs_T", [P, 2, 12, P])
    st = late.put("softmax_stats", [P, 2, 6, 8])
    yc, y2 = mem.put("y_centred", [P, HALF]), mem.put("y_squared", [P, HALF])
    mean_done, centred, squared, var_done, log_var, gn_rstd, gn_scaled, gn_gain, gn_bonus, gn_done = (
        sem(f"gn_{n}") for n in ("mean", "centred", "squared", "var", "log_var", "rstd", "scaled", "gain", "bonus", "done"))
    qa_in, rel_in = sem("qa_in"), sem("rel_in")
    z_done, e_done, l_done = (sem(f"sb_{n}") for n in ("z", "exp", "log"))
    sp_step = sem("sb_softplus")
    RAW, MASKED = -1, 0
    sp_at = lambda u, step: 2 * (u + 1) + step
    acc_done, s_done, w_raw, w_done, av_done, o_out = (sem(f"sb_{n}") for n in ("acc", "s", "w_raw", "w", "av", "o"))
    zero_done, toep_made, toep_kept, toep_out, bias_in = (sem(n) for n in ("zero_done", "toep_made", "toep_kept", "toep_out", "bias_in"))
    l_made, l_kept, stat, stat2, p_done, p_norm, pT_made, pT_kept, o_made, o_kept = (
        sem(f"win_{n}") for n in ("l_made", "l_kept", "stat", "stat2", "p", "p_norm", "pT_made", "pT_kept", "o_made", "o_kept"))

    groups = [(h, qg) for h in range(6) for qg in range(2)]
    diag = [kb >= 4 * qg for _, qg, kb in UNITS]
    first = [kb == 4 * qg + 3 for _, qg, kb in UNITS]
    last = [kb == 0 for _, _, kb in UNITS]
    place = [4 * qg + 3 - kb for _, qg, kb in UNITS]
    c0 = [max(0, (kb - 4 * qg) * P) for _, qg, kb in UNITS]
    N = len(UNITS)
    diags = [sum(diag[:u + 1]) for u in range(N)]
    adds = [sum(not x for x in last[:u + 1]) for u in range(N)]
    group_of = [groups.index((h, qg)) for h, qg, _ in UNITS]

    norm_at = {GN_FIRST + GN_EVERY * v + lag: (lag, v) for v in range(4) for lag in range(GN_LAGS)}

    def norm_part(v):
        g, half = v // 2, v % 2
        hs = slice(half * HALF, (half + 1) * HALF)
        return g, hs, mixT[:, 3 + g, hs]

    NZ = 5
    with ExitStack() as inner:
        gb = inner.enter_context(nc.psum_tensor("norm_bank", [P, HALF], F32))
        zb = [inner.enter_context(nc.psum_tensor(f"z{b}", [P, HALF], F32)) for b in range(NZ)]
        ob = [inner.enter_context(nc.psum_tensor(f"o{b}", [P, HALF], F32)) for b in range(2)]
        tb = zb[NZ - 1]
        with nc.Block() as block:
            @block.sync
            def _(sp_):
                sp_.dma_start(rel[:, 0:6], rel_d).then_inc(rel_in, 16)
                sp_.dma_start(hot[:].rearrange("p a m -> p (a m)"), hot_d).then_inc(rel_in, 16)
                sp_.dma_start(sink[:, 0:6], sinks_d.to_broadcast([P, 6])).then_inc(rel_in, 16)
                for t in range(3):
                    if t == 2:
                        sp_.wait_ge(av_done, 24)
                    if t:
                        sp_.dma_start(qk[:, t % 2, 0, :], qk_dram[t]).then_inc(qk_in[t % 2], 16)
                        sp_.dma_start(qk[:, t % 2, 1, :], qk_dram[3 + t]).then_inc(qk_in[t % 2], 16)
                    if t == 1:
                        for k in range(4):
                            sp_.dma_start(qa[:, k, :], qk_dram[6 + k]).then_inc(qa_in, 16)
                        sp_.wait_ge(toep_kept, 1)
                        sp_.dma_start(toep_dram, toep[0:6, :].unsqueeze(1).to_broadcast([6, P, N_TOEPLITZ])).then_inc(toep_out, 16)
                        sp_.wait_ge(toep_out, 16)
                        sp_.dma_start(bias[:], bass.AP(toep_dram.tensor, 127, [[N_TOEPLITZ - 1, P], [P * N_TOEPLITZ, 6], [1, 256]])
                                      ).then_inc(bias_in, 16)
                        sp_.dma_start(w_out[:].rearrange("p k d -> p (k d)"), w_out_d).then_inc(w_out_in, 16)

            @block.tensor
            def _(pe):
                def scores(u):
                    h, qg, kb = UNITS[u]
                    rows, t = slice((h % 2) * HD, (h % 2 + 1) * HD), h // 2
                    pe.wait_ge(qk_in[t % 2], 32 * (t // 2 + 1))
                    if u >= NZ:
                        pe.wait_ge(w_raw, u - NZ + 1)
                    elif u == NZ - 1:
                        pe.wait_ge(toep_kept, 1)
                    pe.matmul(zb[u % NZ][:, c0[u]:], qk[rows, t % 2, 1, kb * P:(kb + 1) * P],
                              qk[rows, t % 2, 0, qg * HALF + c0[u]:(qg + 1) * HALF],
                              start=True, stop=True).then_inc(z_done, 1)

                def suffix(u):
                    pe.wait_ge(sp_step, sp_at(u, MASKED))
                    mm = pe.matmul(zb[u % NZ][:, c0[u]:], C("suffix"), sp[:, u % ring, c0[u]:], start=False, stop=True,
                                   skip_group_check=True)
                    if not first[u]:
                        pe.wait_ge(acc_done, 2 * adds[u - 1])
                        from_ = c0[u] + P if diag[u] else 0
                        mm = pe.matmul(zb[u % NZ][:, from_:], C("all_later"), acc[:, adds[u - 1] % 3, from_:],
                                       start=False, stop=True, skip_group_check=True)
                    mm.then_inc(s_done, 1)

                def values(u):
                    h, qg, kb = UNITS[u]
                    g = group_of[u]
                    pe.wait_ge(w_done, u + 1)
                    if first[u] and g >= 2:
                        pe.wait_ge(o_out, g - 1)
                    rows = slice((h % 2) * HD, (h % 2 + 1) * HD)
                    pe.matmul(ob[g % 2][rows, c0[u]:], v_tok[:, kb, h * HD:(h + 1) * HD], w[:, u % ring, c0[u]:],
                              start=first[u], stop=last[u], skip_group_check=True).then_inc(av_done, 1)

                def norm(lag, v):
                    if lag == 0:
                        pe.matmul(gb[:], C("head_mean"), norm_part(v)[2], start=True, stop=True).then_inc(mean_done, 1)
                    elif lag == 2:
                        pe.wait_ge(squared, v + 1)
                        pe.wait_ge(centred, v + 1)
                        pe.matmul(gb[:], C("head_mean"), y2[:], start=True, stop=True).then_inc(var_done, 1)

                scores(0)
                scores(1)
                pe.wait_ge(rel_in, 48)
                pe.matmul(tb[0:6, 0:N_TOEPLITZ], rel[:, 0:6], hot[:, 0, :], start=True, stop=True).then_inc(toep_made, 1)
                for u in range(N + 2):
                    if u in norm_at:
                        norm(*norm_at[u])
                    if u + 2 < N:
                        scores(u + 2)
                    if u and u - 1 < N:
                        suffix(u - 1)
                    if u >= 2:
                        values(u - 2)

            @block.scalar
            def _(act):
                def weights(u):
                    act.wait_ge(s_done, u + 1)
                    if u >= ring:
                        act.wait_ge(av_done, u - ring + 1)
                    act.activation(w[:, u % ring, c0[u]:], zb[u % NZ][:, c0[u]:], ACT.Exp).then_inc(w_raw, 1)

                def norm(lag, v):
                    if lag == 1:
                        act.wait_ge(centred, v + 1)
                        act.activation(y2[:], yc[:], ACT.Square).then_inc(squared, 1)
                    elif lag == 3:
                        act.wait_ge(var_done, v + 1)
                        act.activation(y2[:], gb[:], ACT.Ln, bias=GN_EPS).then_inc(log_var, 1)
                        act.wait_ge(log_var, v + 1)
                        act.activation(y2[:], y2[:], ACT.Exp, scale=-0.5).then_inc(gn_rstd, 1)
                    elif lag == 5:
                        act.wait_ge(gn_scaled, v + 1)
                        g = norm_part(v)[0]
                        act.activation(yc[:], yc[:], ACT.Identity, bias=C("lnx_b", g), scale=C("lnx_g", g)).then_inc(gn_gain, 1)

                act.preload_act_table_set("natural_log_exp_and_others")
                for u in range(N + 2):
                    if u in norm_at:
                        norm(*norm_at[u])
                    if u < N:
                        act.wait_ge(z_done, u + 1)
                        if u >= ring:
                            act.wait_ge(sp_step, sp_at(u - ring, RAW))
                        b = ex[:, u % ring, c0[u]:]
                        act.activation(b, zb[u % NZ][:, c0[u]:], ACT.Exp).then_inc(e_done, 1)
                        act.wait_ge(e_done, u + 1)
                        act.activation(b, b, ACT.Ln, bias=1.0).then_inc(l_done, 1)
                    if u >= 2:
                        weights(u - 2)

            @block.vector
            def _(dve):
                dve.memset(zeros[:], 0.0).then_inc(zero_done, 1)
                dve.wait_ge(zero_done, 1)
                for u in range(N + 2):
                    if u == 1:
                        dve.wait_ge(toep_made, 1)
                        dve.tensor_tensor(toep[0:6, :], tb[0:6, 0:N_TOEPLITZ], hot[0:6, 1, :], ALU.add).then_inc(toep_kept, 1)
                    if norm_at.get(u, (1, 0))[0] == 0:
                        v = norm_at[u][1]
                        dve.wait_ge(mean_done, v + 1)
                        if v:
                            dve.wait_ge(gn_done, v)
                        dve.tensor_tensor(yc[:], norm_part(v)[2], gb[:], ALU.subtract).then_inc(centred, 1)
                    if u < N:
                        dve.wait_ge(l_done, u + 1)
                        if u >= ring:
                            dve.wait_ge(s_done, u - ring + 1)
                            dve.wait_ge(acc_done, 2 * adds[u - ring])
                        d = slice(c0[u], c0[u] + P)
                        dve.scalar_tensor_tensor(sp[:, u % ring, c0[u]:], ex[:, u % ring, c0[u]:], CLAMP,
                                                 zb[u % NZ][:, c0[u]:], ALU.min, ALU.max).then_inc(sp_step, 1)
                        dve.wait_ge(sp_step, sp_at(u, RAW))
                        if diag[u]:
                            dve.tensor_tensor(sp[:, u % ring, d], sp[:, u % ring, d], C("key_before"),
                                              ALU.mult).then_inc(sp_step, 1)
                            dve.wait_ge(sp_step, sp_at(u, MASKED))
                        else:
                            dve.nop().then_inc(sp_step, 1)
                    if u >= 2:
                        v = u - 2
                        dve.wait_ge(w_raw, v + 1)
                        if diag[v]:
                            dve.copy_predicated(w[:, v % ring, c0[v]:c0[v] + P], masks[:, N_LEVELS * P:(N_LEVELS + 1) * P],
                                                zeros[:]).then_inc(w_done, 1)
                        else:
                            dve.nop().then_inc(w_done, 1)
                        if last[v]:
                            h, qg, _ = UNITS[v]
                            g = group_of[v]
                            rows = slice((h % 2) * HD, (h % 2 + 1) * HD)
                            dve.wait_ge(av_done, v + 1)
                            dve.tensor_copy(mixT[rows, 5 + h // 2, qg * HALF:(qg + 1) * HALF], ob[g % 2][rows, :]
                                            ).then_inc(o_out, 1)

            @block.gpsimd
            def _(pool):
                def norm(lag, v):
                    g, hs, y = norm_part(v)
                    if lag == 4:
                        pool.wait_ge(gn_rstd, v + 1)
                        pool.tensor_tensor(yc[:], yc[:], y2[:], ALU.mult).then_inc(gn_scaled, 1)
                    elif lag == 6:
                        pool.wait_ge(gn_gain, v + 1)
                        pool.tensor_tensor(yc[:], yc[:], R["bonus"][:, g, hs], ALU.add).then_inc(gn_bonus, 1)
                    elif lag == 7:
                        pool.wait_ge(gn_bonus, v + 1)
                        pool.tensor_tensor(y, yc[:], R["g"][:, g, hs], ALU.mult).then_inc(gn_done, 1)

                for u in range(N):
                    if u in norm_at:
                        norm(*norm_at[u])
                    if last[u]:
                        continue
                    pool.wait_ge(sp_step, sp_at(u, MASKED))
                    k, c = place[u], c0[u]
                    if k >= 1:
                        pool.wait_ge(acc_done, 2 * adds[u - 1])
                    if u >= 2:
                        pool.wait_ge(s_done, u - 1)
                    new, old, here = acc[:, adds[u] % 3, :], acc[:, adds[u - 1] % 3, :], sp[:, u % ring, :]
                    if diag[u]:
                        pool.tensor_copy(new[:, c:c + P], here[:, c:c + P]).then_inc(acc_done, 1 if k else 2)
                        c += P
                    if k:
                        pool.tensor_tensor(new[:, c:], old[:, c:], here[:, c:], ALU.add).then_inc(acc_done, 1 if diag[u] else 2)

    with ExitStack() as inner:
        lb = inner.enter_context(nc.psum_tensor("logit_banks", [P, 4 * HALF], F32))
        pTb = inner.enter_context(nc.psum_tensor("prob_banks", [P, 3 * HALF], F32))
        ob = inner.enter_context(nc.psum_tensor("out_bank", [P, HALF], F32))
        blocks = lambda n: (1,) if n == 0 else (0, 1)
        keys = [slice(P, 256) if n == 0 else slice(0, 256) for n in range(NT)]
        with nc.Block() as block:
            @block.tensor
            def _(pe):
                pe.wait_ge(qa_in, 64)

                def logits(n):
                    if n:
                        pe.wait_ge(l_kept, n)
                    lo = keys[n].start
                    for e in range(2):
                        rows = slice(e * HD, (e + 1) * HD)
                        for j in range(3):
                            at = e * 2 * HALF + j * 256
                            mm = pe.matmul(lb[:, at + lo:at + 256], qa[rows, j, n * P:(n + 1) * P],
                                           qa[rows, 3, (n - 1) * P + lo:(n + 1) * P], start=True, stop=True)
                    mm.then_inc(l_made, 1)

                def turn(n):
                    pe.wait_ge(p_norm, n + 1)
                    if n:
                        pe.wait_ge(pT_kept, n)
                    for h in range(6):
                        for kb in blocks(n):
                            mm = pe.transpose(pTb[:, (2 * h + kb) * P:(2 * h + kb + 1) * P],
                                              Pr[:, n % 2, h, kb * P:(kb + 1) * P], C("ident"))
                    mm.then_inc(pT_made, 1)

                def outputs(n):
                    pe.wait_ge(pT_kept, n + 1)
                    if n:
                        pe.wait_ge(o_kept, n)
                    for h in range(6):
                        e, j = h // 3, h % 3
                        for kb in blocks(n):
                            mm = pe.matmul(ob[e * HD:(e + 1) * HD, j * P:(j + 1) * P],
                                           v_tok[:, n - 1 + kb, 384 + e * HD:384 + (e + 1) * HD], PrT[:, n % 2, 2 * h + kb, :],
                                           start=kb == blocks(n)[0], stop=kb == 1)
                    mm.then_inc(o_made, 1)

                logits(0)
                logits(1)
                for n in range(NT + 1):
                    if n + 2 < NT:
                        logits(n + 2)
                    if n:
                        outputs(n - 1)
                    if n < NT:
                        turn(n)

            @block.scalar
            def _(act):
                def exponentials(n):
                    b = n % 2
                    act.wait_ge(stat, 4 * (n + 1))
                    if n >= 2:
                        act.wait_ge(pT_made, n - 1)
                    for h in range(6):
                        act.activation(Pr[:, b, h, keys[n]], L[:, b, h, keys[n]], ACT.Exp, bias=st[:, b, 1, h:h + 1],
                                       accum_out=st[:, b, 2, h:h + 1])
                    act.activation(st[:, b, 3, 0:6], st[:, b, 3, 0:6], ACT.Exp).then_inc(p_done, 1)

                exponentials(0)
                for n in range(NT):
                    if n + 1 < NT:
                        exponentials(n + 1)
                    act.wait_ge(pT_made, n + 1)
                    if n >= 2:
                        act.wait_ge(o_made, n - 1)
                    if n == 0:
                        act.copy(PrT[:, 0, :, :].rearrange("p (h k) q -> p h k q", k=2)[:, :, 1, :],
                                 pTb[:].rearrange("p (h k q) -> p h k q", h=6, k=2)[:, :, 1, :]).then_inc(pT_kept, 1)
                    else:
                        act.copy(PrT[:, n % 2, :, :].rearrange("p a q -> p (a q)"), pTb[:]).then_inc(pT_kept, 1)

            @block.vector
            def _(dve):
                def row(n, j):
                    return st[:, n % 2, j, 0:6]

                def logits(n):
                    b, k = n % 2, keys[n]
                    dve.wait_ge(l_made, n + 1)
                    if n >= 2:
                        dve.wait_ge(p_done, n - 1)
                    logit = lb[:].rearrange("p (e x) -> p e x", e=2)[:, :, 0:768].rearrange("p e (j k) -> p e j k", j=3)
                    dve.tensor_tensor(L[:, b, :, :].rearrange("p (e j) k -> p e j k", e=2)[:, :, :, k], logit[:, :, :, k],
                                      bias[:].rearrange("p (e j) k -> p e j k", e=2)[:, :, :, k], ALU.add).then_inc(l_kept, 1)
                    dve.wait_ge(l_kept, n + 1)
                    dve.tensor_reduce(row(n, 0), L[:, b, :, k], AX, ALU.max).then_inc(stat, 1)
                    dve.wait_ge(stat, 4 * n + 1)
                    dve.tensor_tensor(row(n, 0), row(n, 0), sink[:, 0:6], ALU.max).then_inc(stat, 1)
                    dve.wait_ge(stat, 4 * n + 2)
                    dve.tensor_scalar(row(n, 1), row(n, 0), -1.0, None, ALU.mult).then_inc(stat, 1)
                    dve.wait_ge(stat, 4 * n + 3)
                    dve.tensor_tensor(row(n, 3), sink[:, 0:6], row(n, 1), ALU.add).then_inc(stat, 1)

                def normalise(n):
                    b, k = n % 2, keys[n]
                    dve.wait_ge(p_done, n + 1)
                    dve.tensor_tensor(row(n, 4), row(n, 2), row(n, 3), ALU.add).then_inc(stat2, 1)
                    dve.wait_ge(stat2, 2 * n + 1)
                    dve.reciprocal(row(n, 5), row(n, 4)).then_inc(stat2, 1)
                    dve.wait_ge(stat2, 2 * n + 2)
                    dve.tensor_tensor(Pr[:, b, :, k], Pr[:, b, :, k], bcast(row(n, 5), [1, 6], [0, k.stop - k.start]),
                                      ALU.mult).then_inc(p_norm, 1)

                dve.wait_ge(bias_in, 16)
                dve.wait_ge(rel_in, 48)
                logits(0)
                for n in range(NT + 1):
                    if n + 1 < NT:
                        logits(n + 1)
                    if n < NT:
                        normalise(n)
                    if n:
                        dve.wait_ge(o_made, n)
                        dve.tensor_copy(mixT[:, 0:3, (n - 1) * P:n * P],
                                        ob[:, 0:3 * P].rearrange("p (j q) -> p j q", j=3)).then_inc(o_kept, 1)


N_EXPERTS, N_GROUPS, PER_GROUP, TOP_K, FF = 16, 4, 4, 2, 256
MAX_BLOCKS = TOP_K * T // P + N_EXPERTS - 1 + 1
MIN_BLOCKS = TOP_K * T // P
PLANNED = MAX_BLOCKS + 1
PLAN_ENDS = PLANNED + 1
PLAN = PLAN_ENDS + N_EXPERTS
EXPERTS_AT = 105600
W_COLS = 2 * ND * FF + 2 * D
N_WBUF = 3
SPARE_ROW = TOP_K * T
SLOT_BLOCKS = MAX_BLOCKS + 3
BIG = 1e30

ROUTE = {"iota16": (0, 16), "group16": (16, 16), "iota4": (32, 4), "edges": (36, 8), "blocks": (48, 35),
         "iota16_far": (84, 16), "iota4_far": (100, 4), "places": (104, P)}
N_ROUTE = 104 + P
FAR = 100.0


def routing_constants():
    c = np.zeros((1, N_ROUTE), np.float32)
    c[0, 0:16] = np.arange(16)
    c[0, 16:32] = np.arange(16) // PER_GROUP
    c[0, 32:36] = np.arange(4)
    c[0, 36:44] = np.arange(8) * P
    c[0, 48:83] = np.arange(35)
    c[0, 84:100] = np.arange(16) + FAR
    c[0, 100:104] = np.arange(4) + FAR
    c[0, 104:] = np.arange(P)
    return c


def mix_and_route(nc, ctx, wgu_d, wd_d, h_dram, h1_dram, rows4, rw_d, rb_d, route_d, C, mixT, w_out, w_out_in, K, mem, upper):
    sem = lambda n: ctx.enter_context(nc.semaphore(n))
    h1, rows, gates, slots, plan = K["h1"], K["rows"], K["gates"], K["slots"], K["plan"]
    hb_at = mem.at
    hb = mem.put("h_in", [P, 2, D])
    r_at = mem.at
    r = mem.put("residual", [P, 2, D])
    xT = upper.put("h1_T", [P, ND, P])
    rw = mem.put("router_w", [P, ND, 16])
    rb = mem.put("router_bias", [P, 16])
    rc = upper.put("route_consts", [P, N_ROUTE])
    stats = mem.put("ln1_stats", [P, 12])
    mv = mem.put("ln1_mv", [P, NT, 2])
    std = mem.put("ln1_std", [P, NT, 2])
    ids = mem.put("token_ids", [P, TOP_K, NT, 2], I32)
    ids_f = upper.put("ids_f", [P, TOP_K, NT, 2])
    where_i = upper.put("where_i", [P, 2, TOP_K, NT], I32)
    where = upper.put("where", [P, 2, TOP_K, NT])
    at_place = nc.alloc_sbuf_tensor_at("at_place", [P, TOP_K * NT, P], F32, offset=hb_at)
    in_block = nc.alloc_sbuf_tensor_at("in_block", [P, TOP_K * NT, SLOT_BLOCKS], F32, offset=r_at)
    block_ids = nc.alloc_sbuf_tensor_at("block_ids", [P, TOP_K * NT, SLOT_BLOCKS, 2], F32,
                                        offset=r_at + 4 * TOP_K * NT * SLOT_BLOCKS)
    big = lambda n: mem.put(n, [P, NT, 16])
    score, sel, selm, t16, oh1, oh2, both, base, rank = (
        big(n) for n in ("score", "sel", "sel_in_group", "t16", "first_choice", "second_choice", "both", "base", "rank"))
    n_e = mem.put("n_e", [P, 16])
    hi = mem.put("hi", [P, NT, 4, 2])
    lo = mem.put("lo", [P, NT, 4, 2])
    g4 = mem.put("g4", [P, 3, NT, 4])
    t8 = mem.put("t8", [P, 6, NT])
    cmp_ = upper.put("block_compare", [P, PLANNED, 16])
    e16 = mem.put("e16", [P, 4, 16])
    plan_f = mem.put("plan_f", [P, PLAN])
    h_in = [sem("h_in0"), sem("h_in1")]
    par_in = sem("route_in")
    m_made, resid, ln_step, ln_std, ln_rstd, xn = (sem(f"ln1_{n}") for n in (
        "m", "resid", "step", "std", "rstd", "xn"))
    xT_made, xT_kept, r_made, h1_step = (sem(n) for n in ("rt_xT_made", "rt_xT_kept", "rt_made", "h1_step"))
    h1_out, ids_done, ids_summed = sem("h1_out"), sem("ids_done"), sem("ids_summed")
    scored, routed, counted, ranked = sem("scored"), sem("routed"), sem("counted"), sem("ranked")
    with ExitStack() as inner:
        mb = [inner.enter_context(nc.psum_tensor(f"m{b}", [P, HALF], F32)) for b in range(4)]
        xb = [inner.enter_context(nc.psum_tensor(f"rx{b}", [P, HALF], F32)) for b in range(2)]
        rbk = inner.enter_context(nc.psum_tensor("router_bank", [P, HALF], F32))
        cb = inner.enter_context(nc.psum_tensor("count_bank", [P, HALF], F32))
        with nc.Block() as block:
            @block.sync
            def _(sp):
                def load_h(i):
                    sp.dma_start(hb[:, i % 2, :], h_dram[i * P:(i + 1) * P, :]).then_inc(h_in[i % 2], 16)

                for i in range(2):
                    load_h(i)
                for k in range(4):
                    sp.dma_start(rows[:, k, :], rows4[k:k + 1, :].to_broadcast([P, D])).then_inc(par_in, 16)
                sp.dma_start(rw[:].rearrange("p k e -> p (k e)"), rw_d).then_inc(par_in, 16)
                sp.dma_start(rb[:], rb_d.to_broadcast([P, 16])).then_inc(par_in, 16)
                sp.dma_start(rc[:], route_d.to_broadcast([P, N_ROUTE])).then_inc(par_in, 16)
                for i in range(2, NT):
                    sp.wait_ge(resid, 2 * (i - 1))
                    load_h(i)
                    sp.wait_ge(h1_step, 2 * (i - 1))
                    sp.dma_start(h1_dram[(i - 2) * P:(i - 1) * P, :], h1[:, i - 2, :]).then_inc(h1_out, 16)
                for i in range(NT - 2, NT):
                    sp.wait_ge(h1_step, 2 * (i + 1))
                    sp.dma_start(h1_dram[i * P:(i + 1) * P, :], h1[:, i, :]).then_inc(h1_out, 16)
                load_expert(sp, 0, K, wgu_d, wd_d)
                sp.wait_ge(m_made, 2 * NT)
                for e in range(1, N_WBUF):
                    load_expert(sp, e, K, wgu_d, wd_d)
                sp.wait_ge(h1_out, 16 * NT)

            @block.tensor
            def _(pe):
                def mix(i, between=None):
                    for half in range(2):
                        if half and between is not None:
                            router(between)
                        n = 2 * i + half
                        if n >= 4:
                            pe.wait_ge(resid, n - 3)
                        for k in range(ND):
                            mm = pe.matmul(mb[n % 4][:], mixT[:, k, i * P:(i + 1) * P],
                                           w_out[:, k, half * HALF:(half + 1) * HALF], start=k == 0, stop=k == ND - 1)
                        mm.then_inc(m_made, 1)

                def turn(i):
                    pe.wait_ge(xn, i + 1)
                    if i:
                        pe.wait_ge(xT_kept, ND * i)
                    for d in range(ND):
                        mm = pe.transpose(xb[d // 4][:, (d % 4) * P:(d % 4 + 1) * P], r[:, i % 2, d * P:(d + 1) * P], C("ident"))
                    mm.then_inc(xT_made, 1)

                def router(i):
                    pe.wait_ge(xT_kept, ND * (i + 1))
                    for d in range(ND):
                        mm = pe.matmul(rbk[:, i * 16:(i + 1) * 16], xT[:, d, :], rw[:, d, :], start=d == 0, stop=d == ND - 1)
                    mm.then_inc(r_made, 1)

                pe.wait_ge(w_out_in, 16)
                mix(0)
                mix(1)
                pe.wait_ge(par_in, 16 * 7)
                for i in range(NT):
                    if i + 2 < NT:
                        mix(i + 2, i - 1 if i else None)
                    elif i:
                        router(i - 1)
                    turn(i)
                router(NT - 1)
                pe.wait_ge(routed, ROUTED["both"])
                pe.matmul(cb[:, 0:P], C("key_before"), both[:].rearrange("p i e -> p (i e)"), start=True, stop=True)
                pe.matmul(cb[:, P:2 * P], C("ones"), both[:].rearrange("p i e -> p (i e)"), start=True, stop=True).then_inc(counted, 1)
                pe.wait_ge(routed, ROUTED["at_place"])
                for n in range(TOP_K * NT):
                    mm = pe.matmul(rbk[:, 0:2 * SLOT_BLOCKS], at_place[:, n, :], block_ids[:, n, :, :].rearrange("p b c -> p (b c)"),
                                   start=n == 0, stop=n == TOP_K * NT - 1)
                mm.then_inc(ids_summed, 1)

            @block.scalar
            def _(act):
                for i in range(NT):
                    act.wait_ge(ln_step, 3 * (i + 1))
                    act.activation(std[:, i, 0:1], mv[:, i, 1:2], ACT.Sqrt, bias=LN_EPS).then_inc(ln_std, 1)
                    act.wait_ge(xT_made, i + 1)
                    if i:
                        act.wait_ge(r_made, i)
                    for d in range(ND):
                        act.activation(xT[:, d, :], xb[d // 4][:, (d % 4) * P:(d % 4 + 1) * P], ACT.Identity,
                                       bias=C("ln1_b", d), scale=C("ln1_g", d)).then_inc(xT_kept, 1)
                act.wait_ge(r_made, NT)
                act.activation(score[:].rearrange("p i e -> p (i e)"), rbk[:, 0:P], ACT.Sigmoid).then_inc(scored, 1)

            @block.gpsimd
            def _(pool):
                for k in range(TOP_K):
                    pool.iota(ids[:, k, :, 0], pattern=[[P, NT]], base=0, channel_multiplier=1).then_inc(ids_done, 1)
                    pool.iota(ids[:, k, :, 1], pattern=[[P, NT]], base=k * T - SPARE_ROW, channel_multiplier=1).then_inc(ids_done, 1)
                pool.wait_ge(par_in, 16 * 7)
                for i in range(NT):
                    pool.wait_ge(xn, i + 1)
                    pool.tensor_tensor(h1[:, i, :], r[:, i % 2, :], rows[:, 0, :], ALU.mult).then_inc(h1_step, 1)
                    pool.wait_ge(h1_step, 2 * i + 1)
                    pool.tensor_tensor(h1[:, i, :], h1[:, i, :], rows[:, 1, :], ALU.add).then_inc(h1_step, 1)

            @block.vector
            def _(dve):
                for i in range(NT):
                    dve.wait_ge(h_in[i % 2], 16 * (i // 2 + 1))
                    if i >= 2:
                        dve.wait_ge(h1_step, 2 * i - 3)
                        dve.wait_ge(xT_made, i - 1)
                    for half in range(2):
                        hs = slice(half * HALF, (half + 1) * HALF)
                        dve.wait_ge(m_made, 2 * i + half + 1)
                        dve.scalar_tensor_tensor(r[:, i % 2, hs], hb[:, i % 2, hs], ALPHA, mb[(2 * i + half) % 4][:],
                                                 ALU.mult, ALU.add).then_inc(resid, 1)
                        dve.wait_ge(resid, 2 * i + half + 1)
                        dve.bn_stats(stats[:, 6 * half:6 * half + 6], r[:, i % 2, hs]).then_inc(ln_step, 1)
                    dve.wait_ge(ln_step, 3 * i + 2)
                    dve.bn_aggr(mv[:, i, :], stats[:]).then_inc(ln_step, 1)
                    dve.wait_ge(ln_std, i + 1)
                    dve.reciprocal(std[:, i, 1:2], std[:, i, 0:1]).then_inc(ln_rstd, 1)
                    dve.wait_ge(ln_rstd, i + 1)
                    dve.tensor_scalar(r[:, i % 2, :], r[:, i % 2, :], mv[:, i, 0:1], std[:, i, 1:2],
                                      ALU.subtract, ALU.mult).then_inc(xn, 1)
                row = lambda n: rc[:, ROUTE[n][0]:ROUTE[n][0] + ROUTE[n][1]]
                per_token = lambda ap: bcast(ap, [1, NT], [0, 16])
                sel4 = sel[:].rearrange("p i (g e) -> p i g e", e=PER_GROUP)
                top, second, gsum = (g4[:, k, :, :] for k in range(3))
                gbest, m1, m2, w1, w2, wsum = (t8[:, k, :] for k in range(6))
                blocks, ends, starts, _ = (e16[:, k, :] for k in range(4))
                dve.wait_ge(par_in, 16 * 7)
                flat = lambda ap: ap.rearrange("p k i -> p (k i)")
                summed = rbk[:, 0:2 * SLOT_BLOCKS].rearrange("p (b c) -> p b c", c=2)
                n = 0
                for name in ROUTE_STEPS:
                    if n:
                        dve.wait_ge(routed, n)
                    if name == "sel":
                        dve.wait_ge(scored, 1)
                        ins = dve.tensor_tensor(sel[:], score[:], bcast(rb[:], [0, NT], [1, 16]), ALU.add)
                    elif name == "hi":
                        ins = dve.tensor_tensor(hi[:], sel4[:, :, :, 0:2], sel4[:, :, :, 2:4], ALU.max)
                    elif name == "lo":
                        ins = dve.tensor_tensor(lo[:], sel4[:, :, :, 0:2], sel4[:, :, :, 2:4], ALU.min)
                    elif name == "top":
                        ins = dve.tensor_tensor(top, hi[:, :, :, 0], hi[:, :, :, 1], ALU.max)
                    elif name == "hi_min":
                        ins = dve.tensor_tensor(second, hi[:, :, :, 0], hi[:, :, :, 1], ALU.min)
                    elif name == "lo_max":
                        ins = dve.tensor_tensor(gsum, lo[:, :, :, 0], lo[:, :, :, 1], ALU.max)
                    elif name == "second":
                        ins = dve.tensor_tensor(second, second, gsum, ALU.max)
                    elif name == "gsum":
                        ins = dve.tensor_tensor(gsum, top, second, ALU.add)
                    elif name == "gmax":
                        ins = dve.tensor_reduce(gbest, gsum, AX, ALU.max)
                    elif name == "g_is":
                        ins = dve.tensor_tensor(top, gsum, bcast(gbest, [1, NT], [0, 4]), ALU.is_equal)
                    elif name == "g_cand":
                        ins = dve.scalar_tensor_tensor(top, top, -FAR, bcast(row("iota4_far"), [0, NT], [1, 4]), ALU.mult, ALU.add)
                    elif name == "g_index":
                        ins = dve.tensor_reduce(gbest, top, AX, ALU.min)
                    elif name == "in_group":
                        ins = dve.tensor_tensor(t16[:], bcast(row("group16"), [0, NT], [1, 16]), per_token(gbest), ALU.is_equal)
                    elif name == "outside":
                        ins = dve.tensor_scalar(t16[:], t16[:], BIG, -BIG, ALU.mult, ALU.add)
                    elif name == "selm":
                        ins = dve.tensor_tensor(selm[:], sel[:], t16[:], ALU.add)
                    elif name in ("max1", "max2"):
                        ins = dve.tensor_reduce(m1 if name == "max1" else m2, selm[:], AX, ALU.max)
                    elif name in ("is1", "is2"):
                        ins = dve.tensor_tensor(t16[:], selm[:], per_token(m1 if name == "is1" else m2), ALU.is_equal)
                    elif name in ("cand1", "cand2"):
                        ins = dve.scalar_tensor_tensor(t16[:], t16[:], -FAR, bcast(row("iota16_far"), [0, NT], [1, 16]),
                                                       ALU.mult, ALU.add)
                    elif name in ("index1", "index2"):
                        ins = dve.tensor_reduce(m1 if name == "index1" else m2, t16[:], AX, ALU.min)
                    elif name in ("hot1", "hot2"):
                        ins = dve.tensor_tensor(oh1[:] if name == "hot1" else oh2[:], bcast(row("iota16"), [0, NT], [1, 16]),
                                                per_token(m1 if name == "hot1" else m2), ALU.is_equal)
                    elif name == "without1":
                        ins = dve.scalar_tensor_tensor(selm[:], oh1[:], -2 * BIG, selm[:], ALU.mult, ALU.add)
                    elif name == "both":
                        ins = dve.tensor_tensor(both[:], oh1[:], oh2[:], ALU.add)
                    elif name in ("s1", "s2"):
                        ins = dve.tensor_tensor(t16[:], oh1[:] if name == "s1" else oh2[:], score[:], ALU.mult)
                    elif name in ("w1", "w2"):
                        ins = dve.tensor_reduce(w1 if name == "w1" else w2, t16[:], AX, ALU.add)
                    elif name == "wsum":
                        ins = dve.tensor_tensor(wsum, w1, w2, ALU.add)
                    elif name == "wrec":
                        ins = dve.reciprocal(wsum, wsum)
                    elif name in ("gate1", "gate2"):
                        k = int(name[4]) - 1
                        ins = dve.tensor_tensor(gates[:, k, :], (w1, w2)[k], wsum, ALU.mult)
                    elif name == "base0":
                        dve.wait_ge(counted, 1)
                        ins = dve.memset(base[:, 0, :], 0.0)
                    elif name[:4] == "base":
                        i = int(name[4:])
                        dst = n_e[:] if i == NT else base[:, i, :]
                        ins = dve.tensor_tensor(dst, base[:, i - 1, :], cb[:, P + 16 * (i - 1):P + 16 * i], ALU.add)
                    elif name == "rank":
                        ins = dve.tensor_tensor(rank[:], cb[:, 0:P].rearrange("p (i e) -> p i e", i=NT), base[:], ALU.add)
                    elif name == "edges":
                        ins = dve.tensor_tensor(cmp_[:, 0:16, 0:8], bcast(n_e[:], [1, 16], [0, 8]),
                                                bcast(row("edges"), [0, 16], [1, 8]), ALU.is_gt)
                    elif name == "blocks":
                        ins = dve.tensor_reduce(blocks, cmp_[:, 0:16, 0:8], AX, ALU.add)
                    elif name == "ends":
                        ins = dve.tensor_tensor_scan(ends, C("ones")[:, 0:16], blocks, 0.0, ALU.mult, ALU.add)
                    elif name == "starts":
                        ins = dve.tensor_tensor(starts, ends, blocks, ALU.subtract)
                    elif name == "start_slots":
                        ins = dve.tensor_scalar(starts, starts, float(P), None, ALU.mult)
                    elif name == "slot":
                        ins = dve.tensor_tensor(rank[:], rank[:], bcast(starts, [0, NT], [1, 16]), ALU.add)
                    elif name in ("slot1", "slot2"):
                        ins = dve.tensor_tensor(t16[:], rank[:], oh1[:] if name == "slot1" else oh2[:], ALU.mult)
                    elif name in ("sum1", "sum2"):
                        ins = dve.tensor_reduce(m1 if name == "sum1" else m2, t16[:], AX, ALU.add)
                    elif name in ("int1", "int2"):
                        k = int(name[3]) - 1
                        ins = dve.tensor_copy(slots[:, k, :], (m1, m2)[k])
                    elif name == "ended":
                        ins = dve.tensor_tensor(cmp_[:], bcast(row("blocks")[:, 0:PLANNED], [1, PLANNED], [0, 16]),
                                                bcast(ends, [0, PLANNED], [1, 16]), ALU.is_ge)
                    elif name == "expert":
                        ins = dve.tensor_reduce(plan_f[:, 0:PLANNED], cmp_[:], AX, ALU.add)
                    elif name == "expert_max":
                        ins = dve.tensor_scalar(plan_f[:, 0:PLANNED], plan_f[:, 0:PLANNED], float(N_EXPERTS - 1), None, ALU.min)
                    elif name == "total":
                        ins = dve.tensor_scalar(plan_f[:, PLANNED:PLANNED + 1], ends[:, 15:16], float(-MIN_BLOCKS), None, ALU.add)
                    elif name == "plan_ends":
                        ins = dve.tensor_copy(plan_f[:, PLAN_ENDS:PLAN], ends)
                    elif name == "plan":
                        ins = dve.tensor_copy(plan[:], plan_f[0:1, :])
                    elif name == "ids_f":
                        dve.wait_ge(ids_done, 2 * TOP_K)
                        ins = dve.tensor_copy(ids_f[:], ids[:])
                    elif name == "block":
                        ins = dve.tensor_scalar(where_i[:, 0, :, :], slots[:], P.bit_length() - 1, None, ALU.logical_shift_right)
                    elif name == "place":
                        ins = dve.tensor_scalar(where_i[:, 1, :, :], slots[:], P - 1, None, ALU.bitwise_and)
                    elif name == "where":
                        ins = dve.tensor_copy(where[:], where_i[:])
                    elif name == "at_place":
                        ins = dve.tensor_tensor(at_place[:], bcast(row("places"), [0, TOP_K * NT], [1, P]),
                                                bcast(flat(where[:, 1, :, :]), [1, TOP_K * NT], [0, P]), ALU.is_equal)
                    elif name == "in_block":
                        dve.wait_ge(h1_step, 2 * NT)
                        dve.wait_ge(xT_made, NT)
                        ins = dve.tensor_tensor(in_block[:], bcast(row("blocks"), [0, TOP_K * NT], [1, SLOT_BLOCKS]),
                                                bcast(flat(where[:, 0, :, :]), [1, TOP_K * NT], [0, SLOT_BLOCKS]), ALU.is_equal)
                    elif name in ("block_ids0", "block_ids1"):
                        c = int(name[-1])
                        each = ids_f[:].rearrange("p k i c -> p (k i) c")[:, :, c]
                        ins = dve.tensor_tensor(block_ids[:, :, :, c], in_block[:], bcast(each, [2, TOP_K * NT], [0, SLOT_BLOCKS]),
                                                ALU.mult)
                    elif name == "slot_ids0":
                        dve.wait_ge(ids_summed, 1)
                        ins = dve.tensor_copy(K["ids"][:, :, 0], summed[:, :, 0])
                    elif name == "slot_ids1":
                        ins = dve.tensor_scalar(K["ids"][:, :, 1], summed[:, :, 1], float(SPARE_ROW), None, ALU.add)
                    ins.then_inc(routed, 1)
                    n += 1


ROUTE_STEPS = ["sel", "hi", "lo", "top", "hi_min", "lo_max", "second", "gsum", "gmax", "g_is", "g_cand", "g_index",
               "in_group", "outside", "selm", "max1", "is1", "cand1", "index1", "hot1",
               "without1", "max2", "is2", "cand2", "index2", "hot2", "both", "s1", "w1", "s2", "w2", "wsum",
               "wrec", "gate1", "gate2", "base0", "base1", "base2", "base3", "base4", "base5", "base6", "base7",
               "base8", "rank", "edges", "blocks", "ends", "starts", "start_slots", "slot", "slot1", "sum1", "int1",
               "slot2", "sum2", "int2", "ids_f", "block", "place", "where", "in_block", "block_ids0", "block_ids1", "at_place",
               "ended", "expert", "expert_max", "total", "plan_ends", "plan", "slot_ids0", "slot_ids1"]
ROUTED = {name: k + 1 for k, name in enumerate(ROUTE_STEPS)}


def load_expert(eng, e, K, wgu_d, wd_d, gu_free=None, down_free=None):
    w = e % N_WBUF
    n = 2 * ND * FF
    if e:
        eng.wait_ge(K["gu_in"], 16 * e)
    if gu_free is not None:
        gu_free()
    eng.dma_start(K["experts"][:, w, 0:n], wgu_d[e, :, :]).then_inc(K["gu_in"], 16)
    if e:
        eng.wait_ge(K["down_in"], 16 * e)
    if down_free is not None:
        down_free()
    eng.dma_start(K["experts"][:, w, n:n + 2 * D], wd_d[e, :, :]).then_inc(K["down_in"], 16)


def experts(nc, ctx, h1_dram, y_dram, wgu_d, wd_d, out, C, K, rows_at, mem, upper):
    sem = lambda n: ctx.enter_context(nc.semaphore(n))
    h1, rows, plan, idx, W, gu_in, down_in = (K[n] for n in ("h1", "rows", "plan", "ids", "experts", "gu_in", "down_in"))
    GROUP = ND * FF
    idx_x = mem.put("gather_ids", [P, 2, 2], I32)
    idx_y = mem.put("scatter_ids", [P, 2, 2], I32)
    turn = mem.put("turn", [P, 1])
    xg = mem.put("slot_rows", [P, 2, D])
    mem2 = Memory(nc, rows_at)
    x_hi, x_lo = ([m.put(f"slot_rows_T_{n}{b}", [P, ND, P], F32R) for b, m in enumerate((mem, mem2))] for n in ("hi", "lo"))
    sg = mem.put("silu_gate", [P, FF])
    ac = mem.put("act", [P, FF])
    a_hi, a_lo = (mem.put(f"act_T_{n}", [P, 2, P], F32R) for n in ("hi", "lo"))
    y = mem.put("slot_out", [P, 2, D])
    w_hi, w_lo = (upper.put(f"weights_{n}", [P, W_COLS], F32R) for n in ("hi", "lo"))
    split_done = sem("blocks_split")
    hi_made = [sem(f"weights_hi{group}") for group in range(3)]
    lo_made = sem("weights_lo")
    lo_down = sem("weights_lo_down")
    x_in, y_out = ([sem(f"{n}{b}") for b in range(2)] for n in ("xg_in", "y_out"))
    idx_x_made, idx_y_made = sem("idx_x_made"), sem("idx_y_made")
    half_made, gu_made, xT_made, d_made, aT_made = sem("gu_half_made"), sem("gu_made"), sem("xg_T_made"), sem("down_made"), sem("act_T_made")
    x_hi_made, x_lo_made, silu_done, act_done, a_made = (sem(n) for n in ("x_hi_made", "x_lo_made", "silu_done", "act_done", "act_T_kept"))
    y_act, y_dve = sem("y_kept_act"), sem("y_kept_dve")

    def trips(eng):
        more = eng.value_load(plan[0:1, PLANNED:PLANNED + 1], min_val=0, max_val=MAX_BLOCKS - MIN_BLOCKS)
        return eng.snap((more + 1) // 2 + MIN_BLOCKS // 2, min_val=MIN_BLOCKS // 2, max_val=MAX_BLOCKS // 2)

    def wait(eng, s, value):
        if not isinstance(value, int) or value > 0:
            eng.wait_ge(s, value)

    def expert(eng, s):
        return eng.value_load(plan[0:1, bass.ds(s, 1)], min_val=0, max_val=N_EXPERTS - 1)

    def raw(eng, e, at, n):
        w = eng.snap(e % N_WBUF, min_val=0, max_val=N_WBUF - 1)
        return W[:, bass.ds(w, 1), at:at + n].rearrange("p o c -> p (o c)")

    def run(eng, step, n):
        for s in range(4):
            step(s, s % 2, s // 2)
        with eng.Fori(2, n) as q:
            for b in range(2):
                step(2 * q + b, b, q)

    with ExitStack() as inner:
        gub = inner.enter_context(nc.psum_tensor("gu_bank", [P, HALF], F32))
        xb = [inner.enter_context(nc.psum_tensor(f"xg_bank{b}", [P, HALF], F32)) for b in range(2)]
        ab = inner.enter_context(nc.psum_tensor("act_bank", [P, HALF], F32))
        yb = [inner.enter_context(nc.psum_tensor(f"y_bank{b}", [P, HALF], F32)) for b in range(4)]
        with nc.Block() as block:
            @block.sync
            def _(sp):
                for e in range(N_WBUF, N_EXPERTS):
                    at = PLAN_ENDS + e - N_WBUF
                    through = sp.value_load(plan[0:1, at:at + 1], min_val=0, max_val=MAX_BLOCKS)

                    def gu_free():
                        sp.wait_ge(lo_made, 2 * through + 1)

                    def down_free():
                        sp.wait_ge(split_done, through + 1)
                        sp.wait_ge(lo_down, through + 1)

                    load_expert(sp, e, K, wgu_d, wd_d, gu_free, down_free)
                sp.wait_ge(gu_in, 16 * N_EXPERTS)
                sp.wait_ge(down_in, 16 * N_EXPERTS)

            @block.gpsimd
            def _(pool):
                def gather(s, b, uses):
                    wait(pool, xT_made, s - 1)
                    wait(pool, x_in[b], 16 * uses)
                    pool.tensor_copy(idx_x[:, b, :], idx[:, bass.ds(s, 1), :].rearrange("p o two -> p (o two)")).then_inc(idx_x_made, 1)
                    pool.wait_ge(idx_x_made, s + 1)
                    pool.tensor_tensor(turn[:], C("ones")[:, 0:1], C("ones")[:, 0:1], ALU.add)
                    pool.indirect_dma_start(xg[:, b, :], None, h1_dram,
                                            bass.IndirectOffsetOnAxis(ap=idx_x[:, b, 0:1], axis=0)).then_inc(x_in[b], 16)

                def scatter(s, b, uses):
                    wait(pool, y_out[b], 16 * uses)
                    pool.tensor_copy(idx_y[:, b, :], idx[:, bass.ds(s, 1), :].rearrange("p o two -> p (o two)")).then_inc(idx_y_made, 1)
                    pool.wait_ge(idx_y_made, s + 1)
                    pool.wait_ge(y_act, s + 1)
                    pool.wait_ge(y_dve, s + 1)
                    wait(pool, y_out[1 - b], 16 * (uses + b))
                    pool.tensor_tensor(turn[:], C("ones")[:, 0:1], C("ones")[:, 0:1], ALU.add)
                    pool.indirect_dma_start(y_dram, bass.IndirectOffsetOnAxis(ap=idx_y[:, b, 1:2], axis=0),
                                            y[:, b, :], None).then_inc(y_out[b], 16)

                def step(s, b, q):
                    gather(s + 3, 1 - b, q + 1 + b)
                    if not isinstance(s, int) or s >= 2:
                        scatter(s - 2, b, q - 1)
                    e = expert(pool, s)
                    pool.wait_ge(hi_made[2], s + 1)
                    pool.wait_ge(lo_made, 2 * (s + 1) + 1)
                    at = 2 * GROUP
                    pool.tensor_tensor(w_lo[:, at:at + D], raw(pool, e, at, D), w_hi[:, at:at + D].bitcast(F32),
                                       ALU.subtract).then_inc(split_done, 1)

                pool.memset(turn[:], 0).then_inc(split_done, 1)
                gather(0, 0, 0)
                gather(1, 1, 0)
                gather(2, 0, 1)
                n = trips(pool)
                run(pool, step, n)
                for b in range(2):
                    scatter(2 * n - 2 + b, b, n - 1)
                for b in range(2):
                    pool.wait_ge(y_out[b], 16 * n)
                    pool.wait_ge(x_in[b], 16 * (n + 2 - b))

            @block.tensor
            def _(pe):
                def gate_up(s, b):
                    pe.wait_ge(x_hi_made, s + 1)
                    pe.wait_ge(x_lo_made, s + 1)
                    wait(pe, act_done, s)
                    for half in range(2):
                        pe.wait_ge(hi_made[half], s + 1)
                        pe.wait_ge(lo_made, 2 * s + half + 2)
                        for k in range(half * ND // 2, (half + 1) * ND // 2):
                            for x, w in ((x_hi, w_hi), (x_hi, w_lo), (x_lo, w_hi)):
                                mm = pe.matmul(gub[:], x[b][:, k, :], w[:, k * HALF:(k + 1) * HALF],
                                               start=k == 0 and w is w_hi and x is x_hi, stop=k == ND - 1 and x is x_lo)
                        mm.then_inc(gu_made if half else half_made, 1)

                def turn_x(s, b, q):
                    pe.wait_ge(x_in[b], 16 * (q + 1))
                    wait(pe, x_hi_made, s)
                    wait(pe, x_lo_made, s)
                    for k in range(ND):
                        mm = pe.transpose(xb[k // 4][:, (k % 4) * P:(k % 4 + 1) * P], xg[:, b, k * P:(k + 1) * P], C("ident"))
                    mm.then_inc(xT_made, 1)

                def down(s, b):
                    pe.wait_ge(hi_made[2], s + 1)
                    pe.wait_ge(split_done, s + 2)
                    pe.wait_ge(lo_down, s + 2)
                    pe.wait_ge(a_made, 2 * (s + 1))
                    wait(pe, y_act, s - 1)
                    wait(pe, y_dve, s - 1)
                    for half in range(2):
                        for k in range(2):
                            at = 2 * GROUP + k * D + half * HALF
                            for a, w in ((a_hi, w_hi), (a_hi, w_lo), (a_lo, w_hi)):
                                mm = pe.matmul(yb[2 * b + half][:], a[:, k, :], w[:, at:at + HALF],
                                               start=k == 0 and w is w_hi and a is a_hi, stop=k == 1 and a is a_lo)
                    mm.then_inc(d_made, 1)

                def turn_act(s):
                    pe.wait_ge(act_done, s + 1)
                    wait(pe, a_made, 2 * s)
                    for k in range(2):
                        mm = pe.transpose(ab[:, k * P:(k + 1) * P], ac[:, k * P:(k + 1) * P], C("ident"))
                    mm.then_inc(aT_made, 1)

                def step(s, b, q):
                    gate_up(s, b)
                    turn_x(s + 2, b, q + 1)
                    if not isinstance(s, int) or s:
                        down(s - 1, 1 - b)
                    turn_act(s)

                n = trips(pe)
                turn_x(0, 0, 0)
                turn_x(1, 1, 0)
                run(pe, step, n)
                down(2 * n - 1, 1)

            @block.scalar
            def _(act):
                def high(s, group, e):
                    at, n = group * GROUP, GROUP if group < 2 else 2 * D
                    act.wait_ge(gu_in if group < 2 else down_in, 16 * (e + 1))
                    if group < 2:
                        wait(act, (half_made, gu_made)[group], s)
                    else:
                        wait(act, d_made, s)
                    act.copy(w_hi[:, at:at + n], raw(act, e, at, n)).then_inc(hi_made[group], 1)

                def x_high(s, b):
                    act.wait_ge(xT_made, s + 1)
                    wait(act, gu_made, s - 1)
                    for k in range(2):
                        ins = act.copy(x_hi[b][:, 4 * k:4 * k + 4, :].rearrange("p k t -> p (k t)"), xb[k][:])
                    ins.then_inc(x_hi_made, 1)

                def keep_y(s, b, q):
                    act.wait_ge(d_made, s + 1)
                    wait(act, y_out[b], 16 * q)
                    act.copy(y[:, b, 0:HALF], yb[2 * b][:]).then_inc(y_act, 1)

                def step(s, b, q):
                    e = expert(act, s + 1)
                    high(s + 1, 0, e)
                    act.wait_ge(gu_made, s + 1)
                    wait(act, act_done, s)
                    act.activation(sg[:], gub[:, 0:FF], ACT.Silu).then_inc(silu_done, 1)
                    high(s + 1, 1, e)
                    x_high(s + 2, b)
                    if not isinstance(s, int) or s:
                        keep_y(s - 1, 1 - b, q - 1 + b)
                    high(s, 2, expert(act, s))

                n = trips(act)
                e = expert(act, 0)
                high(0, 0, e)
                x_high(0, 0)
                high(0, 1, e)
                x_high(1, 1)
                run(act, step, n)
                keep_y(2 * n - 1, 1, n - 1)

            @block.vector
            def _(dve):
                def low(s, group, e):
                    at = group * GROUP
                    dve.wait_ge(hi_made[group], s + 1)
                    dve.tensor_tensor(w_lo[:, at:at + GROUP], raw(dve, e, at, GROUP), w_hi[:, at:at + GROUP].bitcast(F32),
                                      ALU.subtract).then_inc(lo_made, 1)

                def x_low(s, b):
                    dve.wait_ge(x_hi_made, s + 1)
                    for k in range(2):
                        part = slice(4 * k, 4 * k + 4)
                        ins = dve.tensor_tensor(x_lo[b][:, part, :].rearrange("p k t -> p (k t)"), xb[k][:],
                                                x_hi[b][:, part, :].rearrange("p k t -> p (k t)").bitcast(F32), ALU.subtract)
                    ins.then_inc(x_lo_made, 1)

                def keep_y(s, b, q):
                    dve.wait_ge(d_made, s + 1)
                    wait(dve, y_out[b], 16 * q)
                    dve.tensor_copy(y[:, b, HALF:], yb[2 * b + 1][:]).then_inc(y_dve, 1)

                def step(s, b, q):
                    e = expert(dve, s + 1)
                    dve.wait_ge(silu_done, s + 1)
                    wait(dve, aT_made, s)
                    dve.tensor_tensor(ac[:], sg[:], gub[:, FF:2 * FF], ALU.mult).then_inc(act_done, 1)
                    low(s + 1, 0, e)
                    low(s + 1, 1, e)
                    x_low(s + 2, b)
                    if not isinstance(s, int) or s:
                        keep_y(s - 1, 1 - b, q - 1 + b)
                    dve.wait_ge(aT_made, s + 1)
                    wait(dve, d_made, s)
                    turned = ab[:, 0:2 * P]
                    dve.tensor_copy(a_hi[:].rearrange("p k t -> p (k t)"), turned).then_inc(a_made, 1)
                    dve.wait_ge(a_made, 2 * s + 1)
                    dve.tensor_tensor(a_lo[:].rearrange("p k t -> p (k t)"), turned,
                                      a_hi[:].rearrange("p k t -> p (k t)").bitcast(F32), ALU.subtract).then_inc(a_made, 1)
                    at = 2 * GROUP + D
                    e = expert(dve, s)
                    dve.wait_ge(hi_made[2], s + 1)
                    dve.tensor_tensor(w_lo[:, at:at + D], raw(dve, e, at, D), w_hi[:, at:at + D].bitcast(F32),
                                      ALU.subtract).then_inc(lo_down, 1)

                n = trips(dve)
                dve.nop().then_inc(lo_made, 1)
                dve.nop().then_inc(lo_down, 1)
                e = expert(dve, 0)
                low(0, 0, e)
                x_low(0, 0)
                low(0, 1, e)
                x_low(1, 1)
                run(dve, step, n)
                keep_y(2 * n - 1, 1, n - 1)


def combine(nc, ctx, y_dram, out, K, mem):
    sem = lambda n: ctx.enter_context(nc.semaphore(n))
    h1, rows, gates = K["h1"], K["rows"], K["gates"]
    R = 3
    yg = mem.put("y_rows", [P, NT, TOP_K, D])
    f = mem.put("sum", [P, R, D])
    o = mem.put("normed", [P, R, D])
    gain_cols = [0] * (NT - 1) + [5 * P]
    bias_cols = [2 * P] * (NT - 1) + [5 * P]
    stats = mem.put("ln2_stats", [P, NT, 12])
    mv = mem.put("ln2_mv", [P, NT, 2])
    std = mem.put("ln2_std", [P, NT, 4])
    y_in = [sem(f"y_in{b}") for b in range(R)]
    o_out = [sem(f"o_out{b}") for b in range(R)]
    y1_done, sums, dev, inv, shift, xn, gain, gain_dve, bias_pool, bias_dve = (
        sem(f"ln2_{n}") for n in ("y1", "sums", "dev", "inv", "shift", "xn", "gain", "gain_dve",
                                  "bias_pool", "bias_dve"))
    with nc.Block() as block:
        @block.sync
        def _(sp):
            def load(i):
                if i >= R:
                    sp.wait_ge(y_in[i % R], 32 * (i // R))
                for k in range(TOP_K):
                    sp.dma_start(yg[:, i, k, :], y_dram[k * T + i * P:k * T + (i + 1) * P, :]
                                 ).then_inc(y_in[i % R], 16)

            for i in range(NT):
                load(i)
            for i in range(NT):
                sp.wait_ge(bias_pool, i + 1)
                sp.wait_ge(bias_dve, i + 1)
                sp.dma_start(out[i * P:(i + 1) * P, :], o[:, i % R, :]).then_inc(o_out[i % R], 16)
            for b in range(R):
                sp.wait_ge(o_out[b], 16 * len(range(b, NT, R)))

        @block.scalar
        def _(act):
            def first(i):
                act.wait_ge(y_in[i % R], 32 * (i // R + 1))
                if i >= R:
                    act.wait_ge(xn, i - R + 1)
                act.activation(f[:, i % R, :], yg[:, i, 0, :], ACT.Copy, scale=gates[:, 0, i:i + 1]).then_inc(y1_done, 1)

            first(0)
            for i in range(NT):
                if i + 1 < NT:
                    first(i + 1)
                act.wait_ge(sums, 5 * (i + 1))
                act.activation(std[:, i, 0:1], mv[:, i, 1:2], ACT.Sqrt, bias=LN_EPS).then_inc(dev, 1)
                act.wait_ge(shift, i + 1)
                if i >= R:
                    act.wait_ge(o_out[i % R], 16 * (i // R))
                act.activation(o[:, i % R, :], f[:, i % R, :], ACT.Identity, bias=std[:, i, 2:3],
                               scale=std[:, i, 1:2]).then_inc(xn, 1)

        @block.gpsimd
        def _(pool):
            for i in range(NT):
                b = i % R
                pool.wait_ge(xn, i + 1)
                at = gain_cols[i]
                pool.tensor_tensor(o[:, b, at:], o[:, b, at:], rows[:, 2, at:], ALU.mult).then_inc(gain, 1)
                at = bias_cols[i]
                pool.wait_ge(gain, i + 1)
                pool.tensor_tensor(o[:, b, at:], o[:, b, at:], rows[:, 3, at:], ALU.add).then_inc(bias_pool, 1)

        @block.vector
        def _(dve):
            def add_bias(i):
                b = i % R
                n = gain_cols[i]
                if n:
                    dve.wait_ge(xn, i + 1)
                    dve.tensor_tensor(o[:, b, 0:n], o[:, b, 0:n], rows[:, 2, 0:n], ALU.mult).then_inc(gain_dve, 1)
                    dve.wait_ge(gain_dve, 1)
                else:
                    dve.wait_ge(gain, i + 1)
                n = bias_cols[i]
                dve.tensor_tensor(o[:, b, 0:n], o[:, b, 0:n], rows[:, 3, 0:n], ALU.add).then_inc(bias_dve, 1)

            for i in range(NT):
                b = i % R
                dve.wait_ge(y1_done, i + 1)
                dve.scalar_tensor_tensor(f[:, b, :], yg[:, i, 1, :], gates[:, 1, i:i + 1], f[:, b, :],
                                         ALU.mult, ALU.add).then_inc(sums, 1)
                dve.wait_ge(sums, 5 * i + 1)
                dve.scalar_tensor_tensor(f[:, b, :], h1[:, i, :], ALPHA, f[:, b, :], ALU.mult, ALU.add).then_inc(sums, 1)
                dve.wait_ge(sums, 5 * i + 2)
                for k in range(2):
                    dve.bn_stats(stats[:, i, 6 * k:6 * k + 6], f[:, b, k * HALF:(k + 1) * HALF]).then_inc(sums, 1)
                dve.wait_ge(sums, 5 * i + 4)
                dve.bn_aggr(mv[:, i, :], stats[:, i, :]).then_inc(sums, 1)
                if i >= 2:
                    add_bias(i - 2)
                dve.wait_ge(dev, i + 1)
                dve.reciprocal(std[:, i, 1:2], std[:, i, 0:1]).then_inc(inv, 1)
                dve.wait_ge(inv, i + 1)
                dve.scalar_tensor_tensor(std[:, i, 2:3], mv[:, i, 0:1], -1.0, std[:, i, 1:2],
                                         ALU.mult, ALU.mult).then_inc(shift, 1)
            add_bias(NT - 2)
            add_bias(NT - 1)


def hybrid_decoder(nc, d, out, dbg=None, stop=None):
    h_dram = nc.dram_tensor("h_scratch", [T, D], F32).ap()
    toep_dram = nc.dram_tensor("toeplitz_scratch", [6, P, N_TOEPLITZ], F32).ap()
    h1_dram = nc.dram_tensor("h1_scratch", [T, D], F32).ap()
    y_dram = nc.dram_tensor("y_scratch", [SPARE_ROW + 1, D], F32).ap()
    qk_dram = nc.dram_tensor("qk_scratch", [N_CM - N_B, P, T], F32).ap()
    with ExitStack() as ctx:
        keep = Memory(nc, 17408)
        const_sb = keep.put("const_sb", [P, N_CONST])
        par_sb = keep.put("par_sb", [P, N_PC])
        mask_sb = keep.put("mask_sb", [P, (N_LEVELS + 1) * P], I32)

        def C(name, k=0, n=None):
            if name in CONST:
                at, width = CONST[name]
                return const_sb[:, at:at + width]
            at = PC[name][0] + k
            return par_sb[:, at:at + (n or 1)]

        early = keep.at
        v_tok = keep.put("v_tok", [P, NT, HALF])
        spent = keep.at
        pm = keep.put("mixed_channels", [P, N_B, T])
        R = {"AR": keep.put("ar", [P, 2, NT, 2, P]), "bt": keep.put("bt", [P, 2, T])}
        wv_at = keep.at
        R["bh"], R["kh"] = keep.put("bh", [P, 2, T]), keep.put("kh", [P, 2, T])
        R["wv"] = nc.alloc_sbuf_tensor_at("wv_sb", [P, ND, HALF], F32, offset=wv_at)
        R["wv_lo"] = nc.alloc_sbuf_tensor_at("wv_lo", [P, ND, HALF], F32R, offset=wv_at)
        gate_at = keep.at
        R["g"], R["bonus"] = keep.put("gate", [P, 2, T]), keep.put("bonus", [P, 2, T])
        R["PT"] = keep.put("chunk_decay", [P, 2, NCH])
        zone = keep.at
        hT = keep.put("hT", [P, ND, T])
        mixT = nc.alloc_sbuf_tensor_at("mixT", [P, ND, T], F32, offset=zone)
        work = keep.at
        for name, tile in (("bh_tok", 0), ("kh_tok", 5)):
            R[name] = nc.alloc_sbuf_tensor_at(name, [P, NT, 256], F32, offset=zone + tile * 4 * T)
        R["RT"] = nc.alloc_sbuf_tensor_at("r_total", [P, 2, 2, P], F32, offset=zone + 2 * 4 * T)
        R["S"] = nc.alloc_sbuf_tensor_at("state", [P, 2, 2, P], F32, offset=zone + 2 * 4 * T + 4 * 512)
        w_out = nc.alloc_sbuf_tensor_at("w_out", [P, ND, D], F32, offset=work)
        w_out_in = ctx.enter_context(nc.semaphore("w_out_in"))
        qk = nc.alloc_sbuf_tensor_at("qk_ahead", [P, 2, 2, T], F32, offset=spent)
        qk_in = [ctx.enter_context(nc.semaphore(f"qk_in{b}")) for b in range(2)]
        ar_at = spent + 4 * N_B * T
        R["wv_hi"] = nc.alloc_sbuf_tensor_at("wv_hi", [P, ND, HALF], F32R, offset=ar_at)
        over_hi = Memory(nc, work + 4 * N_SPLIT * T, work + 4 * ND * T)
        R["bh_at"], R["kh_at"], R["ar_at"] = wv_at, wv_at + 8 * T, ar_at
        above_hi = Memory(nc, work + 4 * ND * T)
        H = {"x_sb": pm, "hT_hi": nc.alloc_sbuf_tensor_at("hT_hi", [P, ND, T], F32R, offset=work),
             "hT_lo": nc.alloc_sbuf_tensor_at("hT_lo", [P, ND, T], F32R, offset=zone),
             "w_lo": nc.alloc_sbuf_tensor_at("w_lo", [P, 2, ND * P], F32R, offset=above_hi.at),
             "w_ring": above_hi.put("w_ring", [P, 2, ND * P]), "w_hi": above_hi.put("w_hi", [P, 2, ND * P], F32R),
             "hb": nc.alloc_sbuf_tensor_at("h_rows", [P, 2, D], F32, offset=ar_at),
             "gb": nc.alloc_sbuf_tensor_at("ln0_rows", [P, 2, D], F32, offset=ar_at + 8 * D)}
        for name in ("xn_done", "rows_in", "w_hi_made", "w_lo_made", "h_hi", "h_lo"):
            H[name] = ctx.enter_context(nc.semaphore(name))
        H["qk_stored"] = [ctx.enter_context(nc.semaphore(f"qk_stored{b}")) for b in range(2)]
        H["w_in"] = [ctx.enter_context(nc.semaphore(f"w_in{b}")) for b in range(2)]
        after_ring = above_hi.at
        late = Memory(nc, early, zone)
        K = {"h1": late.put("h1", [P, NT, D])}
        rows_at = late.at
        K |= {"rows": late.put("ln_rows", [P, 4, D]),
             "gates": late.put("gates", [P, 2, NT]), "slots": late.put("slots", [P, 2, NT], I32),
             "plan": late.put("plan", [1, PLAN], I32), "ids": late.put("slot_ids", [P, SLOT_BLOCKS, 2], I32)}
        first = EXPERTS_AT
        assert late.at < first and first + 4 * W_COLS <= zone
        K["experts"] = nc.alloc_sbuf_tensor_at("expert_weights", [P, N_WBUF, W_COLS], F32, offset=first)
        K["gu_in"], K["down_in"] = (ctx.enter_context(nc.semaphore(f"expert_{n}_in")) for n in ("gu", "down"))
        stages = {
            "normalise": lambda: normalise_input(
                nc, ctx, d["x"], d["ln_rows"], d["w_cm"], C,
                (const_sb, d["consts"], par_sb, d["params"], mask_sb, d["masks"]), pm, hT, H, Memory(nc, after_ring)),
            "project": lambda: project(nc, ctx, d["w_cm"], d["w_v"], d["up"], d["gate_up"], qk_dram, h_dram, C, hT,
                                       pm, v_tok, R, H, Memory(nc, after_ring), over_hi),
            "rwkv": lambda: rwkv(nc, ctx, qk_dram, H["qk_stored"], qk, qk_in, C, mask_sb, pm, R, mixT, Memory(nc, work)),
            "attend": lambda: attend(nc, ctx, d["w_out"], w_out, w_out_in, qk_dram, toep_dram, d["rel_bias"], d["bucket_hot"], d["sinks"], C, mask_sb,
                                     v_tok, mixT, R, qk, qk_in, Memory(nc, spent, gate_at), Memory(nc, work + 4 * ND * D)),
            "route": lambda: mix_and_route(nc, ctx, d["w_gate_up"], d["w_down"], h_dram, h1_dram, d["ln_rows"][2:6, :], d["router_w"],
                                           d["router_bias"], d["route"], C, mixT, w_out, w_out_in, K,
                                           Memory(nc, late.at, first), Memory(nc, work + 4 * ND * D)),
            "experts": lambda: experts(nc, ctx, h1_dram, y_dram, d["w_gate_up"], d["w_down"], out, C, K, rows_at,
                                       Memory(nc, late.at, first), Memory(nc, first + 4 * N_WBUF * W_COLS)),
            "combine": lambda: combine(nc, ctx, y_dram, out, K, Memory(nc, late.at)),
        }
        for name, stage in stages.items():
            stage()
            if stop == name:
                break
        if dbg is not None:
            dbg(nc, ctx, dict(hT=hT, pm=pm, ob=mixT[:, 3:5, :], v_tok=v_tok, mixT=mixT, par_sb=par_sb, h_dram=h_dram, qk_dram=qk_dram, h1_dram=h1_dram, **R, **K), out)


def lay_out(v):
    f = lambda a: np.ascontiguousarray(a, dtype=np.float32)
    v = {k: np.asarray(a) for k, a in v.items()}
    col = lambda a: a.reshape(-1, P).T
    w = v["w_in"][0]
    b0, c0 = A_COLS, A_COLS + B_COLS
    b_tiles = [w[:, b0 + 768:b0 + 896], w[:, b0 + 896:b0 + 1024]]
    mu = v["shift_mu"][0]
    mus = [mu[768:896], mu[896:1024]]
    for g in range(2):
        for kind in range(3):
            at = 256 * kind + P * g
            b_tiles.append(w[:, b0 + at:b0 + at + P])
            mus.append(mu[at:at + P])
    c_tiles = [w[:, c0 + P * t:c0 + P * (t + 1)] for t in range(6)]
    a_tiles = [np.concatenate([w[:, HD * j:HD * (j + 1)], w[:, HD * (j + 3):HD * (j + 4)]], axis=1) for j in range(3)]
    a_tiles.append(w[:, 384:512])
    tiles = np.stack(b_tiles + c_tiles + a_tiles)
    w_v = np.concatenate([w[:, c0 + 768:c0 + 1152], w[:, 512:640]], axis=1)
    o = v["w_out"][0]
    w_out = np.concatenate([o[HD * (j + 3 * e):HD * (j + 3 * e + 1)] for j in range(3) for e in range(2)] + [o[384:]])
    params = [col(v["ln0_g"]), col(v["ln0_b"]), np.stack(mus, axis=1)]
    params += [col(v[n][0].reshape(-1)) for n in ("decay_w0", "iclr_a0", "k_k", "k_a", "r_k", "lnx_g", "lnx_b")]
    params += [col(v["ln1_g"][0]), col(v["ln1_b"][0])]
    params = np.concatenate(params, axis=1)
    params = np.concatenate([params, np.zeros((P, N_PC - params.shape[1]), np.float32)], axis=1)
    return {
        "x": f(v["x"][0]),
        "consts": f(np.concatenate(list(constants().values()), axis=1)),
        "params": f(params),
        "masks": np.ascontiguousarray(level_masks()),
        "ln_rows": f(np.stack([v["ln0_g"], v["ln0_b"], v["ln1_g"][0], v["ln1_b"][0], v["ln2_g"][0], v["ln2_b"][0]])),
        "route": routing_constants(),
        "router_w": f(v["router_w"].reshape(ND, P, 16).transpose(1, 0, 2).reshape(P, ND * 16)),
        "router_bias": f(v["router_bias"][None, :]),
        "w_out": f(w_out.reshape(ND, P, D).transpose(1, 0, 2).reshape(P, ND * D)),
        "w_gate_up": f(np.concatenate([v["w_gate"][0], v["w_up"][0]], axis=2).reshape(N_EXPERTS, ND, P, 2 * FF)
                       .transpose(0, 2, 1, 3).reshape(N_EXPERTS, P, ND * 2 * FF)),
        "w_down": f(v["w_down"][0].reshape(N_EXPERTS, 2, P, D).transpose(0, 2, 1, 3).reshape(N_EXPERTS, P, 2 * D)),
        "w_cm": f(tiles.reshape(N_CM, ND, P, P).transpose(0, 2, 1, 3).reshape(N_CM, P, ND * P)),
        "w_v": f(w_v.reshape(ND, P, HALF).transpose(1, 0, 2)),
        "up": f(np.concatenate([v["decay_up"][0], v["iclr_up"][0]])),
        "gate_up": f(v["gate_up"][0]),
        "rel_bias": f(v["rel_bias"]),
        "bucket_hot": f(bias_constants()),
        "sinks": f(v["sinks"]),
    }


def kernel(**inputs):
    import concourse.bacc as bacc
    from concourse.bass_utils import run_bass_kernel_spmd

    nc = bacc.Bacc("TRN2", target_bir_lowering=False, num_devices=1)
    arrays = lay_out(inputs)
    d = {name: nc.dram_tensor(name, a.shape, mybir.dt.from_np(a.dtype), kind="ExternalInput").ap()
         for name, a in arrays.items()}
    out = nc.dram_tensor("result", (T, D), F32, kind="ExternalOutput").ap()
    hybrid_decoder(nc, d, out)
    done = run_bass_kernel_spmd(nc, [arrays], core_ids=[0])
    return done.results[0]["result"].reshape(1, T, D)
```
